# Optimizing a Trainium2 kernel written in Bass

```python
import math
import jax, jax.numpy as jnp
from jax import lax
import numpy as np

D_MODEL = 1024
BATCH = 1
SEQ = 1024
DEPTH = 1
DEC_BATCH = 8
DEC_SEQ = 1
PAST_LEN = 1024
PAGE_SIZE = 128

CHUNK = 128
A_GROUPS = 8
A_GROUP_DIM = 64
A_WIDTH = A_GROUPS * A_GROUP_DIM
HEAD_DIM = 64
HEADS_PER_GROUP = 4
DILATION_GROUPS = ((128, 1), (512, 4), (2048, 16))
N_DGROUPS = len(DILATION_GROUPS)
B_QK_WIDTH = N_DGROUPS * HEADS_PER_GROUP * HEAD_DIM
B_OUT_WIDTH = HEADS_PER_GROUP * HEAD_DIM
ROPE_THETA = 10000.0
IN_SPLITS = (A_WIDTH, 2 * A_WIDTH, 2 * A_WIDTH + B_QK_WIDTH, 2 * A_WIDTH + 2 * B_QK_WIDTH,
             2 * A_WIDTH + 3 * B_QK_WIDTH, 2 * A_WIDTH + 3 * B_QK_WIDTH + D_MODEL)
IN_WIDTH = 2 * A_WIDTH + 3 * B_QK_WIDTH + 2 * D_MODEL
N_EXPERT_GROUPS = 4
EXPERTS_PER_GROUP = 8
N_EXPERTS = N_EXPERT_GROUPS * EXPERTS_PER_GROUP
TOP_K = 2
D_EXPERT = 512
MOE_BLOCK = 128
EPS = 1e-6

kernel_name = 'gated_gmlp_dilated_swa_hiermoe_step'

def rms_norm(x, g):
    xf = x.astype(jnp.float32)
    y = xf * lax.rsqrt(jnp.mean(xf * xf, axis=-1, keepdims=True) + EPS)
    return (y * g.astype(jnp.float32)).astype(x.dtype)

def layer_norm(x, g, b):
    xf = x.astype(jnp.float32)
    mu = jnp.mean(xf, axis=-1, keepdims=True)
    var = jnp.mean(jnp.square(xf - mu), axis=-1, keepdims=True)
    y = (xf - mu) * lax.rsqrt(var + EPS)
    return (y * g.astype(jnp.float32) + b.astype(jnp.float32)).astype(x.dtype)

def rope(x, pos):
    half = HEAD_DIM // 2
    inv = 1.0 / (ROPE_THETA ** (jnp.arange(half, dtype=jnp.float32) * (2.0 / HEAD_DIM)))
    ang = pos.astype(jnp.float32)[:, None] * inv[None, :]
    cos = jnp.cos(ang)[None, :, None, :]
    sin = jnp.sin(ang)[None, :, None, :]
    xf = x.astype(jnp.float32)
    x1, x2 = xf[..., :half], xf[..., half:]
    return jnp.concatenate([x1 * cos - x2 * sin, x2 * cos + x1 * sin], axis=-1).astype(x.dtype)

def input_projection(h, w_in, b_in, a_ln_g, a_ln_b, pos):
    bn, L, _ = h.shape
    z = h @ w_in + b_in
    u, va, q, k, vb, gate_a, gate_b = jnp.split(z, IN_SPLITS, axis=-1)
    u = jax.nn.gelu(u)
    va = layer_norm(jax.nn.gelu(va), a_ln_g, a_ln_b)
    nh = N_DGROUPS * HEADS_PER_GROUP
    q = rope(q.reshape(bn, L, nh, HEAD_DIM), pos).reshape(bn, L, N_DGROUPS, HEADS_PER_GROUP, HEAD_DIM)
    k = rope(k.reshape(bn, L, nh, HEAD_DIM), pos).reshape(bn, L, N_DGROUPS, HEADS_PER_GROUP, HEAD_DIM)
    vb = vb.reshape(bn, L, N_DGROUPS, HEADS_PER_GROUP, HEAD_DIM)
    return u, va, q, k, vb, gate_a, gate_b

def chunk_spatial_gate(u, v, w_s, b_s):
    bn, L, _ = u.shape
    lp = -(-L // CHUNK) * CHUNK
    vp = jnp.pad(v, ((0, 0), (0, lp - L), (0, 0))).reshape(bn, lp // CHUNK, CHUNK, A_GROUPS, A_GROUP_DIM)
    causal = jnp.tril(jnp.ones((CHUNK, CHUNK), dtype=bool))
    ws = jnp.where(causal[None], w_s, 0.0).astype(v.dtype)
    mixed = jnp.einsum('gts,bnsgc->bntgc', ws, vp) + b_s.T[:, :, None]
    mixed = mixed.reshape(bn, lp, A_WIDTH)[:, :L]
    return u * mixed

def dilated_attention_prompt(q, k, v, dilation, span):
    bn, S, H, dh = q.shape
    unit = dilation * span
    sp = -(-S // unit) * unit
    m = sp // dilation
    nb = m // span

    def to_blocks(t):
        t = jnp.pad(t, ((0, 0), (0, sp - S), (0, 0), (0, 0)))
        return t.reshape(bn, m, dilation, H, dh).transpose(0, 2, 1, 3, 4).reshape(bn, dilation, nb, span, H, dh)

    def with_prev(t):
        prev = jnp.pad(t[:, :, :-1], ((0, 0), (0, 0), (1, 0), (0, 0), (0, 0), (0, 0)))
        return jnp.concatenate([prev, t], axis=3)

    qb = to_blocks(q)
    kk = with_prev(to_blocks(k))
    vv = with_prev(to_blocks(v))
    s = jnp.einsum('bdnqhe,bdnkhe->bdnhqk', qb, kk, preferred_element_type=jnp.float32) * (dh ** -0.5)
    qi = jnp.arange(span)[:, None]
    ki = jnp.arange(2 * span)[None, :]
    band = (ki >= qi) & (ki <= qi + span)
    has_prev = (jnp.arange(nb) > 0)[:, None, None] | (ki >= span)[None]
    mask = band[None] & has_prev
    s = jnp.where(mask[None, None, :, None], s, -jnp.inf)
    lse = jax.nn.logsumexp(s, axis=-1)
    p = jnp.exp(s - lse[..., None])
    o = jnp.einsum('bdnhqk,bdnkhe->bdnqhe', p.astype(v.dtype), vv)

    def from_blocks(t):
        x_dim = t.shape[-1]
        t = t.reshape(bn, dilation, m, H, x_dim).transpose(0, 2, 1, 3, 4)
        return t.reshape(bn, sp, H, x_dim)[:, :S]

    o = from_blocks(o)
    lse = from_blocks(lse.transpose(0, 1, 2, 4, 3)[..., None])[..., 0]
    return o, lse

def dilated_attention_sample(q, k_new, v_new, kv_cache, dilation, span):
    wb = kv_cache.shape[1]
    L = q.shape[1]
    keys = jnp.concatenate([kv_cache[:, :, 0], k_new.astype(kv_cache.dtype)], axis=1)
    vals = jnp.concatenate([kv_cache[:, :, 1], v_new.astype(kv_cache.dtype)], axis=1)
    qidx = wb + jnp.arange(L)
    kidx = qidx[:, None] - dilation * jnp.arange(span + 1)[None, :]
    valid = kidx >= 0
    kidx = jnp.maximum(kidx, 0)
    kg = keys[:, kidx]
    vg = vals[:, kidx]
    s = jnp.einsum('blhe,bljhe->blhj', q, kg.astype(q.dtype), preferred_element_type=jnp.float32) * (HEAD_DIM ** -0.5)
    s = jnp.where(valid[None, :, None, :], s, -jnp.inf)
    lse = jax.nn.logsumexp(s, axis=-1)
    p = jnp.exp(s - lse[..., None])
    o = jnp.einsum('blhj,bljhe->blhe', p.astype(q.dtype), vg.astype(q.dtype))
    return o, lse

def combine_by_denominator(outs, lses):
    o = jnp.stack(outs, axis=0).astype(jnp.float32)
    w = jax.nn.softmax(jnp.stack(lses, axis=0), axis=0)
    comb = jnp.sum(w[..., None] * o, axis=0).astype(outs[0].dtype)
    return comb.reshape(comb.shape[0], comb.shape[1], B_OUT_WIDTH)

def grouped_expert_ffn(hf, expert_ids, gates, w_gate, w_up, w_down):
    T, D = hf.shape
    a = T * TOP_K
    flat_e = expert_ids.reshape(a)
    flat_tok = jnp.repeat(jnp.arange(T, dtype=jnp.int32), TOP_K)
    flat_g = gates.reshape(a)
    order = jnp.argsort(flat_e)
    se, stok, sg = flat_e[order], flat_tok[order], flat_g[order]
    counts = jax.ops.segment_sum(jnp.ones((a,), jnp.int32), flat_e, num_segments=N_EXPERTS)
    starts = jnp.cumsum(counts) - counts
    padded = (counts + MOE_BLOCK - 1) // MOE_BLOCK * MOE_BLOCK
    pstarts = jnp.cumsum(padded) - padded
    dest = pstarts[se] + (jnp.arange(a, dtype=jnp.int32) - starts[se])
    n_blocks = -(-a // MOE_BLOCK) + N_EXPERTS
    rows = n_blocks * MOE_BLOCK
    xs = jnp.zeros((rows, D), hf.dtype).at[dest].set(hf[stok])
    block_e = jnp.minimum(jnp.searchsorted(pstarts + padded, jnp.arange(n_blocks) * MOE_BLOCK, side='right'),
                          N_EXPERTS - 1)

    def expert_block(args):
        xb, e = args
        hid = jax.nn.silu(xb @ w_gate[e]) * (xb @ w_up[e])
        return hid @ w_down[e]

    ys = lax.map(expert_block, (xs.reshape(n_blocks, MOE_BLOCK, D), block_e)).reshape(rows, D)
    return jnp.zeros((T, D), hf.dtype).at[stok].add(ys[dest] * sg[:, None].astype(hf.dtype))

def hierarchical_moe(h, w_group_router, b_group_router, w_expert_router, b_expert_router, w_gate, w_up, w_down):
    bn, L, D = h.shape
    hf = h.reshape(bn * L, D)
    g_logits = (hf @ w_group_router + b_group_router).astype(jnp.float32)
    g_prob = jax.nn.softmax(g_logits, axis=-1)
    grp = jnp.argmax(g_logits, axis=-1).astype(jnp.int32)
    p_grp = jnp.take_along_axis(g_prob, grp[:, None], axis=-1)[:, 0]
    e_logits = (hf @ w_expert_router + b_expert_router).astype(jnp.float32)
    e_logits = e_logits.reshape(-1, N_EXPERT_GROUPS, EXPERTS_PER_GROUP)
    sel = jnp.take_along_axis(e_logits, grp[:, None, None], axis=1)[:, 0]
    top_val, top_idx = lax.top_k(sel, TOP_K)
    gates = p_grp[:, None] * jax.nn.softmax(top_val, axis=-1)
    expert_ids = grp[:, None] * EXPERTS_PER_GROUP + top_idx.astype(jnp.int32)
    return grouped_expert_ffn(hf, expert_ids, gates, w_gate, w_up, w_down).reshape(bn, L, D)

def layer_forward(x, pos, kv_caches, norm1_g, w_in, b_in, a_ln_g, a_ln_b, w_spatial, b_spatial,
                  w_a_proj, w_b_proj, w_o, norm2_g, w_group_router, b_group_router,
                  w_expert_router, b_expert_router, w_gate, w_up, w_down):
    h = rms_norm(x, norm1_g)
    u, va, q, k, vb, gate_a, gate_b = input_projection(h, w_in, b_in, a_ln_g, a_ln_b, pos)
    s_a = chunk_spatial_gate(u, va, w_spatial, b_spatial)
    outs, lses, kv_rows = [], [], []
    for g, (window, dilation) in enumerate(DILATION_GROUPS):
        span = window // dilation
        qg, kg, vg = q[:, :, g], k[:, :, g], vb[:, :, g]
        if kv_caches is None:
            o, lse = dilated_attention_prompt(qg, kg, vg, dilation, span)
            keep = min(window, x.shape[1])
            kv_rows.append(jnp.stack([kg[:, -keep:], vg[:, -keep:]], axis=2))
        else:
            o, lse = dilated_attention_sample(qg, kg, vg, kv_caches[g], dilation, span)
            kv_rows.append(jnp.stack([kg, vg], axis=2))
        outs.append(o)
        lses.append(lse)
    o_b = combine_by_denominator(outs, lses)
    merged = jax.nn.sigmoid(gate_a) * (s_a @ w_a_proj) + jax.nn.sigmoid(gate_b) * (o_b @ w_b_proj)
    x = x + merged @ w_o
    x = x + hierarchical_moe(rms_norm(x, norm2_g), w_group_router, b_group_router,
                             w_expert_router, b_expert_router, w_gate, w_up, w_down)
    return x, kv_rows, va

def setup_inputs(seed: int = 0) -> dict:
    key = jax.random.key(seed)
    ks = jax.random.split(key, 24)

    def nrm(k, shape, scale):
        return jax.random.normal(k, shape, jnp.float32) * scale

    d = D_MODEL
    cache_shape = lambda w: (DEPTH, DEC_BATCH, min(w, PAST_LEN), 2, HEADS_PER_GROUP, HEAD_DIM)
    return {
        'x_prompt': nrm(ks[0], (BATCH, SEQ, d), 1.0),
        'x_sample': nrm(ks[1], (DEC_BATCH, DEC_SEQ, d), 1.0),
        'cache_kv_g0': nrm(ks[2], cache_shape(DILATION_GROUPS[0][0]), 1.0),
        'cache_kv_g1': nrm(ks[3], cache_shape(DILATION_GROUPS[1][0]), 1.0),
        'cache_kv_g2': nrm(ks[4], cache_shape(DILATION_GROUPS[2][0]), 1.0),
        'norm1_g': 1.0 + nrm(ks[5], (DEPTH, d), 0.02),
        'w_in': nrm(ks[6], (DEPTH, d, IN_WIDTH), d ** -0.5),
        'b_in': nrm(ks[7], (DEPTH, IN_WIDTH), 0.02),
        'a_ln_g': 1.0 + nrm(ks[8], (DEPTH, A_WIDTH), 0.02),
        'a_ln_b': nrm(ks[9], (DEPTH, A_WIDTH), 0.02),
        'w_spatial': nrm(ks[10], (DEPTH, A_GROUPS, CHUNK, CHUNK), CHUNK ** -0.5),
        'b_spatial': 1.0 + nrm(ks[11], (DEPTH, A_GROUPS, CHUNK), 0.02),
        'w_a_proj': nrm(ks[12], (DEPTH, A_WIDTH, d), A_WIDTH ** -0.5),
        'w_b_proj': nrm(ks[13], (DEPTH, B_OUT_WIDTH, d), B_OUT_WIDTH ** -0.5),
        'w_o': nrm(ks[14], (DEPTH, d, d), d ** -0.5),
        'norm2_g': 1.0 + nrm(ks[15], (DEPTH, d), 0.02),
        'w_group_router': nrm(ks[16], (DEPTH, d, N_EXPERT_GROUPS), d ** -0.5),
        'b_group_router': nrm(ks[17], (DEPTH, N_EXPERT_GROUPS), 0.01),
        'w_expert_router': nrm(ks[18], (DEPTH, d, N_EXPERTS), d ** -0.5),
        'b_expert_router': nrm(ks[19], (DEPTH, N_EXPERTS), 0.01),
        'w_gate': nrm(ks[20], (DEPTH, N_EXPERTS, d, D_EXPERT), d ** -0.5),
        'w_up': nrm(ks[21], (DEPTH, N_EXPERTS, d, D_EXPERT), d ** -0.5),
        'w_down': nrm(ks[22], (DEPTH, N_EXPERTS, D_EXPERT, d), D_EXPERT ** -0.5),
        'final_norm_g': 1.0 + nrm(ks[23], (d,), 0.02),
    }

def reference(x_prompt, x_sample, cache_kv_g0, cache_kv_g1, cache_kv_g2, norm1_g, w_in, b_in, a_ln_g, a_ln_b,
              w_spatial, b_spatial, w_a_proj, w_b_proj, w_o, norm2_g, w_group_router, b_group_router,
              w_expert_router, b_expert_router, w_gate, w_up, w_down, final_norm_g):
    pos_prompt = jnp.arange(x_prompt.shape[1], dtype=jnp.int32)
    pos_sample = PAST_LEN + jnp.arange(x_sample.shape[1], dtype=jnp.int32)
    xp, xs = x_prompt, x_sample
    kv_p = [[] for _ in range(N_DGROUPS)]
    kv_s = [[] for _ in range(N_DGROUPS)]
    v_rows = []
    for l in range(DEPTH):
        lw = (norm1_g[l], w_in[l], b_in[l], a_ln_g[l], a_ln_b[l], w_spatial[l], b_spatial[l],
              w_a_proj[l], w_b_proj[l], w_o[l], norm2_g[l], w_group_router[l], b_group_router[l],
              w_expert_router[l], b_expert_router[l], w_gate[l], w_up[l], w_down[l])
        xp, rows_p, _ = layer_forward(xp, pos_prompt, None, *lw)
        xs, rows_s, v_new = layer_forward(xs, pos_sample, (cache_kv_g0[l], cache_kv_g1[l], cache_kv_g2[l]), *lw)
        for g in range(N_DGROUPS):
            kv_p[g].append(rows_p[g])
            kv_s[g].append(rows_s[g])
        v_rows.append(v_new)
    y_prompt = rms_norm(xp, final_norm_g)
    y_sample = rms_norm(xs, final_norm_g)
    return (y_prompt, y_sample,
            jnp.stack(kv_p[0]), jnp.stack(kv_p[1]), jnp.stack(kv_p[2]),
            jnp.stack(kv_s[0]), jnp.stack(kv_s[1]), jnp.stack(kv_s[2]),
            jnp.stack(v_rows))


_drawn_inputs = setup_inputs


def setup_inputs(seed=0):
    import zlib

    import numpy as np

    out = dict(_drawn_inputs(seed))
    spreads = {}
    factors = {'a_ln_g': 9.011,
     'a_ln_b': 8.624,
     'b_spatial': 10.965,
     'b_group_router': 24.801,
     'b_expert_router': 11.06,
     'final_norm_g': 8.439,
     'cache_kv_g0': 3.002,
     'cache_kv_g2': 4.353,
     'norm2_g': 4.005}
    for name, (base, spread) in spreads.items():
        noise = np.random.default_rng([zlib.crc32(name.encode()), seed]).standard_normal(out[name].shape)
        drawn = base * np.exp(spread * noise) if base else spread * noise
        out[name] = __import__('jax').numpy.asarray(drawn.astype(out[name].dtype))
    for name, factor in factors.items():
        out[name] = (out[name] * factor).astype(out[name].dtype)
    return out
```

```python
from contextlib import ExitStack

import numpy as np

import concourse.bass as bass
from concourse import mybir
from concourse.alu_op_type import AluOpType as ALU

ACT = mybir.ActivationFunctionType
F32 = mybir.dt.float32
F32R = mybir.dt.float32r
I32 = mybir.dt.int32
X = mybir.AxisListType.X

P = 128
D = 1024
KD = D // P
SEQ = 1024
NS = 8
TOK = SEQ + NS
NT = SEQ // P
TILES = NT + 1
PAST = 1024
AW = 512
NG = 3
DIL = (1, 4, 16)
WIN = (128, 512, 2048)
KEEP = tuple(min(w, SEQ) for w in WIN)
CACHED = (128, 128, 64)
H = 4
DH = 64
HW = H * DH
SCALE = DH ** -0.5
EPS = 1e-6
NEG = -1.0e30
NE = 32
NEG_GROUPS = 4
PER_GROUP = 8
DE = 512
BLK = 128
NBMAX = (2 * TOK + NE * (BLK - 1)) // BLK
CW = 256
AR = HW + 2 * H

COL_U, COL_VA, COL_Q, COL_K, COL_V = 0, AW, 2 * AW, 2 * AW + NG * HW, 2 * AW + 2 * NG * HW
COL_GA = 2 * AW + 3 * NG * HW
COL_GB = COL_GA + D
ZW = COL_GB + D

CHUNKS = []
for _g in range(NG):
    CHUNKS += [("q", _g, COL_Q + _g * HW), ("k", _g, COL_K + _g * HW), ("v", _g, COL_V + _g * HW)]
    if _g < 2:
        CHUNKS.append(("va", _g, COL_VA + _g * CW))
CHUNKS += [("u", i, COL_U + i * CW) for i in range(2)]
NC1 = len(CHUNKS)
for _i in range(4):
    CHUNKS += [("ga", _i, COL_GA + _i * CW), ("gb", _i, COL_GB + _i * CW)]
NCH = len(CHUNKS)
TC = 344
NTC = TOK // TC

STEPS = []
for _c in range(NC1):
    if CHUNKS[_c][0] == "u":
        STEPS += [(_c, n, j) for n in range(2) for j in range(NTC)]
    else:
        STEPS += [(_c, t, 0) for t in range(TILES)]
NSTEP = len(STEPS)
FIRST_STEP = [min(i for i, s in enumerate(STEPS) if s[0] == c) for c in range(NC1)]
FIRST_STEP.append(NSTEP)
ATT = [(g, j) for g in range(NG) for j in range(NT)]
ATT_AT = [FIRST_STEP[4 * g + 3] + 1 + j for g, j in ATT]
AT_STEP = {s: a for a, s in enumerate(ATT_AT)}


def rows(t):
    return P if t < NT else NS


def has_prev(g, j):
    return (g == 0 and j > 0) or (g == 1 and j % 2 == 1)


def perm_cols(ap, g, t):
    if t == NT:
        return ap[:, SEQ:TOK]
    if g == 0:
        return ap[:, t * P:(t + 1) * P]
    if g == 1:
        return ap[:, 0:SEQ].rearrange("p (i r) -> p r i", r=4)[:, t // 2, (t % 2) * P:(t % 2 + 1) * P]
    return ap[:, 0:SEQ].rearrange("p (i r) -> p r i", r=NT)[:, t, :]


def perm_rows(ap, g, t, keep=SEQ):
    if g == 0:
        return ap[t * P - (SEQ - keep):(t + 1) * P - (SEQ - keep)]
    if g == 1:
        first = (t % 2) * P - (SEQ - keep) // 4
        return ap.rearrange("(i r) c -> r i c", r=4)[t // 2, first:first + P]
    return ap.rearrange("(i r) c -> r i c", r=NT)[t]


def keeps(g, t):
    return t < NT and (g == 2 or (g == 1 and t % 2 == 1) or (g == 0 and t == NT - 1))


def build(nc, a, out):
    ctx = ExitStack()
    with ctx:
        front = []

        def sem(name):
            front.append(nc.alloc_semaphore(name))
            return front[-1]

        def sem_b(name):
            return ctx.enter_context(nc.semaphore(name))

        def scratch(name, shape, dt=F32):
            return nc.dram_tensor(name, shape, dt, kind="Internal").ap()

        att_d = scratch("att_records", (NG, TOK, AR))
        new_d = scratch("sample_qkv", (NG * 3, NS, HW))
        stat_d = scratch("sample_stats", (NG, 2, NS * H))
        mt_d = scratch("merged_T", (D, TOK))
        x2_d = scratch("x_after_mix", (TOK, D))
        h2_d = scratch("moe_input", (TOK, D))
        tab_d = scratch("slot_token", ((NBMAX + 1) * BLK, 1), I32)
        ys_d = scratch("expert_rows", (NBMAX * BLK, D))

        base = (nc.sbuf_base + 63) // 64 * 64
        top = nc.sbuf_usable_end

        class Region:
            def __init__(self, at, end=top):
                self.at, self.end = at, end

            def __call__(self, name, shape, dt=F32):
                size = int(np.prod(shape[1:])) * 4
                t = nc.alloc_sbuf_tensor_at(name, shape, dt, offset=self.at)
                self.at += (size + 31) // 32 * 32
                assert self.at <= self.end, (name, self.at, self.end)
                return t

        keep = Region(base)
        ident = keep("ident", [P, P])
        logits = keep("logits", [P, TILES, 36])
        dest = keep("dest", [P, TILES, 2], I32)
        gate2 = keep("gate2", [P, TILES, 2])
        blk_e = keep("block_expert", [1, NBMAX + 1], I32)
        nblk = keep("n_blocks", [1, 2], I32)
        bcol = keep("bias_columns", [P, ZW // P])
        eps = keep("epsilon", [P, 1])
        mv = keep("va_moments", [P, TILES, 2])
        ss = keep("square_sums", [P, TILES])
        rstd = keep("rstd", [P, TILES])
        hh_at = keep.at
        r0 = Region(hh_at)
        hh = r0("h_T_hi", [P, KD, TOK], F32R)
        hl = r0("h_T_lo", [P, KD, TOK], F32R)
        raw_at = r0.at
        raw = r0("w_raw", [P, 2, KD, CW])
        wh = r0("w_hi", [P, 2, KD, CW], F32R)
        wl = r0("w_lo", [P, 2, KD, CW], F32R)
        r1_at = r0.at

        psum = ctx.enter_context(nc.psum_tensor("psum", [P, 8, 512], F32))

        def bank(i):
            return psum[:, i, :]

        def chain_of(eng, s):
            n = [0]

            def link(ins):
                n[0] += 1
                ins.then_inc(s, 1)
                eng.wait_ge(s, n[0])
            return link

        w_in_v = a["w_in"][0].rearrange("(k p) n -> p k n", p=P)
        wa_v = a["w_a_proj"][0].rearrange("(k p) n -> p k n", p=P)
        wb_v = a["w_b_proj"][0].rearrange("(k p) n -> p k n", p=P)
        x_rows = [a["x_prompt"][0, t * P:(t + 1) * P] for t in range(NT)] + \
                 [a["x_sample"].rearrange("b s d -> (b s) d")]
        kv_p = [out[2 + g].rearrange("l b s two h e -> (l b s) two (h e)") for g in range(NG)]
        kv_s = [out[5 + g].rearrange("l b s two h e -> (l b s) two (h e)") for g in range(NG)]
        v_chunk = out[8].rearrange("l b s c -> (l b s) c")

        r1 = Region(r1_at)
        va = r1("va", [P, TILES, AW])
        uT = r1("u_T", [P, 4, TOK])
        r1b_at = r1.at
        qT = r1("q_T", [P, 2, SEQ])
        kT = r1("k_T", [P, 2, SEQ])
        vg = r1("v_group", [P, NT, HW])
        cs = r1("cos_sin", [P, TILES, 2 * DH])
        brow = r1("bias_row", [P, 2, CW])
        prob = r1("prob", [P, H, 2 * P])
        probT = r1("prob_T", [P, 2 * H, P])
        rec = r1("record", [P, 4, AR])
        mask = r1("mask_band", [P, 2 * P])
        mask2 = r1("mask_residues", [P, P])
        lnst = r1("ln_stats", [P, 16])
        zr = r1("z_rows", [P, 2, HW])
        rot = r1("rotated", [P, 3, HW])
        rx = Region(r1b_at)
        xin = rx("x_in", [P, 3, D])
        junk = rx("square_junk", [P, D])
        g1row = rx("norm1_row", [P, D])
        brows = rx("bias_rows", [ZW // P, P])
        rl = Region(r1.at)
        ropet = rl("rope_term", [P, 2, HW])

        s_const = sem("const_in")
        s_x = [sem(f"x_in{i}") for i in range(3)]
        s_bT = sem("bias_transposed")
        s_bcol = sem("bias_columns_ready")
        s_eps = sem("epsilon_set")
        s_sq = sem("squares_summed")
        s_hn = sem("h_normed")
        s_hT = sem("h_transposed")
        s_hh = sem("h_hi_ready")
        s_hl = sem("h_lo_ready")
        s_w = [sem(f"w_chunk_in{i}") for i in range(2)]
        s_b = [sem(f"bias_chunk_in{i}") for i in range(2)]
        s_cs = sem("cos_sin_in")
        s_wh = sem("w_hi_ready")
        s_wl = sem("w_lo_ready")
        s_pj = sem("projected")
        s_z = sem("z_rows_ready")
        s_fm = sem("feature_rows_ready")
        s_rope = sem("rotated_ready")
        s_rT = sem("rotated_transposed")
        s_qk = sem("qk_T_ready")
        s_ro = [sem(f"rotated_stored{i}") for i in range(3)]
        s_vo = sem("v_group_stored")
        s_gelu = sem("va_gelu_done")
        s_ln = sem("va_moments_ready")
        s_sc = sem("scores_ready")
        s_sb = sem("scores_masked")
        s_nm = sem("row_max_ready")
        s_ex = sem("prob_ready")
        s_pT = sem("prob_transposed")
        s_pTa = sem("prob_T_half0")
        s_pTb = sem("prob_T_half1")
        s_pv = sem("values_weighted")
        s_rec = sem("record_ready")
        s_recd = [sem(f"record_stored{i}") for i in range(4)]
        s_dve = sem("vector_chain")
        s_pool = sem("pool_chain")

        RING = [i for i, (c, t, _) in enumerate(STEPS)
                if CHUNKS[c][0] in "qk" or (CHUNKS[c][0] == "v" and t == NT)]
        RPOS = {s: n for n, s in enumerate(RING)}

        def stores(i):
            c, t, _ = STEPS[i]
            kind, g, _ = CHUNKS[c]
            if t == NT:
                return 1 if kind == "q" else 2
            return 1 if kind == "k" and keeps(g, t) else 0

        def ring_stored(n):
            return sum(stores(RING[m]) for m in range(n % 3, n + 1, 3))

        def v_stored(g):
            return sum(keeps(gg, t) for gg in range(g + 1) for t in range(NT))

        TRANSPOSED = [i for i in RING if STEPS[i][1] < NT and CHUNKS[STEPS[i][0]][0] in "qk"]
        TPOS = {s: n for n, s in enumerate(TRANSPOSED)}
        ROTATED = [i for i in RING if CHUNKS[STEPS[i][0]][0] in "qk"]
        ROTPOS = {s: n for n, s in enumerate(ROTATED)}
        EVICT_DVE = [i for i, s in enumerate(STEPS) if CHUNKS[s[0]][0] != "u"]
        DPOS = {s: n for n, s in enumerate(EVICT_DVE)}

        def wait_evicted(eng, i):
            if i in DPOS:
                eng.wait_ge(s_z, DPOS[i] + 1)
            else:
                eng.wait_ge(s_fm, i - len(EVICT_DVE) + 1)

        def with_prev(n):
            return sum(has_prev(*ATT[m]) for m in range(n))

        def rec_stored(n):
            return n // 4 + 1

        with nc.Block() as block:
            @block.sync
            def _(sp):
                def load_x(t):
                    if t >= 3:
                        sp.wait_ge(s_hT, t - 2)
                    sp.dma_start(xin[0:rows(t), t % 3, :], x_rows[t]).then_inc(s_x[t % 3], 16)

                def load_chunk(c):
                    kind, _, col = CHUNKS[c]
                    if c >= 2:
                        sp.wait_ge(s_wl, c - 1)
                    sp.dma_start(raw[:, c % 2], w_in_v[:, :, col:col + CW]).then_inc(s_w[c % 2], 16)
                    if kind != "u":
                        if c >= 2:
                            sp.wait_ge(s_z, DPOS[FIRST_STEP[c - 1] - 1] + 1)
                        sp.dma_start(brow[:, c % 2, :], a["b_in"][0, col:col + CW].partition_broadcast(P)) \
                          .then_inc(s_b[c % 2], 16)

                sp.dma_start(ident[:], a["c_ident"]).then_inc(s_const, 16)
                sp.dma_start(g1row[:], a["norm1_g"][0].partition_broadcast(P)).then_inc(s_const, 16)
                for t in range(3):
                    load_x(t)
                sp.dma_start(brows[:], a["b_in"][0].rearrange("(j p) -> j p", p=P)).then_inc(s_const, 16)
                for t in range(3, TILES):
                    load_x(t)
                sp.dma_start(raw[:, 0], w_in_v[:, :, CHUNKS[0][2]:CHUNKS[0][2] + CW]).then_inc(s_w[0], 16)
                sp.dma_start(raw[:, 1], w_in_v[:, :, CHUNKS[1][2]:CHUNKS[1][2] + CW]).then_inc(s_w[1], 16)
                sp.wait_ge(s_hT, TILES)
                for c in range(2):
                    sp.dma_start(brow[:, c], a["b_in"][0, CHUNKS[c][2]:CHUNKS[c][2] + CW].partition_broadcast(P)) \
                      .then_inc(s_b[c], 16)
                sp.dma_start(mask[:], a["c_mask"]).then_inc(s_const, 16)
                sp.dma_start(mask2[:], a["c_mask2"]).then_inc(s_const, 16)

                def store_rows(i):
                    c, t, _ = STEPS[i]
                    kind, g, _ = CHUNKS[c]
                    if kind in "qk":
                        if stores(i):
                            sp.wait_ge(s_rope, ROTPOS[i] + 1)
                    elif t == NT:
                        sp.wait_ge(s_z, DPOS[i] + 1)
                    if i in RPOS:
                        s = RPOS[i] % 3
                        which = "qkv".index(kind)
                        if t == NT:
                            sp.dma_start(new_d[3 * g + which], rot[0:NS, s, :]).then_inc(s_ro[s], 16)
                            if kind != "q":
                                sp.dma_start(kv_s[g][:, which - 1], rot[0:NS, s, :]).then_inc(s_ro[s], 16)
                        elif kind == "k" and keeps(g, t):
                            sp.dma_start(perm_rows(kv_p[g][:, 0], g, t, KEEP[g]), rot[:, s, :]) \
                              .then_inc(s_ro[s], 16)
                    elif kind == "v" and keeps(g, t):
                        sp.wait_ge(s_z, DPOS[i] + 1)
                        sp.dma_start(perm_rows(kv_p[g][:, 1], g, t, KEEP[g]), vg[:, t, :]).then_inc(s_vo, 16)

                def store_record(n):
                    g, j = ATT[n]
                    sp.wait_ge(s_rec, n + 1)
                    sp.dma_start(perm_rows(att_d[g, 0:SEQ], g, j), rec[:, n % 4, :]) \
                      .then_inc(s_recd[n % 4], 16)

                for i in range(NSTEP + 3):
                    c = STEPS[i][0] if i < NSTEP else None
                    if i < NSTEP and i == FIRST_STEP[c]:
                        if CHUNKS[c][0] == "q":
                            g = CHUNKS[c][1]
                            if g:
                                sp.wait_ge(s_rope, ROTPOS[FIRST_STEP[c - 2] - 1] + 1)
                            sp.dma_start(cs[:], a["c_rope"][g].rearrange("t p c -> p t c")).then_inc(s_cs, 16)
                        if 1 <= c and c + 1 < NC1:
                            load_chunk(c + 1)
                    if 2 <= i < NSTEP + 2:
                        store_rows(i - 2)
                    if i - 4 in AT_STEP:
                        store_record(AT_STEP[i - 4])
                for s in range(3):
                    sp.wait_ge(s_ro[s], 16 * ring_stored(max(n for n in range(len(RING)) if n % 3 == s)))
                for s in range(4):
                    sp.wait_ge(s_recd[s], 16 * rec_stored(max(n for n in range(len(ATT)) if n % 4 == s)))
                sp.wait_ge(s_vo, 16 * v_stored(NG - 1))

            @block.gpsimd
            def _(pool):
                link = chain_of(pool, s_pool)
                pool.wait_ge(s_hT, TILES)
                for i in ROTATED:
                    c, t, _ = STEPS[i]
                    g, r, n = CHUNKS[c][1], rows(STEPS[i][1]), ROTPOS[i]
                    slot = RPOS[i] % 3
                    pool.wait_ge(s_z, DPOS[i] + 1)
                    pool.wait_ge(s_cs, 16 * (g + 1))
                    z = zr[0:r, n % 2, :].rearrange("p (h e) -> p h e", h=H)
                    cosb = cs[0:r, t, 0:DH].unsqueeze(1).to_broadcast([r, H, DH])
                    sin_lo = cs[0:r, t, DH:DH + 32].unsqueeze(1).to_broadcast([r, H, 32])
                    sin_hi = cs[0:r, t, DH + 32:2 * DH].unsqueeze(1).to_broadcast([r, H, 32])
                    t0 = ropet[0:r, 0, :].rearrange("p (h e) -> p h e", h=H)
                    t1 = ropet[0:r, 1, :].rearrange("p (h e) -> p h e", h=H)
                    pool.tensor_tensor(t0, z, cosb, ALU.mult).then_inc(s_pool, 1)
                    pool.tensor_tensor(t1[:, :, 0:32], z[:, :, 32:DH], sin_lo, ALU.mult).then_inc(s_pool, 1)
                    pool.tensor_tensor(t1[:, :, 32:DH], z[:, :, 0:32], sin_hi, ALU.mult).then_inc(s_pool, 1)
                    pool.wait_ge(s_pool, 3 * (n + 1))
                    if RPOS[i] >= 3:
                        old = RING[RPOS[i] - 3]
                        if old in TPOS:
                            pool.wait_ge(s_rT, TPOS[old] + 1)
                        if ring_stored(RPOS[old]):
                            pool.wait_ge(s_ro[slot], 16 * ring_stored(RPOS[old]))
                    pool.tensor_tensor(rot[0:r, slot, :], ropet[0:r, 0, :], ropet[0:r, 1, :], ALU.add) \
                        .then_inc(s_rope, 1)
                    pool.wait_ge(s_rope, n + 1)

            @block.scalar
            def _(act):
                def h_hi(t):
                    r = rows(t)
                    act.wait_ge(s_hT, t + 1)
                    for half in range(2):
                        src = bank(3 + 2 * (t % 2) + half).rearrange("p (k q) -> p k q", k=4)[:, :, 0:r]
                        nc.scalar.copy(hh[:, 4 * half:4 * half + 4, t * P:t * P + r], src).then_inc(s_hh, 1)

                act.wait_ge(s_const, 16 * 3)
                act.wait_ge(s_eps, 2)
                act.wait_ge(s_bT, 1)
                nc.scalar.copy(bcol[:], bank(0)[:, 0:ZW // P]).then_inc(s_bcol, 1)
                for t in range(TILES):
                    r = rows(t)
                    act.wait_ge(s_x[t % 3], 16 * (t // 3 + 1))
                    nc.scalar.activation(junk[0:r, :], xin[0:r, t % 3, :], ACT.Square,
                                         accum_out=ss[0:r, t:t + 1]).then_inc(s_sq, 1)
                    if t:
                        h_hi(t - 1)
                    act.wait_ge(s_sq, 2 * t + 1)
                    nc.scalar.activation(ss[0:r, t:t + 1], ss[0:r, t:t + 1], ACT.Sqrt, scale=1.0 / D,
                                         bias=eps[0:r, :]).then_inc(s_sq, 1)
                h_hi(TILES - 1)

                def split_hi(c):
                    act.wait_ge(s_w[c % 2], 16 * (c // 2 + 1))
                    if c >= 2:
                        act.wait_ge(s_pj, FIRST_STEP[c - 1])
                    nc.scalar.activation(wh[:, c % 2].rearrange("p k n -> p (k n)"),
                                         raw[:, c % 2].rearrange("p k n -> p (k n)"),
                                         ACT.Copy).then_inc(s_wh, 1)

                split_hi(0)
                for i in range(NSTEP + 3):
                    if i < NSTEP and STEPS[i][0] + 1 < NC1 and i == FIRST_STEP[STEPS[i][0]] + 1:
                        split_hi(STEPS[i][0] + 1)
                    if i < NSTEP and CHUNKS[STEPS[i][0]][0] == "u":
                        c, n, j = STEPS[i]
                        f = 2 * CHUNKS[c][1] + n
                        act.wait_ge(s_pj, i + 1)
                        act.wait_ge(s_bcol, 1)
                        nc.scalar.activation(uT[:, f, j * TC:(j + 1) * TC], bank(i % 2)[:, 0:TC],
                                             ACT.Gelu_apprx_tanh,
                                             bias=bcol[:, COL_U // P + f:COL_U // P + f + 1]).then_inc(s_fm, 1)
                    if i >= 2 and i - 2 in TPOS:
                        n = TPOS[i - 2]
                        c, t, _ = STEPS[i - 2]
                        dst = qT if CHUNKS[c][0] == "q" else kT
                        act.wait_ge(s_rT, n + 1)
                        nc.scalar.copy(dst[:, :, t * P:(t + 1) * P],
                                       bank(2)[:, 0:2 * P].rearrange("p (a q) -> p a q", a=2)).then_inc(s_qk, 1)
                    if i >= 1 and i - 1 in AT_STEP:
                        b = AT_STEP[i - 1]
                        act.wait_ge(s_pT, b + 1)
                        nc.scalar.copy(probT[:, 0:H, :].rearrange("p a q -> p (a q)"), bank(5)).then_inc(s_pTa, 1)
                    if i in AT_STEP:
                        b = AT_STEP[i]
                        g, j = ATT[b]
                        k0 = 0 if has_prev(g, j) else P
                        act.wait_ge(s_nm, b + 1)
                        for h in range(H):
                            e = nc.scalar.activation(prob[:, h, k0:2 * P], prob[:, h, k0:2 * P], ACT.Exp,
                                                     bias=rec[:, b % 4, HW + h:HW + h + 1],
                                                     accum_out=rec[:, b % 4, HW + H + h:HW + H + h + 1])
                        e.then_inc(s_ex, 1)
                    if i >= 1 and i - 1 < NSTEP and CHUNKS[STEPS[i - 1][0]][0] == "va":
                        c, t, _ = STEPS[i - 1]
                        half = va[0:rows(t), t, CHUNKS[c][1] * CW:(CHUNKS[c][1] + 1) * CW]
                        act.wait_ge(s_z, DPOS[i - 1] + 1)
                        nc.scalar.activation(half, half, ACT.Gelu_apprx_tanh).then_inc(s_gelu, 1)

            @block.vector
            def _(dve):
                link = chain_of(dve, s_dve)
                nc.vector.memset(eps[:], EPS).then_inc(s_eps, 1)
                nc.vector.memset(logits[:, NT, :], 0.0).then_inc(s_eps, 1)
                dve.wait_ge(s_const, 16 * 3)

                def h_lo(t):
                    r = rows(t)
                    for half in range(2):
                        dve.wait_ge(s_hh, 2 * t + half + 1)
                        src = bank(3 + 2 * (t % 2) + half).rearrange("p (k q) -> p k q", k=4)[:, :, 0:r]
                        cols = slice(t * P, t * P + r)
                        ks = slice(4 * half, 4 * half + 4)
                        nc.vector.tensor_tensor(hl[:, ks, cols], src, hh[:, ks, cols].bitcast(F32),
                                                ALU.subtract).then_inc(s_hl, 1)

                for t in range(TILES):
                    r = rows(t)
                    dve.wait_ge(s_sq, 2 * (t + 1))
                    rs = rstd[0:r, t:t + 1]
                    link(nc.vector.reciprocal(rs, ss[0:r, t:t + 1]))
                    nc.vector.scalar_tensor_tensor(xin[0:r, t % 3, :], xin[0:r, t % 3, :], rs, g1row[0:r, :],
                                                   ALU.mult, ALU.mult).then_inc(s_hn, 1)
                    if t:
                        h_lo(t - 1)
                h_lo(TILES - 1)

                def split_lo(c):
                    dve.wait_ge(s_wh, c + 1)
                    nc.vector.tensor_tensor(wl[:, c % 2].rearrange("p k n -> p (k n)"),
                                            raw[:, c % 2].rearrange("p k n -> p (k n)"),
                                            wh[:, c % 2].rearrange("p k n -> p (k n)").bitcast(F32),
                                            ALU.subtract).then_inc(s_wl, 1)

                split_lo(0)
                for i in range(NSTEP + 3):
                    if i < NSTEP and STEPS[i][0] + 1 < NC1 and i == FIRST_STEP[STEPS[i][0]] + 1:
                        split_lo(STEPS[i][0] + 1)
                    if i in DPOS:
                        c, t, _ = STEPS[i]
                        kind, g, _ = CHUNKS[c]
                        r = rows(t)
                        dve.wait_ge(s_pj, i + 1)
                        dve.wait_ge(s_b[c % 2], 16 * (c // 2 + 1))
                        if kind in "qk":
                            if ROTPOS[i] >= 2:
                                dve.wait_ge(s_rope, ROTPOS[i] - 1)
                            dst = zr[0:r, ROTPOS[i] % 2, :]
                        elif kind == "va":
                            dst = va[0:r, t, g * CW:(g + 1) * CW]
                        elif t < NT:
                            if g and t == 0:
                                dve.wait_ge(s_vo, 16 * v_stored(g - 1))
                                dve.wait_ge(s_pv, NT * g)
                            dst = vg[:, t, :]
                        else:
                            old = RING[RPOS[i] - 3]
                            if old in TPOS:
                                dve.wait_ge(s_rT, TPOS[old] + 1)
                            if ring_stored(RPOS[old]):
                                dve.wait_ge(s_ro[RPOS[i] % 3], 16 * ring_stored(RPOS[old]))
                            dst = rot[0:r, RPOS[i] % 3, :]
                        nc.vector.tensor_tensor(dst, bank(i % 2)[0:r, 0:CW], brow[0:r, c % 2, :],
                                                ALU.add).then_inc(s_z, 1)
                    if i >= 2 and i - 2 in AT_STEP:
                        b = AT_STEP[i - 2]
                        dve.wait_ge(s_pv, b + 1)
                        nc.vector.tensor_copy(rec[:, b % 4, 0:HW], bank(7)[:, 0:HW]).then_inc(s_rec, 1)
                    if i >= 1 and i - 1 in AT_STEP:
                        b = AT_STEP[i - 1]
                        if has_prev(*ATT[b]):
                            dve.wait_ge(s_pT, b + 1)
                            nc.vector.tensor_copy(probT[:, H:2 * H, :].rearrange("p a q -> p (a q)"),
                                                  bank(6)).then_inc(s_pTb, 1)
                    if i in AT_STEP:
                        b = AT_STEP[i]
                        g, j = ATT[b]
                        k0 = 0 if has_prev(g, j) else P
                        m = (mask2[:, :] if g == 2 else mask[:, k0:2 * P]).unsqueeze(1)
                        dve.wait_ge(s_sc, b + 1)
                        if b == 0:
                            dve.wait_ge(s_const, 16 * 5)
                        if b:
                            dve.wait_ge(s_pT, b)
                        if b >= 4:
                            dve.wait_ge(s_recd[b % 4], 16 * rec_stored(b - 4))
                        for pair in range(2):
                            src = bank(3 + pair).rearrange("p (h k) -> p h k", h=2)[:, :, k0:2 * P]
                            nc.vector.scalar_tensor_tensor(
                                prob[:, pair:H:2, k0:2 * P], src, SCALE,
                                m.to_broadcast([P, 2, 2 * P - k0]), ALU.mult, ALU.add).then_inc(s_sb, 1)
                        dve.wait_ge(s_sb, 2 * b + 2)
                        nc.vector.tensor_reduce(rec[:, b % 4, HW:HW + H], prob[:, :, k0:2 * P], X, ALU.max,
                                                negate=True).then_inc(s_nm, 1)
                    if i >= 2 and i - 2 < NSTEP and CHUNKS[STEPS[i - 2][0]][:2] == ("va", 1):
                        t = STEPS[i - 2][1]
                        r = rows(t)
                        dve.wait_ge(s_gelu, TILES + t + 1)
                        v = va[0:r, t, :]
                        link(nc.vector.bn_stats(lnst[0:r, 0:6], v))
                        nc.vector.bn_aggr(mv[0:r, t, :], lnst[0:r, 0:6]).then_inc(s_ln, 1)
                        dve.wait_ge(s_ln, t + 1)

            @block.tensor
            def _(pe):
                pe.wait_ge(s_const, 16 * 3)
                nc.tensor.transpose(bank(0)[:, 0:ZW // P], brows[:], ident[0:ZW // P, 0:ZW // P]).then_inc(s_bT, 1)
                for t in range(TILES):
                    r = rows(t)
                    pe.wait_ge(s_hn, t + 1)
                    if t >= 2:
                        pe.wait_ge(s_hl, 2 * (t - 1))
                    for k in range(KD):
                        dst = bank(3 + 2 * (t % 2) + k // 4)[:, (k % 4) * P:(k % 4) * P + r]
                        m = nc.tensor.transpose(dst, xin[0:r, t % 3, k * P:(k + 1) * P], ident[0:r, 0:r])
                    m.then_inc(s_hT, 1)

                def project(i):
                    c, t, j = STEPS[i]
                    kind, g, _ = CHUNKS[c]
                    if i == 0:
                        pe.wait_ge(s_hl, 2 * TILES)
                        pe.wait_ge(s_bcol, 1)
                    if i == FIRST_STEP[c]:
                        pe.wait_ge(s_wl, c + 1)
                    if i >= 2:
                        wait_evicted(pe, i - 2)
                    for k in range(KD):
                        H_, L_ = wh[:, c % 2, k], wl[:, c % 2, k]
                        if kind == "u":
                            dst = bank(i % 2)[:, 0:TC]
                            xs = (hh[:, k, j * TC:(j + 1) * TC], hl[:, k, j * TC:(j + 1) * TC])
                            H_, L_ = H_[:, t * P:(t + 1) * P], L_[:, t * P:(t + 1) * P]
                            trio = ((H_, xs[0]), (H_, xs[1]), (L_, xs[0]))
                        else:
                            dst = bank(i % 2)[0:rows(t), 0:CW]
                            order = g if kind in "qkv" else 0
                            xs = (perm_cols(hh[:, k, :], order, t), perm_cols(hl[:, k, :], order, t))
                            trio = ((xs[0], H_), (xs[0], L_), (xs[1], H_))
                        for n, (st, mv) in enumerate(trio):
                            m = nc.tensor.matmul(dst, st, mv, start=(k == 0 and n == 0),
                                                 stop=(k == KD - 1 and n == 2))
                    m.then_inc(s_pj, 1)

                for i in range(NSTEP + 3):
                    if i < NSTEP:
                        project(i)
                    if i >= 2 and i - 2 in TPOS:
                        n = TPOS[i - 2]
                        pe.wait_ge(s_rope, ROTPOS[i - 2] + 1)
                        if n:
                            pe.wait_ge(s_qk, n)
                        for pair in range(2):
                            m = nc.tensor.transpose(bank(2)[:, pair * P:(pair + 1) * P],
                                                    rot[:, RPOS[i - 2] % 3, pair * P:(pair + 1) * P], ident[:])
                        m.then_inc(s_rT, 1)
                    if i >= 2 and i - 2 in AT_STEP:
                        b = AT_STEP[i - 2]
                        g, j = ATT[b]
                        pe.wait_ge(s_pTa, b + 1)
                        if has_prev(g, j):
                            pe.wait_ge(s_pTb, with_prev(b + 1))
                        if b:
                            pe.wait_ge(s_rec, b)
                        for h in range(H):
                            vcols = slice(h * DH, (h + 1) * DH)
                            m = nc.tensor.matmul(bank(7)[:, vcols], probT[:, h], vg[:, j, vcols],
                                                 start=True, stop=not has_prev(g, j))
                            if has_prev(g, j):
                                m = nc.tensor.matmul(bank(7)[:, vcols], probT[:, H + h], vg[:, j - 1, vcols],
                                                     start=False, stop=True)
                        m.then_inc(s_pv, 1)
                    if i >= 1 and i - 1 in AT_STEP:
                        b = AT_STEP[i - 1]
                        g, j = ATT[b]
                        pe.wait_ge(s_ex, b + 1)
                        if b:
                            pe.wait_ge(s_pTa, b)
                        if with_prev(b):
                            pe.wait_ge(s_pTb, with_prev(b))
                        for h in range(H):
                            m = nc.tensor.transpose(bank(5)[:, h * P:(h + 1) * P], prob[:, h, P:2 * P], ident[:])
                            if has_prev(g, j):
                                m = nc.tensor.transpose(bank(6)[:, h * P:(h + 1) * P], prob[:, h, 0:P], ident[:])
                        m.then_inc(s_pT, 1)
                    if i in AT_STEP:
                        b = AT_STEP[i]
                        g, j = ATT[b]
                        k0 = 0 if has_prev(g, j) else P
                        pe.wait_ge(s_qk, 2 * NT * (g + 1))
                        if b:
                            pe.wait_ge(s_sb, 2 * b)
                        for h in range(H):
                            hp = slice(DH * (h % 2), DH * (h % 2) + DH)
                            keys = kT[hp, h // 2, j * P - P + k0:(j + 1) * P]
                            m = nc.tensor.matmul(bank(3 + h % 2)[:, (h // 2) * 2 * P + k0:(h // 2 + 1) * 2 * P],
                                                 qT[hp, h // 2, j * P:(j + 1) * P], keys, start=True, stop=True)
                        m.then_inc(s_sc, 1)

        r2 = Region(r1b_at)
        sah = r2("s_a_T_hi", [P, 4, TOK], F32R)
        sal = r2("s_a_T_lo", [P, 4, TOK], F32R)
        r2b_at = r2.at
        wsT = r2("w_spatial_T", [P, 8, P])
        wsp = r2("w_spatial_rows", [P, 8, P])
        bsb = r2("b_spatial_rows", [P, 4, P])
        lng = r2("ln_gain_row", [P, AW])
        sar = r2("s_a_T", [P, AW])
        lnb = r2("ln_bias_row", [P, AW])
        causal = r2("causal_T", [P, P])
        w00 = r2("w_spatial_first", [NS, 8])
        b00 = r2("b_spatial_first", [NS, 8])

        s_mc = sem("mix_consts_in")
        s_dve2 = sem("vector_chain_mix")
        s_smix = sem("sample_mix_ready")
        s_wsT = sem("w_spatial_transposed")
        s_wsm = sem("w_spatial_masked")
        s_sd = sem("va_deviation_ready")
        s_ri = sem("va_scale_ready")
        s_nv = sem("va_scaled")
        s_vn = sem("va_normed")
        s_vno = sem("v_chunk_stored")
        s_mx = sem("mixed")
        s_sa = sem("s_a_ready")
        s_sah = sem("s_a_hi_ready")
        s_sal = sem("s_a_lo_ready")

        def split_hi_chunk(act, c):
            act.wait_ge(s_w[c % 2], 16 * (c // 2 + 1))
            nc.scalar.activation(wh[:, c % 2].rearrange("p k n -> p (k n)"),
                                 raw[:, c % 2].rearrange("p k n -> p (k n)"), ACT.Copy).then_inc(s_wh, 1)

        def split_lo_chunk(dve, c):
            dve.wait_ge(s_wh, c + 1)
            nc.vector.tensor_tensor(wl[:, c % 2].rearrange("p k n -> p (k n)"),
                                    raw[:, c % 2].rearrange("p k n -> p (k n)"),
                                    wh[:, c % 2].rearrange("p k n -> p (k n)").bitcast(F32),
                                    ALU.subtract).then_inc(s_wl, 1)

        with nc.Block() as block:
            @block.sync
            def _(sp):
                sp.dma_start(wsp[:], a["w_spatial"][0].rearrange("g t s -> t g s")).then_inc(s_mc, 16)
                sp.dma_start(causal[:], a["c_causal_T"]).then_inc(s_mc, 16)
                sp.dma_start(lng[:], a["a_ln_g"][0].partition_broadcast(P)).then_inc(s_mc, 16)
                sp.dma_start(lnb[:], a["a_ln_b"][0].partition_broadcast(P)).then_inc(s_mc, 16)
                bs = a["b_spatial"][0].rearrange("(m two) t -> two m t", two=2)
                for two in range(2):
                    sp.dma_start(bsb[64 * two:64 * two + 64], bs[two].partition_broadcast(64)).then_inc(s_mc, 16)
                with nc.allow_non_contiguous_dma(reason="eight single elements each"):
                    sp.dma_start(w00[:], a["w_spatial"][0, :, 0, 0:1].rearrange("g o -> o g")[0]
                                 .partition_broadcast(NS)).then_inc(s_mc, 16)
                    sp.dma_start(b00[:], a["b_spatial"][0, :, 0:1].rearrange("g o -> o g")[0]
                                 .partition_broadcast(NS)).then_inc(s_mc, 16)
                for c in range(NC1, NC1 + 2):
                    col = CHUNKS[c][2]
                    sp.dma_start(raw[:, c % 2], w_in_v[:, :, col:col + CW]).then_inc(s_w[c % 2], 16)
                sp.wait_ge(s_vn, TILES)
                sp.dma_start(v_chunk, va[0:NS, NT, :]).then_inc(s_vno, 16)
                sp.wait_ge(s_vno, 16)

            @block.gpsimd
            def _(pool):
                pool.wait_ge(s_mc, 16 * 8)
                for t in range(TILES):
                    r = rows(t)
                    pool.wait_ge(s_nv, t + 1)
                    pool.tensor_tensor(va[0:r, t, :], va[0:r, t, :], lng[0:r, :], ALU.mult).then_inc(s_pool, 1)
                    pool.wait_ge(s_pool, 3 * len(ROTATED) + t + 1)
                    pool.tensor_tensor(va[0:r, t, :], va[0:r, t, :], lnb[0:r, :], ALU.add).then_inc(s_vn, 1)

            @block.scalar
            def _(act):
                nc.scalar.activation(mv[:, 0:NT, 1], mv[:, 0:NT, 1], ACT.Sqrt, bias=eps[:]).then_inc(s_sd, 1)
                nc.scalar.activation(mv[0:NS, NT, 1:2], mv[0:NS, NT, 1:2], ACT.Sqrt,
                                     bias=eps[0:NS, :]).then_inc(s_sd, 1)
                for c in range(NC1, NC1 + 2):
                    split_hi_chunk(act, c)
                for t in range(TILES):
                    r = rows(t)
                    act.wait_ge(s_sa, t + 1)
                    nc.scalar.copy(sah[:, :, t * P:t * P + r],
                                   sar[:, 0:4 * r].rearrange("p (m q) -> p m q", m=4)).then_inc(s_sah, 1)

            @block.vector
            def _(dve):
                link = chain_of(dve, s_dve2)
                dve.wait_ge(s_sd, 2)
                nc.vector.reciprocal(mv[:, 0:NT, 1], mv[:, 0:NT, 1]).then_inc(s_ri, 1)
                nc.vector.reciprocal(mv[0:NS, NT, 1:2], mv[0:NS, NT, 1:2]).then_inc(s_ri, 1)
                dve.wait_ge(s_ri, 2)
                for t in range(TILES):
                    r = rows(t)
                    nc.vector.tensor_scalar(va[0:r, t, :], va[0:r, t, :], mv[0:r, t, 0:1], mv[0:r, t, 1:2],
                                            ALU.subtract, ALU.mult).then_inc(s_nv, 1)
                dve.wait_ge(s_mc, 16 * 8)
                for half in range(2):
                    dve.wait_ge(s_wsT, half + 1)
                    nc.vector.tensor_tensor(wsT[:, 4 * half:4 * half + 4, :],
                                            bank(6 + half).rearrange("p (g t) -> p g t", g=4),
                                            causal[:].unsqueeze(1).to_broadcast([P, 4, P]),
                                            ALU.mult).then_inc(s_wsm, 1)
                split_lo_chunk(dve, NC1)
                split_lo_chunk(dve, NC1 + 1)
                for t in range(TILES):
                    r = rows(t)
                    cols = slice(t * P, t * P + r)
                    sa4 = sar[:, 0:4 * r].rearrange("p (m q) -> p m q", m=4)
                    ps4 = bank(t % 2)[:, 0:4 * r].rearrange("p (m q) -> p m q", m=4)
                    if t == NT:
                        dve.wait_ge(s_vn, TILES)
                        dve.wait_ge(s_sal, NT)
                        v8 = sar[0:NS, :].rearrange("p (g c) -> p g c", g=8)
                        link(nc.vector.tensor_tensor(v8, va[0:NS, NT, :].rearrange("p (g c) -> p g c", g=8),
                                                     w00[:].unsqueeze(2).to_broadcast([NS, 8, 64]), ALU.mult))
                        nc.vector.tensor_tensor(v8, v8, b00[:].unsqueeze(2).to_broadcast([NS, 8, 64]),
                                                ALU.add).then_inc(s_smix, 1)
                        dve.wait_ge(s_mx, TILES)
                        nc.vector.tensor_tensor(sa4, ps4, uT[:, :, cols], ALU.mult).then_inc(s_sa, 1)
                    else:
                        dve.wait_ge(s_mx, t + 1)
                        if t:
                            dve.wait_ge(s_sal, t)
                        link(nc.vector.tensor_tensor(sa4, ps4, bsb[:], ALU.add))
                        nc.vector.tensor_tensor(sa4, sa4, uT[:, :, cols], ALU.mult).then_inc(s_sa, 1)
                    dve.wait_ge(s_sah, t + 1)
                    nc.vector.tensor_tensor(sal[:, :, cols], sa4, sah[:, :, cols].bitcast(F32),
                                            ALU.subtract).then_inc(s_sal, 1)

            @block.tensor
            def _(pe):
                pe.wait_ge(s_mc, 16 * 8)
                for g in range(8):
                    m = nc.tensor.transpose(bank(6 + g // 4)[:, (g % 4) * P:(g % 4 + 1) * P], wsp[:, g, :], ident[:])
                    if g % 4 == 3:
                        m.then_inc(s_wsT, 1)
                pe.wait_ge(s_wsm, 2)
                for t in range(NT):
                    pe.wait_ge(s_vn, t + 1)
                    if t >= 2:
                        pe.wait_ge(s_sa, t - 1)
                    for g in range(8):
                        dst = bank(t % 2)[64 * (g % 2):64 * (g % 2) + 64, (g // 2) * P:(g // 2 + 1) * P]
                        m = nc.tensor.matmul(dst, va[:, t, g * 64:(g + 1) * 64], wsT[:, g, :], start=True, stop=True)
                    m.then_inc(s_mx, 1)
                pe.wait_ge(s_smix, 1)
                for m4 in range(4):
                    m = nc.tensor.transpose(bank(NT % 2)[:, m4 * NS:(m4 + 1) * NS], sar[0:NS, m4 * P:(m4 + 1) * P],
                                            ident[0:NS, 0:NS])
                m.then_inc(s_mx, 1)

        r3 = Region(r1_at, r1b_at)
        kc = r3("cached_kv", [P, NS, 2 * HW])
        qb = r3("sample_q_rows", [P, NS, HW])
        us = r3("sample_values", [H, NS, HW])
        r3b = Region(r2b_at)
        oh_ = r3b("o_T_hi", [P, 2, TOK], F32R)
        ol_ = r3b("o_T_lo", [P, 2, TOK], F32R)
        cmb_at = r3b.at
        cmb = r3b("records", [P, 2, NG, AR])
        ocm = r3b("combined_rows", [P, HW])
        wgt = r3b("chunk_weights", [P, 6, H])
        nrm = r3b("chunk_sums", [P, 6, H])
        mlo = r3b("least_minus_max", [P, H])
        den = r3b("denominator", [P, H])
        r3r = Region(raw_at, raw_at + 2 * KD * CW * 4)
        new = r3r("sample_new", [NS, 9, HW])
        ssc = r3r("sample_scores", [P, NS * H])
        spT = r3r("sample_prob_T", [P, NS * H])
        prs = r3r("sample_prob", [NS * H, P])
        sst = r3r("sample_row_stats", [NS * H, NG, 2])
        st6 = r3r("sample_stats6", [NS, 2, 6, H])

        s_kc = sem("cached_kv_in")
        s_qb = sem("sample_q_in")
        s_new = sem("sample_new_in")
        s_cd = sem("vector_chain_combine")
        s_ss = sem("sample_scores_ready")
        s_ssT = sem("sample_scores_transposed")
        s_snm = sem("sample_max_ready")
        s_sex = sem("sample_prob_ready")
        s_spT = sem("sample_prob_transposed")
        s_spc = sem("sample_prob_T_ready")
        s_spv = sem("sample_values_in_psum")
        s_us = sem("sample_values_ready")
        s_uso = sem("sample_records_stored")
        s_cm = [sem(f"records_in{i}") for i in range(2)]
        s_scu = sem("sample_records_in")
        s_cdf = sem("chunk_differences_ready")
        s_cw = sem("chunk_weights_ready")
        s_oc = sem("combined_ready")
        s_oT = sem("combined_transposed")
        s_oh = sem("o_T_hi_ready")
        s_ol = sem("o_T_lo_ready")

        with nc.Block() as block:
            @block.sync
            def _(sp):
                caches = [a[f"cache_kv_g{g}"][0].rearrange("b (s d) two h e -> s b d (two h e)", d=d)[:, :, 0, :]
                          for g, d in enumerate(DIL)]

                def load_group(g):
                    if g:
                        sp.wait_ge(s_spv, g)
                    sp.dma_start(kc[0:CACHED[g]], caches[g]).then_inc(s_kc, 16)
                    sp.dma_start(qb[:].rearrange("p b c -> p (b c)"),
                                 new_d[3 * g].rearrange("b c -> (b c)").partition_broadcast(P)).then_inc(s_qb, 16)

                def load_records(t):
                    if t >= 2:
                        sp.wait_ge(s_oc, t - 1)
                    sp.dma_start(cmb[:, t % 2], att_d[:, t * P:(t + 1) * P, :].rearrange("g t c -> t g c")) \
                        .then_inc(s_cm[t % 2], 16)

                load_group(0)
                sp.dma_start(new[:], new_d.rearrange("n b c -> b n c")).then_inc(s_new, 16)
                load_records(0)
                load_records(1)
                for g in range(NG):
                    if g + 1 < NG:
                        load_group(g + 1)
                    sp.wait_ge(s_us, g + 1)
                    for h in range(H):
                        sp.dma_start(att_d[g, SEQ:TOK, h * DH:(h + 1) * DH],
                                     us[h:h + 1, :, h * DH:(h + 1) * DH]).then_inc(s_uso, 16)
                    for n in range(2):
                        sp.dma_start(stat_d[g, n].rearrange("(r o) -> r o", o=1), sst[:, g, n:n + 1]) \
                            .then_inc(s_uso, 16)
                for t in range(2, NT):
                    load_records(t)
                sp.wait_ge(s_uso, 16 * 6 * NG)
                sp.wait_ge(s_oc, NT - 1)
                sp.dma_start(cmb[0:NS, 0, :, 0:HW], att_d[:, SEQ:TOK, 0:HW].rearrange("g b c -> b g c")) \
                    .then_inc(s_scu, 16)
                for n in range(2):
                    sp.dma_start(st6[:, n, 0:NG, :], stat_d[:, n].rearrange("g (b h) -> b g h", h=H)) \
                        .then_inc(s_scu, 16)

            @block.scalar
            def _(act):
                def group_exp(g):
                    nk = CACHED[g]
                    act.wait_ge(s_snm, g + 1)
                    nc.scalar.activation(prs[:, 0:nk], prs[:, 0:nk], ACT.Exp, bias=sst[:, g, 0:1],
                                         accum_out=sst[:, g, 1:2]).then_inc(s_sex, 1)
                    act.wait_ge(s_spv, g + 1)
                    if g:
                        act.wait_ge(s_uso, 16 * 6 * g)
                    for half in range(2):
                        u = nc.scalar.copy(us[:, 4 * half:4 * half + 4, :].rearrange("p b c -> p (b c)"),
                                           psum[0:H, 2 * half:2 * half + 2, :].rearrange("p b c -> p (b c)"))
                    u.then_inc(s_us, 1)

                for t in range(TILES + 1):
                    if t < NG:
                        group_exp(t)
                    if t < TILES:
                        n = 6 if t == NT else NG
                        r = rows(t)
                        act.wait_ge(s_cdf, t + 1)
                        nc.scalar.activation(wgt[0:r, 0:n], nrm[0:r, 0:n], ACT.Exp).then_inc(s_cw, 1)
                    if t:
                        r = rows(t - 1)
                        cols = slice((t - 1) * P, (t - 1) * P + r)
                        act.wait_ge(s_oT, t)
                        nc.scalar.copy(oh_[:, :, cols], bank(6)[:, 0:2 * r].rearrange("p (a q) -> p a q", a=2)) \
                            .then_inc(s_oh, 1)

            @block.vector
            def _(dve):
                link = chain_of(dve, s_cd)

                def group_scores(g):
                    nk = CACHED[g]
                    dve.wait_ge(s_kc, 16 * (g + 1))
                    dve.wait_ge(s_qb, 16 * (g + 1))
                    if g:
                        dve.wait_ge(s_ssT, g)
                    link(nc.vector.tensor_tensor(kc[0:nk, :, 0:HW], kc[0:nk, :, 0:HW], qb[0:nk], ALU.mult))
                    nc.vector.tensor_reduce(ssc[0:nk, :],
                                            kc[0:nk, :, 0:HW].rearrange("p b (h e) -> p b h e", h=H),
                                            X, ALU.add).then_inc(s_ss, 1)

                def group_max(g):
                    nk = CACHED[g]
                    dve.wait_ge(s_ssT, g + 1)
                    if g:
                        dve.wait_ge(s_spT, g)
                    link(nc.vector.tensor_scalar(prs[:, 0:nk], bank(4)[0:NS * H, 0:nk], SCALE, None, ALU.mult))
                    nc.vector.tensor_reduce(sst[:, g, 0:1], prs[:, 0:nk], X, ALU.max, negate=True).then_inc(s_snm, 1)
                    dve.wait_ge(s_spT, g + 1)
                    if g:
                        dve.wait_ge(s_spv, g)
                    nc.vector.tensor_copy(spT[0:nk, :], bank(5)[0:nk, 0:NS * H]).then_inc(s_spc, 1)

                def combine(t):
                    r = rows(t)
                    if t < NT:
                        n = NG
                        dve.wait_ge(s_cm[t % 2], 16 * (t // 2 + 1))
                        rec_ = cmb[:, t % 2]
                        nm, ls = rec_[:, :, HW:HW + H], rec_[:, :, HW + H:AR]
                    else:
                        n = 6
                        dve.wait_ge(s_scu, 16 * 3)
                        dve.wait_ge(s_new, 16)
                        rec_ = cmb[0:NS, 0]
                        q3 = new[:].rearrange("p (g w) c -> p g w c", g=NG)
                        link(nc.vector.tensor_tensor(q3[:, :, 0, :], q3[:, :, 0, :], q3[:, :, 1, :], ALU.mult))
                        link(nc.vector.tensor_reduce(st6[:, 0, NG:6, :],
                                                     q3[:, :, 0, :].rearrange("p g (h e) -> p g h e", h=H),
                                                     X, ALU.add))
                        link(nc.vector.tensor_scalar(st6[:, 0, NG:6, :], st6[:, 0, NG:6, :], -SCALE, None,
                                                     ALU.mult))
                        link(nc.vector.memset(st6[:, 1, NG:6, :], 1.0))
                        nm, ls = st6[:, 0], st6[:, 1]
                    lo, w, dd = mlo[0:r, :], wgt[0:r, 0:n], den[0:r, :]
                    link(nc.vector.tensor_reduce(lo, nm.rearrange("p g h -> p h g"), X, ALU.min))
                    if t:
                        dve.wait_ge(s_cw, t)
                    nc.vector.tensor_tensor(nrm[0:r, 0:n], lo.unsqueeze(1).to_broadcast([r, n, H]), nm,
                                            ALU.subtract).then_inc(s_cdf, 1)
                    dve.wait_ge(s_cw, t + 1)
                    link(nc.vector.tensor_tensor(nrm[0:r, 0:n], w, ls, ALU.mult))
                    link(nc.vector.tensor_reduce(dd, nrm[0:r, 0:n].rearrange("p g h -> p h g"), X, ALU.add))
                    link(nc.vector.reciprocal(dd, dd))
                    link(nc.vector.tensor_tensor(w, w, dd.unsqueeze(1).to_broadcast([r, n, H]), ALU.mult))
                    u4 = rec_[:, :, 0:HW].rearrange("p g (h e) -> p g h e", h=H)
                    link(nc.vector.tensor_tensor(u4, u4, w[:, 0:NG].unsqueeze(3).to_broadcast([r, NG, H, DH]),
                                                 ALU.mult))
                    if t:
                        dve.wait_ge(s_oT, t)
                    red = nc.vector.tensor_reduce(ocm[0:r, :], rec_[:, :, 0:HW].rearrange("p g c -> p c g"),
                                                  X, ALU.add)
                    if t < NT:
                        red.then_inc(s_oc, 1)
                    else:
                        link(red)
                        vs = new[:].rearrange("p (g w) c -> p g w c", g=NG)
                        for g in range(NG):
                            v3 = vs[:, g, 2, :].rearrange("p (h e) -> p h e", h=H)
                            link(nc.vector.tensor_tensor(v3, v3, w[:, NG + g].unsqueeze(2)
                                                         .to_broadcast([NS, H, DH]), ALU.mult))
                            add = nc.vector.tensor_tensor(ocm[0:NS, :], ocm[0:NS, :], vs[:, g, 2, :], ALU.add)
                            if g < NG - 1:
                                link(add)
                        add.then_inc(s_oc, 1)

                for t in range(TILES + 1):
                    if t < NG:
                        group_scores(t)
                        group_max(t)
                    if t < TILES:
                        combine(t)
                    if t:
                        r = rows(t - 1)
                        cols = slice((t - 1) * P, (t - 1) * P + r)
                        dve.wait_ge(s_oh, t)
                        nc.vector.tensor_tensor(ol_[:, :, cols], bank(6)[:, 0:2 * r].rearrange("p (a q) -> p a q", a=2),
                                                oh_[:, :, cols].bitcast(F32), ALU.subtract).then_inc(s_ol, 1)

            @block.tensor
            def _(pe):
                for t in range(TILES):
                    if t < NG:
                        g, nk = t, CACHED[t]
                        pe.wait_ge(s_ss, g + 1)
                        if g:
                            pe.wait_ge(s_snm, g)
                        nc.tensor.transpose(bank(4)[0:NS * H, 0:nk], ssc[0:nk, :], ident[0:nk, 0:nk]).then_inc(s_ssT, 1)
                        pe.wait_ge(s_sex, g + 1)
                        if g:
                            pe.wait_ge(s_spc, g)
                        nc.tensor.transpose(bank(5)[0:nk, 0:NS * H], prs[:, 0:nk],
                                            ident[0:NS * H, 0:NS * H]).then_inc(s_spT, 1)
                        pe.wait_ge(s_spc, g + 1)
                        if g:
                            pe.wait_ge(s_us, g)
                        for b in range(NS):
                            m = nc.tensor.matmul(bank(b // 2)[0:H, (b % 2) * HW:(b % 2 + 1) * HW],
                                                 spT[0:nk, b * H:(b + 1) * H], kc[0:nk, b, HW:2 * HW],
                                                 start=True, stop=True)
                        m.then_inc(s_spv, 1)
                    r = rows(t)
                    pe.wait_ge(s_oc, t + 1)
                    if t:
                        pe.wait_ge(s_ol, t)
                    for pair in range(2):
                        m = nc.tensor.transpose(bank(6)[:, pair * r:(pair + 1) * r], ocm[0:r, pair * P:(pair + 1) * P],
                                                ident[0:r, 0:r])
                    m.then_inc(s_oT, 1)

        r4 = Region(r1_at, r1b_at)
        abh = r4("proj_hi", [P, 2, 4, CW], F32R)
        abl = r4("proj_lo", [P, 2, 4, CW], F32R)
        abr = r4("proj_raw", [P, 4, CW])
        mrg = r4("merged_T", [P, 2, TOK])
        sig = r4("gate_sigmoid", [P, 2, TC])
        prd = r4("gated_product", [P, 2, TC])

        s_ab = sem("proj_in")
        s_abh = sem("proj_hi_ready")
        s_abl = sem("proj_lo_ready")
        s_gt = sem("gate_products")
        s_pr = sem("proj_products")
        s_sg = sem("sigmoid_ready")
        s_gp = sem("gated_ready")
        s_mg = sem("merged_ready")
        s_mo = [sem(f"merged_stored{n}") for n in range(2)]
        zero = Region(cmb_at)("zero_rows", [P, D])
        s_zr = sem("zero_rows_set")
        s_zf = sem("expert_rows_cleared")
        FULL = 2 * TOK // BLK
        NU = NCH - NC1
        GS = [(u, n, j) for u in range(NU) for n in range(2) for j in range(NTC)]

        def proj_k(u):
            return 4 if u % 2 == 0 else 2

        with nc.Block() as block:
            @block.sync
            def _(sp):
                def load_unit(u):
                    if u:
                        sp.wait_ge(s_abl, u)
                    cols = slice((u // 2) * CW, (u // 2 + 1) * CW)
                    w = wa_v if u % 2 == 0 else wb_v
                    sp.dma_start(abr[:, 0:proj_k(u)], w[:, :, cols]).then_inc(s_ab, 16)

                def store_merged(i, n):
                    sp.wait_ge(s_mg, (2 * i + n + 1) * NTC)
                    row = (2 * i + n) * P
                    sp.dma_start(mt_d[row:row + P, :], mrg[:, n, :]).then_inc(s_mo[n], 16)

                load_unit(0)
                sp.wait_ge(s_zr, 1)
                sp.dma_start(ys_d[FULL * BLK:].rearrange("(b p) c -> p b c", p=P),
                             zero[:].unsqueeze(1).to_broadcast([P, NBMAX - FULL, D])).then_inc(s_zf, 16)
                for u in range(NU):
                    if u + 1 < NU:
                        load_unit(u + 1)
                    if u + 2 < NU:
                        c = NC1 + u + 2
                        sp.wait_ge(s_wl, c - 1)
                        sp.dma_start(raw[:, c % 2], w_in_v[:, :, CHUNKS[c][2]:CHUNKS[c][2] + CW]) \
                            .then_inc(s_w[c % 2], 16)
                    if u % 2 == 0 and u:
                        store_merged(u // 2 - 1, 0)
                        store_merged(u // 2 - 1, 1)
                store_merged(NU // 2 - 1, 0)
                store_merged(NU // 2 - 1, 1)
                for n in range(2):
                    sp.wait_ge(s_mo[n], 16 * (NU // 2))
                sp.wait_ge(s_zf, 16)

            @block.gpsimd
            def _(pool):
                pool.memset(zero[:], 0.0).then_inc(s_zr, 1)

            @block.scalar
            def _(act):
                def unit_hi(u):
                    act.wait_ge(s_ab, 16 * (u + 1))
                    if u >= 2:
                        act.wait_ge(s_pr, 6 * (u - 1))
                    nc.scalar.copy(abh[:, u % 2, 0:proj_k(u)], abr[:, 0:proj_k(u)]).then_inc(s_abh, 1)

                unit_hi(0)
                for s, (u, n, j) in enumerate(GS):
                    if n == 0 and j == 1:
                        if u + 1 < NU:
                            unit_hi(u + 1)
                            if u:
                                act.wait_ge(s_gt, 6 * u)
                                split_hi_chunk(act, NC1 + u + 1)
                    f = (2 * (u // 2) + n) + (COL_GA if u % 2 == 0 else COL_GB) // P
                    act.wait_ge(s_gt, s + 1)
                    if s >= 2:
                        act.wait_ge(s_gp, s - 1)
                    nc.scalar.activation(sig[:, s % 2], bank(s % 2)[:, 0:TC], ACT.Sigmoid,
                                         bias=bcol[:, f:f + 1]).then_inc(s_sg, 1)

            @block.vector
            def _(dve):
                def unit_lo(u):
                    dve.wait_ge(s_abh, u + 1)
                    nc.vector.tensor_tensor(abl[:, u % 2, 0:proj_k(u)], abr[:, 0:proj_k(u)],
                                            abh[:, u % 2, 0:proj_k(u)].bitcast(F32), ALU.subtract).then_inc(s_abl, 1)

                unit_lo(0)
                nm = 0
                for s, (u, n, j) in enumerate(GS):
                    if n == 0 and j == 1:
                        if u + 1 < NU:
                            unit_lo(u + 1)
                            if u:
                                split_lo_chunk(dve, NC1 + u + 1)
                    dst = mrg[:, n, j * TC:(j + 1) * TC]
                    dve.wait_ge(s_sg, s + 1)
                    dve.wait_ge(s_pr, s + 1)
                    if u % 2 == 0:
                        if u:
                            dve.wait_ge(s_mo[n], 16 * (u // 2))
                        nc.vector.tensor_tensor(dst, bank(2 + s % 2)[:, 0:TC], sig[:, s % 2], ALU.mult) \
                            .then_inc(s_gp, 1)
                    else:
                        if nm >= 2:
                            dve.wait_ge(s_mg, nm - 1)
                        nc.vector.tensor_tensor(prd[:, nm % 2], bank(2 + s % 2)[:, 0:TC], sig[:, s % 2], ALU.mult) \
                            .then_inc(s_gp, 1)
                        dve.wait_ge(s_gp, s + 1)
                        nc.vector.tensor_tensor(dst, dst, prd[:, nm % 2], ALU.add).then_inc(s_mg, 1)
                        nm += 1

            @block.tensor
            def _(pe):
                for s, (u, n, j) in enumerate(GS):
                    c = NC1 + u
                    tok, col = slice(j * TC, (j + 1) * TC), slice(n * P, (n + 1) * P)
                    pe.wait_ge(s_wl, c + 1)
                    if s >= 2:
                        pe.wait_ge(s_sg, s - 1)
                    for k in range(KD):
                        for i, (w_, x_) in enumerate(((wh, hh), (wh, hl), (wl, hh))):
                            m = nc.tensor.matmul(bank(s % 2)[:, 0:TC], w_[:, c % 2, k, col], x_[:, k, tok],
                                                 start=(k == 0 and i == 0), stop=(k == KD - 1 and i == 2))
                    m.then_inc(s_gt, 1)
                    pe.wait_ge(s_abl, u + 1)
                    if s >= 2:
                        pe.wait_ge(s_gp, s - 1)
                    xh, xl = (sah, sal) if u % 2 == 0 else (oh_, ol_)
                    for k in range(proj_k(u)):
                        for i, (w_, x_) in enumerate(((abh, xh), (abh, xl), (abl, xh))):
                            m = nc.tensor.matmul(bank(2 + s % 2)[:, 0:TC], w_[:, u % 2, k, col], x_[:, k, tok],
                                                 start=(k == 0 and i == 0), stop=(k == proj_k(u) - 1 and i == 2))
                    m.then_inc(s_pr, 1)

        nc.clear_and_free_semaphores(front)
        nc.all_engine_barrier()

        rw = Region(hh_at, raw_at)
        woh = rw("w_o_hi", [P, KD, D], F32R)
        wol = rw("w_o_lo", [P, KD, D], F32R)
        r5 = Region(r1_at)
        mtr = r5("merged_raw", [P, 2, KD, P])
        mth = r5("merged_hi", [P, 2, KD, P], F32R)
        mtl = r5("merged_lo", [P, 2, KD, P], F32R)
        xo = r5("x_rows", [P, 2, D])
        x2 = r5("x_mixed", [P, 2, D])
        h2 = r5("moe_rows", [P, 2, D])
        h2T = r5("moe_T", [P, 2, KD, P])
        jk5 = r5("square_junk2", [P, D])
        g2row = r5("norm2_row", [P, D])
        wr = r5("w_router", [P, KD, 36])
        brr = r5("b_router_row", [P, 36])
        z5 = r5("no_tokens", [P, NBMAX + 1], I32)

        s_rc = sem_b("router_consts_in")
        s_wo = [sem_b(f"w_o_chunk_in{i}") for i in range(2)]
        s_woh = sem_b("w_o_hi_ready")
        s_wol = sem_b("w_o_lo_ready")
        s_mi = [sem_b(f"merged_in{i}") for i in range(2)]
        s_xi = [sem_b(f"x_rows_in{i}") for i in range(2)]
        s_mth = sem_b("merged_hi_ready")
        s_mtl = sem_b("merged_lo_ready")
        s_wop = sem_b("w_o_products")
        s_x2 = sem_b("x_mixed_ready")
        s_x2o = [sem_b(f"x_mixed_stored{i}") for i in range(2)]
        s_sq5 = sem_b("squares2_summed")
        s_h2 = sem_b("moe_rows_ready")
        s_h2o = [sem_b(f"moe_rows_stored{i}") for i in range(2)]
        s_h2T = sem_b("moe_transposed")
        s_h2c = sem_b("moe_T_ready")
        s_rt = sem_b("router_products")
        s_lg = sem_b("logits_ready")
        s_c5 = sem_b("vector_chain_router")
        s_tab = sem_b("slot_table_cleared")

        with nc.Block() as block:
            @block.sync
            def _(sp):
                wo_v = a["w_o"][0].rearrange("(k p) n -> p k n", p=P)

                def load_wo(c):
                    if c >= 2:
                        sp.wait_ge(s_wol, c - 1)
                    sp.dma_start(raw[:, c % 2], wo_v[:, :, c * CW:(c + 1) * CW]).then_inc(s_wo[c % 2], 16)

                def load_tile(t):
                    r = rows(t)
                    if t >= 2:
                        sp.wait_ge(s_mtl, t - 1)
                        sp.wait_ge(s_x2, 2 * (t - 1))
                    sp.dma_start(mtr[:, t % 2, :, 0:r],
                                 mt_d[:, t * P:t * P + r].rearrange("(k p) q -> p k q", p=P)).then_inc(s_mi[t % 2], 16)
                    sp.dma_start(xo[0:r, t % 2, :], x_rows[t]).then_inc(s_xi[t % 2], 16)

                load_wo(0)
                load_wo(1)
                load_tile(0)
                load_wo(2)
                load_wo(3)
                load_tile(1)
                sp.dma_start(g2row[:], a["norm2_g"][0].partition_broadcast(P)).then_inc(s_rc, 16)
                sp.dma_start(wr[:, :, 0:4], a["w_group_router"][0].rearrange("(k p) n -> p k n", p=P)).then_inc(s_rc, 16)
                sp.dma_start(wr[:, :, 4:36], a["w_expert_router"][0].rearrange("(k p) n -> p k n", p=P)) \
                    .then_inc(s_rc, 16)
                sp.dma_start(brr[:, 0:4], a["b_group_router"][0].partition_broadcast(P)).then_inc(s_rc, 16)
                sp.dma_start(brr[:, 4:36], a["b_expert_router"][0].partition_broadcast(P)).then_inc(s_rc, 16)
                sp.dma_start(z5[:], a["c_zero"]).then_inc(s_rc, 16)
                sp.wait_ge(s_rc, 16 * 6)
                sp.dma_start(tab_d.rearrange("(p c) o -> p (c o)", p=P), z5[:]).then_inc(s_tab, 16)
                for t in range(TILES):
                    r = rows(t)
                    if t + 2 < TILES:
                        load_tile(t + 2)
                    sp.wait_ge(s_x2, 2 * (t + 1))
                    sp.dma_start(x2_d[t * P:t * P + r], x2[0:r, t % 2, :]).then_inc(s_x2o[t % 2], 16)
                    sp.wait_ge(s_h2, t + 1)
                    sp.dma_start(h2_d[t * P:t * P + r], h2[0:r, t % 2, :]).then_inc(s_h2o[t % 2], 16)
                for i in range(2):
                    sp.wait_ge(s_x2o[i], 16 * len(range(i, TILES, 2)))
                    sp.wait_ge(s_h2o[i], 16 * len(range(i, TILES, 2)))
                sp.wait_ge(s_tab, 16)

            @block.scalar
            def _(act):
                def tile_hi(t):
                    r = rows(t)
                    act.wait_ge(s_mi[t % 2], 16 * (t // 2 + 1))
                    if t >= 2:
                        act.wait_ge(s_wop, t - 1)
                    nc.scalar.copy(mth[:, t % 2, :, 0:r], mtr[:, t % 2, :, 0:r]).then_inc(s_mth, 1)

                def wo_hi(c):
                    act.wait_ge(s_wo[c % 2], 16 * (c // 2 + 1))
                    nc.scalar.copy(woh[:, :, c * CW:(c + 1) * CW], raw[:, c % 2]).then_inc(s_woh, 1)

                wo_hi(0)
                wo_hi(1)
                tile_hi(0)
                wo_hi(2)
                wo_hi(3)
                for t in range(TILES + 1):
                    if t + 1 < TILES:
                        tile_hi(t + 1)
                    if t < TILES:
                        r = rows(t)
                        act.wait_ge(s_x2, 2 * (t + 1))
                        nc.scalar.activation(jk5[0:r, :], x2[0:r, t % 2, :], ACT.Square,
                                             accum_out=ss[0:r, t:t + 1]).then_inc(s_sq5, 1)
                        act.wait_ge(s_sq5, 2 * t + 1)
                        nc.scalar.activation(ss[0:r, t:t + 1], ss[0:r, t:t + 1], ACT.Sqrt, scale=1.0 / D,
                                             bias=eps[0:r, :]).then_inc(s_sq5, 1)
                    if t:
                        r = rows(t - 1)
                        act.wait_ge(s_h2T, t)
                        for half in range(2):
                            nc.scalar.copy(h2T[:, (t - 1) % 2, 4 * half:4 * half + 4, 0:r],
                                           bank(4 + half).rearrange("p (k q) -> p k q", k=4)[:, :, 0:r]) \
                                .then_inc(s_h2c, 1)

            @block.vector
            def _(dve):
                link = chain_of(dve, s_c5)

                def tile_lo(t):
                    r = rows(t)
                    dve.wait_ge(s_mth, t + 1)
                    nc.vector.tensor_tensor(mtl[:, t % 2, :, 0:r], mtr[:, t % 2, :, 0:r],
                                            mth[:, t % 2, :, 0:r].bitcast(F32), ALU.subtract).then_inc(s_mtl, 1)

                def wo_lo(c):
                    dve.wait_ge(s_woh, c + 1)
                    nc.vector.tensor_tensor(wol[:, :, c * CW:(c + 1) * CW], raw[:, c % 2],
                                            woh[:, :, c * CW:(c + 1) * CW].bitcast(F32),
                                            ALU.subtract).then_inc(s_wol, 1)

                wo_lo(0)
                wo_lo(1)
                tile_lo(0)
                wo_lo(2)
                wo_lo(3)
                for t in range(TILES + 1):
                    if t + 1 < TILES:
                        tile_lo(t + 1)
                    if t < TILES:
                        r = rows(t)
                        dve.wait_ge(s_wop, t + 1)
                        dve.wait_ge(s_xi[t % 2], 16 * (t // 2 + 1))
                        if t >= 2:
                            dve.wait_ge(s_x2o[t % 2], 16 * (t // 2))
                        for half in range(2):
                            cols = slice(512 * half, 512 * half + 512)
                            nc.vector.tensor_tensor(x2[0:r, t % 2, cols], bank(2 * (t % 2) + half)[0:r, :],
                                                    xo[0:r, t % 2, cols], ALU.add).then_inc(s_x2, 1)
                        dve.wait_ge(s_sq5, 2 * t + 2)
                        link(nc.vector.reciprocal(rstd[0:r, t:t + 1], ss[0:r, t:t + 1]))
                        if t == 0:
                            dve.wait_ge(s_rc, 16 * 6)
                        if t >= 2:
                            dve.wait_ge(s_h2o[t % 2], 16 * (t // 2))
                            dve.wait_ge(s_h2T, t - 1)
                        nc.vector.scalar_tensor_tensor(h2[0:r, t % 2, :], x2[0:r, t % 2, :], rstd[0:r, t:t + 1],
                                                       g2row[0:r, :], ALU.mult, ALU.mult).then_inc(s_h2, 1)
                    if t:
                        r = rows(t - 1)
                        dve.wait_ge(s_rt, t)
                        nc.vector.tensor_tensor(logits[0:r, t - 1, :], bank(6)[0:r, 0:36], brr[0:r, :],
                                                ALU.add).then_inc(s_lg, 1)

            @block.tensor
            def _(pe):
                for t in range(TILES + 1):
                    if t < TILES:
                        r = rows(t)
                        pe.wait_ge(s_mtl, t + 1)
                        if t >= 2:
                            pe.wait_ge(s_x2, 2 * (t - 1))
                        for half in range(2):
                            cols = slice(512 * half, 512 * half + 512)
                            if t == 0:
                                pe.wait_ge(s_wol, 2 * half + 2)
                            for k in range(KD):
                                for i, (x_, w_) in enumerate(((mth, woh), (mth, wol), (mtl, woh))):
                                    m = nc.tensor.matmul(bank(2 * (t % 2) + half)[0:r, :], x_[:, t % 2, k, 0:r],
                                                         w_[:, k, cols], start=(k == 0 and i == 0),
                                                         stop=(k == KD - 1 and i == 2))
                        m.then_inc(s_wop, 1)
                    if t:
                        r = rows(t - 1)
                        pe.wait_ge(s_h2, t)
                        if t >= 2:
                            pe.wait_ge(s_h2c, 2 * (t - 1))
                        for k in range(KD):
                            m = nc.tensor.transpose(bank(4 + k // 4)[:, (k % 4) * P:(k % 4) * P + r],
                                                    h2[0:r, (t - 1) % 2, k * P:(k + 1) * P], ident[0:r, 0:r])
                        m.then_inc(s_h2T, 1)
                        pe.wait_ge(s_h2c, 2 * t)
                        if t == 1:
                            pe.wait_ge(s_rc, 16 * 6)
                        if t >= 2:
                            pe.wait_ge(s_lg, t - 1)
                        for k in range(KD):
                            m = nc.tensor.matmul(bank(6)[0:r, 0:36], h2T[:, (t - 1) % 2, k, 0:r], wr[:, k, :],
                                                 start=(k == 0), stop=(k == KD - 1))
                        m.then_inc(s_rt, 1)

        r6 = Region(r1_at)
        cbef = r6("before", [P, P])
        cone = r6("ones", [P, P])
        ramp = r6("ramps", [P, 4 + NE + NBMAX + 1 + TILES])
        valid = r6("valid", [P, TILES])
        ctok = r6("token_ids", [P, TILES], I32)
        gmx = r6("group_max", [P, TILES])
        ge = r6("group_exp", [P, TILES, 4])
        oh4 = r6("group_onehot", [P, TILES, 4])
        pg = r6("group_prob", [P, TILES])
        em = r6("expert_logits", [P, TILES, NE])
        tmp = r6("weighted_match", [P, TILES, NE])
        oh1 = r6("first_onehot", [P, TILES, NE])
        oh2 = r6("second_onehot", [P, TILES, NE])
        v12 = r6("top_values", [P, 2, TILES])
        wmx = r6("match_max", [P, TILES])
        msk = r6("chosen", [P, TILES, NE])
        pre = r6("earlier_in_tile", [P, TILES, NE])
        tbs = r6("earlier_tiles", [P, TILES + 1, NE])
        cmp9 = r6("block_compare", [P, NE, TILES])
        nb32 = r6("expert_blocks", [P, NE])
        scn = r6("scan", [P, 2, NE])
        slot = r6("slot", [P, TILES, NE])
        dsf = r6("dest_float", [P, 2, TILES])
        cmpb = r6("owner_compare", [1, NBMAX + 1, NE])
        bef = r6("owner_float", [1, NBMAX + 1])
        R4, R32, RB, R128 = 0, 4, 4 + NE, 4 + NE + NBMAX + 1

        s_fc = sem_b("routing_consts_in")
        s_c6 = sem_b("vector_chain_routing")
        s_ge = sem_b("group_diff_ready")
        s_gx = sem_b("group_exp_ready")
        s_vd = sem_b("value_diff_ready")
        s_vx = sem_b("value_exp_ready")
        s_mk = sem_b("chosen_ready")
        s_cn = sem_b("counts_ready")
        s_ds = sem_b("dest_ready")
        s_st = sem_b("slots_scattered")

        with nc.Block() as block:
            @block.sync
            def _(sp):
                sp.dma_start(cbef[:], a["c_before"]).then_inc(s_fc, 16)
                sp.dma_start(cone[:], a["c_ones"]).then_inc(s_fc, 16)
                sp.dma_start(ramp[:], a["c_ramp"].partition_broadcast(P)).then_inc(s_fc, 16)
                sp.dma_start(valid[:], a["c_valid"]).then_inc(s_fc, 16)
                sp.dma_start(ctok[:], a["c_token"]).then_inc(s_fc, 16)

            @block.scalar
            def _(act):
                act.wait_ge(s_ge, 1)
                nc.scalar.activation(ge[:], ge[:], ACT.Exp).then_inc(s_gx, 1)
                act.wait_ge(s_vd, 1)
                nc.scalar.activation(v12[:, 1], v12[:, 1], ACT.Exp).then_inc(s_vx, 1)

            @block.vector
            def _(dve):
                link = chain_of(dve, s_c6)
                V = nc.vector
                dve.wait_ge(s_fc, 16 * 5)
                gl, el = logits[:, :, 0:4], logits[:, :, 4:36]
                B = [P, TILES, NE]

                def col(x, n=NE):
                    return x.unsqueeze(2).to_broadcast([P, TILES, n])

                def first_match(out_, val, mx, ramp0, n):
                    rp = ramp[:, ramp0:ramp0 + n].unsqueeze(1).to_broadcast([P, TILES, n])
                    w = tmp[:, :, 0:n]
                    link(V.tensor_tensor(w, val, col(mx, n), ALU.is_equal))
                    link(V.tensor_tensor(w, w, rp, ALU.mult))
                    link(V.tensor_reduce(wmx[:], w, X, ALU.max))
                    link(V.tensor_tensor(out_, w, col(wmx[:], n), ALU.is_equal))

                link(V.tensor_reduce(gmx[:], gl, X, ALU.max))
                V.tensor_tensor(ge[:], gl, col(gmx[:], 4), ALU.subtract).then_inc(s_ge, 1)
                first_match(oh4[:], gl, gmx[:], R4, 4)
                link(V.tensor_scalar(oh4[:], oh4[:], 1.0, -NEG, ALU.subtract, ALU.mult))
                link(V.tensor_tensor(em[:].rearrange("p t (g e) -> p t g e", g=4),
                                     el.rearrange("p t (g e) -> p t g e", g=4),
                                     oh4[:].unsqueeze(3).to_broadcast([P, TILES, 4, PER_GROUP]), ALU.add))
                link(V.tensor_reduce(v12[:, 0], em[:], X, ALU.max))
                first_match(oh1[:], em[:], v12[:, 0], R32, NE)
                link(V.scalar_tensor_tensor(em[:], oh1[:], NEG, em[:], ALU.mult, ALU.add))
                link(V.tensor_reduce(v12[:, 1], em[:], X, ALU.max))
                first_match(oh2[:], em[:], v12[:, 1], R32, NE)
                V.tensor_tensor(v12[:, 1], v12[:, 1], v12[:, 0], ALU.subtract).then_inc(s_vd, 1)
                link(V.tensor_tensor(msk[:], oh1[:], oh2[:], ALU.add))
                V.tensor_tensor(msk[:], msk[:], col(valid[:]), ALU.mult).then_inc(s_mk, 1)
                dve.wait_ge(s_gx, 1)
                link(V.tensor_reduce(pg[:], ge[:], X, ALU.add))
                link(V.reciprocal(pg[:], pg[:]))
                dve.wait_ge(s_vx, 1)
                link(V.tensor_scalar(wmx[:], v12[:, 1], 1.0, None, ALU.add))
                link(V.reciprocal(wmx[:], wmx[:]))
                link(V.tensor_tensor(gate2[:, :, 0], pg[:], wmx[:], ALU.mult))
                link(V.tensor_tensor(gate2[:, :, 1], gate2[:, :, 0], v12[:, 1], ALU.mult))
                dve.wait_ge(s_cn, 1)
                link(V.tensor_copy(pre[:].rearrange("p t e -> p (t e)"), bank(0)[:, 0:TILES * NE]))
                tot = bank(1)[:, 0:TILES * NE].rearrange("p (t e) -> p t e", t=TILES)
                link(V.memset(tbs[:, 0, :], 0.0))
                for t in range(TILES):
                    link(V.tensor_tensor(tbs[:, t + 1, :], tbs[:, t, :], tot[:, t, :], ALU.add))
                link(V.tensor_tensor(cmp9[:], tbs[:, TILES, :].unsqueeze(2).to_broadcast([P, NE, TILES]),
                                     ramp[:, R128:R128 + TILES].unsqueeze(1).to_broadcast([P, NE, TILES]), ALU.is_gt))
                link(V.tensor_reduce(nb32[:], cmp9[:], X, ALU.add))
                link(V.tensor_copy(scn[:, 0], nb32[:]))
                cur, step = 0, 1
                while step < NE:
                    link(V.tensor_copy(scn[:, 1 - cur, 0:step], scn[:, cur, 0:step]))
                    link(V.tensor_tensor(scn[:, 1 - cur, step:NE], scn[:, cur, step:NE], scn[:, cur, 0:NE - step],
                                         ALU.add))
                    cur, step = 1 - cur, 2 * step
                ends = scn[:, cur, :]
                first = scn[:, 1 - cur, :]
                link(V.tensor_tensor(first, ends, nb32[:], ALU.subtract))
                link(V.tensor_scalar(first, first, float(BLK), None, ALU.mult))
                link(V.tensor_tensor(slot[:], pre[:], tbs[:, 0:TILES, :], ALU.add))
                link(V.tensor_tensor(slot[:], slot[:], first.unsqueeze(1).to_broadcast(B), ALU.add))
                for k, oh in enumerate((oh1, oh2)):
                    link(V.tensor_tensor(tmp[:], oh[:], slot[:], ALU.mult))
                    link(V.tensor_reduce(dsf[:, k], tmp[:], X, ALU.add))
                V.tensor_copy(dest[:].rearrange("p t k -> p k t"), dsf[:]).then_inc(s_ds, 1)
                link(V.tensor_tensor(cmpb[:], ramp[0:1, RB:RB + NBMAX + 1].unsqueeze(2)
                                     .to_broadcast([1, NBMAX + 1, NE]),
                                     ends[0:1].unsqueeze(1).to_broadcast([1, NBMAX + 1, NE]), ALU.is_ge))
                link(V.tensor_reduce(bef[:], cmpb[:], X, ALU.add))
                link(V.tensor_scalar(bef[:], bef[:], float(NE - 1), None, ALU.min))
                link(V.tensor_copy(blk_e[:], bef[:]))
                link(V.tensor_copy(nblk[:, 0:1], ends[0:1, NE - 1:NE]))
                link(V.tensor_scalar(nblk[:, 1:2], ends[0:1, NE - 1:NE], -2.0, None, ALU.add))

            @block.tensor
            def _(pe):
                pe.wait_ge(s_mk, 1)
                pe.wait_ge(s_fc, 16 * 5)
                mv_ = msk[:].rearrange("p t e -> p (t e)")
                nc.tensor.matmul(bank(0)[:, 0:TILES * NE], cbef[:], mv_, start=True, stop=True)
                nc.tensor.matmul(bank(1)[:, 0:TILES * NE], cone[:], mv_, start=True, stop=True).then_inc(s_cn, 1)

            @block.gpsimd
            def _(pool):
                pool.wait_ge(s_ds, 1)
                pool.wait_ge(s_fc, 16 * 5)
                for t in range(TILES):
                    r = rows(t)
                    for k in range(2):
                        pool.indirect_dma_start(tab_d[:, :], bass.IndirectOffsetOnAxis(ap=dest[0:r, t, k:k + 1], axis=0),
                                                ctok[0:r, t:t + 1], None).then_inc(s_st, 16)
                pool.wait_ge(s_st, 16 * 2 * TILES)

        r7 = Region(hh_at)
        UN = 6
        wraw = r7("expert_raw", [P, UN, 2048])
        weh = r7("expert_hi", [P, UN, 2048], F32R)
        wel = r7("expert_lo", [P, UN, 2048], F32R)
        idx = r7("block_tokens", [P, 1], I32)
        xg = r7("block_rows", [P, D])
        xTh = r7("block_T_hi", [P, KD, P], F32R)
        xTl = r7("block_T_lo", [P, KD, P], F32R)
        sil = r7("silu_gate", [P, DE])
        hid = r7("hidden", [P, DE])
        hTh = r7("hidden_T_hi", [P, 4, P], F32R)
        hTl = r7("hidden_T_lo", [P, 4, P], F32R)
        yb = r7("block_out", [P, D])

        s_ui = [sem_b(f"expert_half_in{u}") for u in range(UN)]
        s_uh = [sem_b(f"{n}_hi_ready") for n in ("gate", "up", "down")]
        s_ul = [sem_b(f"{n}_lo_ready") for n in ("gate", "up", "down")]
        s_um = [sem_b(f"{n}_multiplied") for n in ("gate", "up", "down")]
        s_ix = sem_b("block_tokens_in")
        s_xg = sem_b("block_rows_in")
        s_xT = sem_b("block_transposed")
        s_xh = sem_b("block_T_hi_ready")
        s_xl = sem_b("block_T_lo_ready")
        s_si = sem_b("silu_ready")
        s_hd = sem_b("hidden_ready")
        s_hT7 = sem_b("hidden_transposed")
        s_th = sem_b("hidden_T_hi_ready")
        s_tl = sem_b("hidden_T_lo_ready")
        s_y = sem_b("block_out_ready")
        s_yo = sem_b("block_out_stored")

        def over_blocks(eng, body, n):
            body(0)
            body(1)
            with eng.Fori(2, NBMAX) as b:
                with eng.If(b < n):
                    body(b)

        def later(b, d):
            return not isinstance(b, int) or b >= d

        with nc.Block() as block:
            @block.sync
            def _(sp):
                n = sp.value_load(nblk[0:1, 0:1], min_val=2 * TOK // BLK, max_val=NBMAX)
                gate_v = a["w_gate"][0].rearrange("e (u k p) n -> e u p k n", u=2, p=P)
                up_v = a["w_up"][0].rearrange("e (u k p) n -> e u p k n", u=2, p=P)
                down_v = a["w_down"][0].rearrange("e (u k p) n -> e u p k n", u=2, p=P)

                def body(b):
                    e = sp.value_load(blk_e[0:1, bass.ds(b, 1)], min_val=0, max_val=NE - 1)
                    for u in range(UN):
                        if later(b, 1):
                            sp.wait_ge(s_ul[u // 2], 2 * b - 1 + u % 2)
                        src = (gate_v, up_v, down_v)[u // 2]
                        sp.dma_start(wraw[:, u].rearrange("p (k n) -> p k n", k=(2 if u >= 4 else 4)),
                                     src[bass.ds(e, 1), u % 2].rearrange("o p k n -> (o p) k n")) \
                            .then_inc(s_ui[u], 16)
                over_blocks(sp, body, n)

            @block.gpsimd
            def _(pool):
                n = pool.value_load(nblk[0:1, 0:1], min_val=2 * TOK // BLK, max_val=NBMAX)
                landed = pool.alloc_register("tokens_landed")
                tab_v = tab_d.rearrange("(b p) o -> b p o", p=P)

                def body(b):
                    if later(b, 1):
                        pool.wait_ge(s_xg, 16 * b)
                    pool.dma_start(idx[:], tab_v[bass.ds(b, 1)].rearrange("b p o -> (b p) o")).then_inc(s_ix, 16)
                    pool.reg_mov(landed, 16 * b + 16)
                    pool.wait_ge(s_ix, 16)
                    pool.wait_ge(s_ix, landed)
                    if later(b, 1):
                        pool.wait_ge(s_xT, b)
                    pool.indirect_dma_start(xg[:], None, h2_d[:, :],
                                            bass.IndirectOffsetOnAxis(ap=idx[:, 0:1], axis=0)).then_inc(s_xg, 16)
                over_blocks(pool, body, n)

            @block.scalar
            def _(act):
                n = act.value_load(nblk[0:1, 0:1], min_val=2 * TOK // BLK, max_val=NBMAX)
                last2 = act.value_load(nblk[0:1, 1:2], min_val=2 * TOK // BLK - 2, max_val=NBMAX - 2)

                def split_hi(m, b):
                    for u in (2 * m, 2 * m + 1):
                        act.wait_ge(s_ui[u], 16 * b + 16)
                        if later(b, 1):
                            act.wait_ge(s_um[m], 2 * b - 1 + u % 2)
                        nc.scalar.copy(weh[:, u], wraw[:, u]).then_inc(s_uh[m], 1)

                def silu(b):
                    act.wait_ge(s_um[0], 2 * b + 2)
                    if later(b, 1):
                        act.wait_ge(s_hd, b)
                    nc.scalar.activation(sil[:], bank(0), ACT.Silu).then_inc(s_si, 1)

                def rows_hi(b):
                    act.wait_ge(s_xT, b + 1)
                    for half in range(2):
                        nc.scalar.copy(xTh[:, 4 * half:4 * half + 4].rearrange("p k q -> p (k q)"),
                                       bank(2 + half)).then_inc(s_xh, 1)

                def hidden_hi(b):
                    act.wait_ge(s_hT7, b + 1)
                    nc.scalar.copy(hTh[:].rearrange("p k q -> p (k q)"), bank(4)).then_inc(s_th, 1)

                def out_rows(b):
                    act.wait_ge(s_um[2], 2 * b + 2)
                    if later(b, 1):
                        act.wait_ge(s_yo, 16 * b)
                    for half in range(2):
                        nc.scalar.copy(yb[:, 512 * half:512 * half + 512], bank(5 + half)).then_inc(s_y, 1)
                    act.wait_ge(s_y, 2 * b + 2)
                    act.dma_start(ys_v[bass.ds(b, 1)].rearrange("b p c -> (b p) c"), yb[:]).then_inc(s_yo, 16)

                ys_v = ys_d.rearrange("(b p) c -> b p c", p=P)

                def body(b):
                    split_hi(0, b)
                    if later(b, 1):
                        silu(b - 1)
                    rows_hi(b)
                    split_hi(1, b)
                    if later(b, 2):
                        out_rows(b - 2)
                    if later(b, 1):
                        hidden_hi(b - 1)
                        split_hi(2, b - 1)
                over_blocks(act, body, n)
                silu(last2 + 1)
                out_rows(last2)
                hidden_hi(last2 + 1)
                split_hi(2, last2 + 1)
                out_rows(last2 + 1)
                stored = act.alloc_register("rows_stored")
                act.reg_mov(stored, 16 * last2 + 32)
                act.wait_ge(s_yo, 16)
                act.wait_ge(s_yo, stored)

            @block.vector
            def _(dve):
                n = dve.value_load(nblk[0:1, 0:1], min_val=2 * TOK // BLK, max_val=NBMAX)
                last2 = dve.value_load(nblk[0:1, 1:2], min_val=2 * TOK // BLK - 2, max_val=NBMAX - 2)

                def split_lo(m, b):
                    for u in (2 * m, 2 * m + 1):
                        dve.wait_ge(s_uh[m], 2 * b + 1 + u % 2)
                        nc.vector.tensor_tensor(wel[:, u], wraw[:, u], weh[:, u].bitcast(F32),
                                                ALU.subtract).then_inc(s_ul[m], 1)

                def hidden(b):
                    dve.wait_ge(s_si, b + 1)
                    dve.wait_ge(s_um[1], 2 * b + 2)
                    if later(b, 1):
                        dve.wait_ge(s_hT7, b)
                    nc.vector.tensor_tensor(hid[:], bank(1), sil[:], ALU.mult).then_inc(s_hd, 1)

                def rows_lo(b):
                    for half in range(2):
                        dve.wait_ge(s_xh, 2 * b + half + 1)
                        nc.vector.tensor_tensor(
                            xTl[:, 4 * half:4 * half + 4].rearrange("p k q -> p (k q)"), bank(2 + half),
                            xTh[:, 4 * half:4 * half + 4].rearrange("p k q -> p (k q)").bitcast(F32),
                            ALU.subtract).then_inc(s_xl, 1)

                def hidden_lo(b):
                    dve.wait_ge(s_th, b + 1)
                    nc.vector.tensor_tensor(hTl[:].rearrange("p k q -> p (k q)"), bank(4),
                                            hTh[:].rearrange("p k q -> p (k q)").bitcast(F32),
                                            ALU.subtract).then_inc(s_tl, 1)

                def body(b):
                    split_lo(0, b)
                    if later(b, 1):
                        hidden(b - 1)
                    rows_lo(b)
                    split_lo(1, b)
                    if later(b, 1):
                        hidden_lo(b - 1)
                        split_lo(2, b - 1)
                over_blocks(dve, body, n)
                hidden(last2 + 1)
                hidden_lo(last2 + 1)
                split_lo(2, last2 + 1)

            @block.tensor
            def _(pe):
                n = pe.value_load(nblk[0:1, 0:1], min_val=2 * TOK // BLK, max_val=NBMAX)
                last2 = pe.value_load(nblk[0:1, 1:2], min_val=2 * TOK // BLK - 2, max_val=NBMAX - 2)

                def rows_T(b):
                    pe.wait_ge(s_xg, 16 * b + 16)
                    if later(b, 1):
                        pe.wait_ge(s_xl, 2 * b)
                    for k in range(KD):
                        m = nc.tensor.transpose(bank(2 + k // 4)[:, (k % 4) * P:(k % 4 + 1) * P],
                                                xg[:, k * P:(k + 1) * P], ident[:])
                    m.then_inc(s_xT, 1)

                def gate_up(m_, b):
                    if later(b, 1):
                        pe.wait_ge((s_si, s_hd)[m_], b)
                    for u in range(2):
                        pe.wait_ge(s_ul[m_], 2 * b + 1 + u)
                        if m_ == 0:
                            pe.wait_ge(s_xl, 2 * b + 1 + u)
                        for k in range(4):
                            cols = slice(512 * k, 512 * k + 512)
                            h_, l_ = weh[:, 2 * m_ + u, cols], wel[:, 2 * m_ + u, cols]
                            xh, xl = xTh[:, 4 * u + k], xTl[:, 4 * u + k]
                            for i, (x_, w_) in enumerate(((xh, h_), (xh, l_), (xl, h_))):
                                m = nc.tensor.matmul(bank(m_), x_, w_, start=(u == 0 and k == 0 and i == 0),
                                                     stop=(u == 1 and k == 3 and i == 2))
                        m.then_inc(s_um[m_], 1)

                def hidden_T(b):
                    pe.wait_ge(s_hd, b + 1)
                    if later(b, 1):
                        pe.wait_ge(s_tl, b)
                    for k in range(4):
                        m = nc.tensor.transpose(bank(4)[:, k * P:(k + 1) * P], hid[:, k * P:(k + 1) * P], ident[:])
                    m.then_inc(s_hT7, 1)

                def down(b):
                    pe.wait_ge(s_tl, b + 1)
                    if later(b, 1):
                        pe.wait_ge(s_y, 2 * b)
                    for u in range(2):
                        pe.wait_ge(s_ul[2], 2 * b + 1 + u)
                        for k in range(2):
                            for half in range(2):
                                cols = slice(1024 * k + 512 * half, 1024 * k + 512 * half + 512)
                                h_, l_ = weh[:, 4 + u, cols], wel[:, 4 + u, cols]
                                xh, xl = hTh[:, 2 * u + k], hTl[:, 2 * u + k]
                                for i, (x_, w_) in enumerate(((xh, h_), (xh, l_), (xl, h_))):
                                    m = nc.tensor.matmul(bank(5 + half), x_, w_,
                                                         start=(u == 0 and k == 0 and i == 0),
                                                         stop=(u == 1 and k == 1 and i == 2))
                        m.then_inc(s_um[2], 1)

                def body(b):
                    rows_T(b)
                    if later(b, 2):
                        down(b - 2)
                    if later(b, 1):
                        hidden_T(b - 1)
                    gate_up(0, b)
                    gate_up(1, b)
                over_blocks(pe, body, n)
                down(last2)
                hidden_T(last2 + 1)
                down(last2 + 1)

        r8 = Region(hh_at)
        y1 = r8("first_rows", [P, 2, D])
        y2 = r8("second_rows", [P, 2, D])
        xf = r8("x_rows_final", [P, 2, D])
        yo = r8("y_out", [P, 2, D])
        jk8 = r8("square_junk3", [P, D])
        gfr = r8("final_norm_row", [P, D])

        s_gf = sem_b("final_gain_in")
        s_yi = [sem_b(f"expert_rows_in{i}") for i in range(2)]
        s_xf = [sem_b(f"x_final_in{i}") for i in range(2)]
        s_f1 = sem_b("first_added")
        s_f2 = sem_b("second_added")
        s_sq8 = sem_b("squares3_summed")
        s_r8 = sem_b("scale3_ready")
        s_fo = sem_b("y_ready")
        s_out = [sem_b(f"y_stored{i}") for i in range(2)]
        y_rows = [out[0][0, t * P:(t + 1) * P] for t in range(NT)] + [out[1].rearrange("b s d -> (b s) d")]

        with nc.Block() as block:
            @block.sync
            def _(sp):
                sp.dma_start(gfr[:], a["final_norm_g"].partition_broadcast(P)).then_inc(s_gf, 16)
                for t in range(TILES + 1):
                    if t < TILES:
                        r = rows(t)
                        if t >= 2:
                            sp.wait_ge(s_f1, t - 1)
                        sp.dma_start(xf[0:r, t % 2, :], x2_d[t * P:t * P + r]).then_inc(s_xf[t % 2], 16)
                    if t:
                        r = rows(t - 1)
                        sp.wait_ge(s_fo, t)
                        sp.dma_start(y_rows[t - 1], yo[0:r, (t - 1) % 2, :]).then_inc(s_out[(t - 1) % 2], 16)
                for i in range(2):
                    sp.wait_ge(s_out[i], 16 * len(range(i, TILES, 2)))

            @block.gpsimd
            def _(pool):
                for t in range(TILES):
                    r = rows(t)
                    for k, y in enumerate((y1, y2)):
                        if t >= 2:
                            pool.wait_ge(s_f2 if k else s_fo, t - 1)
                        pool.indirect_dma_start(y[0:r, t % 2, :], None, ys_d[:, :],
                                                bass.IndirectOffsetOnAxis(ap=dest[0:r, t, k:k + 1], axis=0)) \
                            .then_inc(s_yi[t % 2], 16)

            @block.scalar
            def _(act):
                for t in range(TILES):
                    r = rows(t)
                    act.wait_ge(s_f2, t + 1)
                    nc.scalar.activation(jk8[0:r, :], y1[0:r, t % 2, :], ACT.Square,
                                         accum_out=ss[0:r, t:t + 1]).then_inc(s_sq8, 1)
                    act.wait_ge(s_sq8, 2 * t + 1)
                    nc.scalar.activation(ss[0:r, t:t + 1], ss[0:r, t:t + 1], ACT.Sqrt, scale=1.0 / D,
                                         bias=eps[0:r, :]).then_inc(s_sq8, 1)

            @block.vector
            def _(dve):
                dve.wait_ge(s_gf, 16)
                for t in range(TILES + 1):
                    if t < TILES:
                        r = rows(t)
                        dve.wait_ge(s_yi[t % 2], 32 * (t // 2 + 1))
                        dve.wait_ge(s_xf[t % 2], 16 * (t // 2 + 1))
                        nc.vector.scalar_tensor_tensor(y1[0:r, t % 2, :], y1[0:r, t % 2, :], gate2[0:r, t, 0:1],
                                                       xf[0:r, t % 2, :], ALU.mult, ALU.add).then_inc(s_f1, 1)
                        dve.wait_ge(s_f1, t + 1)
                        nc.vector.scalar_tensor_tensor(y1[0:r, t % 2, :], y2[0:r, t % 2, :], gate2[0:r, t, 1:2],
                                                       y1[0:r, t % 2, :], ALU.mult, ALU.add).then_inc(s_f2, 1)
                    if t:
                        r = rows(t - 1)
                        p = (t - 1) % 2
                        dve.wait_ge(s_sq8, 2 * t)
                        nc.vector.reciprocal(rstd[0:r, t - 1:t], ss[0:r, t - 1:t]).then_inc(s_r8, 1)
                        dve.wait_ge(s_r8, t)
                        if t >= 3:
                            dve.wait_ge(s_out[p], 16 * ((t - 1) // 2))
                        nc.vector.scalar_tensor_tensor(yo[0:r, p, :], y1[0:r, p, :], rstd[0:r, t - 1:t],
                                                       gfr[0:r, :], ALU.mult, ALU.mult).then_inc(s_fo, 1)


_INS = ["x_prompt", "x_sample", "cache_kv_g0", "cache_kv_g1", "cache_kv_g2", "norm1_g", "w_in", "b_in",
        "a_ln_g", "a_ln_b", "w_spatial", "b_spatial", "w_a_proj", "w_b_proj", "w_o", "norm2_g",
        "w_group_router", "b_group_router", "w_expert_router", "b_expert_router", "w_gate", "w_up",
        "w_down", "final_norm_g"]
_OUTS = [(1, SEQ, D), (NS, 1, D)] + [(1, 1, KEEP[g], 2, H, DH) for g in range(NG)] + \
        [(1, NS, 1, 2, H, DH)] * NG + [(1, NS, 1, AW)]


def _constants():
    f = np.float32
    c = {"c_ident": np.eye(P, dtype=f)}
    q, k = np.arange(P)[:, None], np.arange(P)[None, :]
    band = np.concatenate([k >= q, k <= q], axis=1)
    c["c_mask"] = np.where(band, f(0), f(NEG)).astype(f)
    c["c_mask2"] = np.where(((q - k) % 2 == 0) & (k <= q), f(0), f(NEG)).astype(f)
    inv = (f(1.0) / (f(10000.0) ** (np.arange(DH // 2, dtype=f) * f(2.0 / DH)))).astype(f)
    table = np.zeros((NG, TILES, P, 2 * DH), f)
    tokens = np.arange(SEQ)
    for g, d in enumerate((1, 4, NT)):
        order = tokens.reshape(SEQ // d, d).T.reshape(-1)
        pos = np.concatenate([order, np.full(P, PAST)]).astype(f)
        ang = (pos[:, None] * inv[None]).astype(f).astype(np.float64)
        cos, sin = np.cos(ang).astype(f), np.sin(ang).astype(f)
        table[g] = np.concatenate([cos, cos, -sin, sin], axis=1).reshape(TILES, P, 2 * DH)
    c["c_rope"] = table
    c["c_before"] = (q < k).astype(f)
    c["c_ones"] = np.ones((P, P), f)
    c["c_causal_T"] = (q <= k).astype(f)
    c["c_ramp"] = np.concatenate([NEG_GROUPS - np.arange(NEG_GROUPS), NE - np.arange(NE),
                                  np.arange(NBMAX + 1), BLK * np.arange(TILES)]).astype(f)
    c["c_token"] = (np.arange(TILES)[None] * P + np.arange(P)[:, None]).astype(np.int32)
    c["c_valid"] = (c["c_token"] < TOK).astype(f)
    c["c_zero"] = np.zeros((P, NBMAX + 1), np.int32)
    return c


def kernel(**inputs):
    import concourse.bacc as _bacc
    from concourse.bass_utils import run_bass_kernel_spmd as _run

    nc = _bacc.Bacc("TRN2", target_bir_lowering=False, num_devices=1)
    arrays, a = {}, {}
    for name, v in [(n, np.ascontiguousarray(inputs[n])) for n in _INS] + list(_constants().items()):
        arrays[f"in_{name}_dram"] = v
        a[name] = nc.dram_tensor(f"in_{name}_dram", v.shape, mybir.dt.from_np(v.dtype), kind="ExternalInput").ap()
    outs = [nc.dram_tensor(f"out_{i}_dram", shape, F32, kind="ExternalOutput").ap()
            for i, shape in enumerate(_OUTS)]
    build(nc, a, outs)
    r = _run(nc, [arrays], core_ids=[0])
    return tuple(r.results[0][f"out_{i}_dram"] for i in range(len(_OUTS)))
```

```python
from contextlib import ExitStack, contextmanager

import numpy as np

import concourse.bass as bass
from concourse import mybir
from concourse.alu_op_type import AluOpType as ALU

ACT = mybir.ActivationFunctionType
F32 = mybir.dt.float32
F32R = mybir.dt.float32r
I32 = mybir.dt.int32
X = mybir.AxisListType.X

P = 128
D = 1024
KD = D // P
SEQ = 1024
NS = 8
TOK = SEQ + NS
NT = SEQ // P
TILES = NT + 1
PAST = 1024
AW = 512
NG = 3
DIL = (1, 4, 16)
WIN = (128, 512, 2048)
KEEP = tuple(min(w, SEQ) for w in WIN)
CACHED = (128, 128, 64)
H = 4
DH = 64
HW = H * DH
SCALE = DH ** -0.5
EPS = 1e-6
NEG = -1.0e30
NE = 32
NEG_GROUPS = 4
PER_GROUP = 8
DE = 512
BLK = 128
NBMAX = NE + 2 * TOK // BLK
NONE = 1 << 12
assert NONE > 2 * TOK
CW = 256
AR = HW + 2 * H

COL_U, COL_VA, COL_Q, COL_K, COL_V = 0, AW, 2 * AW, 2 * AW + NG * HW, 2 * AW + 2 * NG * HW
COL_GA = 2 * AW + 3 * NG * HW
COL_GB = COL_GA + D
ZW = COL_GB + D

CHUNKS = []
for _g in range(NG):
    CHUNKS += [("q", _g, COL_Q + _g * HW), ("k", _g, COL_K + _g * HW), ("v", _g, COL_V + _g * HW)]
    if _g < 2:
        CHUNKS.append(("va", _g, COL_VA + _g * CW))
CHUNKS += [("u", i, COL_U + i * CW) for i in range(2)]
NC1 = len(CHUNKS)
for _i in range(4):
    CHUNKS += [("ga", _i, COL_GA + _i * CW), ("gb", _i, COL_GB + _i * CW)]
NCH = len(CHUNKS)
TC = 344
NTC = TOK // TC

STEPS = []
for _c in range(NC1):
    if CHUNKS[_c][0] == "u":
        STEPS += [(_c, n, j) for n in range(2) for j in range(NTC)]
    else:
        STEPS += [(_c, t, 0) for t in range(TILES)]
NSTEP = len(STEPS)
FIRST_STEP = [min(i for i, s in enumerate(STEPS) if s[0] == c) for c in range(NC1)]
FIRST_STEP.append(NSTEP)
ATT = [(g, j) for g in range(NG) for j in range(NT)]
ATT_AT = [FIRST_STEP[4 * g + 3] + 1 + j for g, j in ATT]
AT_STEP = {s: a for a, s in enumerate(ATT_AT)}


def rows(t):
    return P if t < NT else NS


def has_prev(g, j):
    return (g == 0 and j > 0) or (g == 1 and j % 2 == 1)


def perm_cols(ap, g, t):
    if t == NT:
        return ap[:, SEQ:TOK]
    if g == 0:
        return ap[:, t * P:(t + 1) * P]
    if g == 1:
        return ap[:, 0:SEQ].rearrange("p (i r) -> p r i", r=4)[:, t // 2, (t % 2) * P:(t % 2 + 1) * P]
    return ap[:, 0:SEQ].rearrange("p (i r) -> p r i", r=NT)[:, t, :]


def perm_rows(ap, g, t, keep=SEQ):
    if g == 0:
        return ap[t * P - (SEQ - keep):(t + 1) * P - (SEQ - keep)]
    if g == 1:
        first = (t % 2) * P - (SEQ - keep) // 4
        return ap.rearrange("(i r) c -> r i c", r=4)[t // 2, first:first + P]
    return ap.rearrange("(i r) c -> r i c", r=NT)[t]


def keeps(g, t):
    return t < NT and (g == 2 or (g == 1 and t % 2 == 1) or (g == 0 and t == NT - 1))


def build(nc, a, out):
    ctx = ExitStack()
    with ctx:
        front = []

        def sem(name):
            front.append(nc.alloc_semaphore(name))
            return front[-1]

        def sem_b(name):
            return ctx.enter_context(nc.semaphore(name))

        def scratch(name, shape, dt=F32):
            return nc.dram_tensor(name, shape, dt, kind="Internal").ap()

        att_d = scratch("att_records", (NG, TOK, AR))
        new_d = scratch("sample_qkv", (NG * 3, NS, HW))
        stat_d = scratch("sample_stats", (NG, 2, NS * H))
        mt_d = scratch("merged_T", (D, TOK))
        gl_d = scratch("first_gate_logits", (2 * 2, P, NTC, TC))
        x2_d = scratch("x_after_mix", (TOK, D))
        h2_d = scratch("moe_input", (TOK, D))
        ys_d = scratch("expert_rows", (2 * TOK, D))

        base = (nc.sbuf_base + 63) // 64 * 64
        top = nc.sbuf_usable_end

        class Region:
            def __init__(self, at, end=top):
                self.at, self.end = at, end

            def __call__(self, name, shape, dt=F32):
                size = int(np.prod(shape[1:])) * 4
                t = nc.alloc_sbuf_tensor_at(name, shape, dt, offset=self.at)
                self.at += (size + 31) // 32 * 32
                assert self.at <= self.end, (name, self.at, self.end)
                return t

        keep = Region(base)
        ident = keep("ident", [P, P])
        logits = keep("logits", [P, TILES, 36])
        gate2 = keep("gate2", [P, TILES, 2])
        blk = keep("block_table", [1, 2, NBMAX], I32)
        nblk = keep("n_blocks", [1, 2], I32)
        bcol = keep("bias_columns", [P, ZW // P])
        eps = keep("epsilon", [P, 1])
        mv = keep("va_moments", [P, TILES, 2])
        ss = keep("square_sums", [P, TILES])
        rstd = keep("rstd", [P, TILES])
        hh_at = keep.at
        r0 = Region(hh_at)
        hh = r0("h_T_hi", [P, KD, TOK], F32R)
        hl = r0("h_T_lo", [P, KD, TOK], F32R)
        raw_at = r0.at
        raw = r0("w_raw", [P, 2, KD, CW])
        wh = r0("w_hi", [P, 2, KD, CW], F32R)
        wl = r0("w_lo", [P, 2, KD, CW], F32R)
        r1_at = r0.at

        psum = ctx.enter_context(nc.psum_tensor("psum", [P, 8, 512], F32))

        def bank(i):
            return psum[:, i, :]

        def chain_of(eng, s):
            n = [0]

            def link(ins):
                n[0] += 1
                ins.then_inc(s, 1)
                eng.wait_ge(s, n[0])
            return link

        w_in_v = a["w_in"][0].rearrange("(k p) n -> p k n", p=P)
        wa_v = a["w_a_proj"][0].rearrange("(k p) n -> p k n", p=P)
        wb_v = a["w_b_proj"][0].rearrange("(k p) n -> p k n", p=P)
        x_rows = [a["x_prompt"][0, t * P:(t + 1) * P] for t in range(NT)] + \
                 [a["x_sample"].rearrange("b s d -> (b s) d")]
        kv_p = [out[2 + g].rearrange("l b s two h e -> (l b s) two (h e)") for g in range(NG)]
        kv_s = [out[5 + g].rearrange("l b s two h e -> (l b s) two (h e)") for g in range(NG)]
        v_chunk = out[8].rearrange("l b s c -> (l b s) c")

        r1 = Region(r1_at)
        va = r1("va", [P, TILES, AW])
        u_at = r1.at
        uT = r1("u_T", [P, 4, TOK])
        r1b_at = r1.at
        qT = r1("q_T", [P, 2, SEQ])
        kT = r1("k_T", [P, 2, SEQ])
        vg = r1("v_group", [P, NT, HW])
        cs = r1("cos_sin", [P, TILES, 2 * DH])
        brow = r1("bias_row", [P, 2, CW])
        prob = r1("prob", [P, H, 2 * P])
        probT = r1("prob_T", [P, 2 * H, P])
        rec = r1("record", [P, 4, AR])
        mask = r1("mask_band", [P, 2 * P])
        mask2 = r1("mask_residues", [P, P])
        lnst = r1("ln_stats", [P, 16])
        zr = r1("z_rows", [P, 2, HW])
        rot = r1("rotated", [P, 3, HW])
        ropet = r1("rope_term", [P, 2, HW])
        rx = Region(u_at, r1b_at)
        xin = rx("x_in", [P, 3, D])
        g1row = rx("norm1_row", [P, D])
        rx = Region(r1_at, u_at)
        junk = rx("square_junk", [P, D])
        brows = rx("bias_rows", [ZW // P, P])

        s_const = sem("const_in")
        s_mask = sem("masks_in")
        s_x = [sem(f"x_in{i}") for i in range(3)]
        s_bT = sem("bias_transposed")
        s_bcol = sem("bias_columns_ready")
        s_eps = sem("epsilon_set")
        s_sq = sem("squares_summed")
        s_hn = sem("h_normed")
        s_hT = sem("h_transposed")
        s_hh = sem("h_hi_ready")
        s_hl = sem("h_lo_ready")
        s_w = [sem(f"w_chunk_in{i}") for i in range(2)]
        s_b = [sem(f"bias_chunk_in{i}") for i in range(2)]
        s_cs = sem("cos_sin_in")
        s_wh = sem("w_hi_ready")
        s_wl = sem("w_lo_ready")
        s_pj = sem("projected")
        s_z = sem("z_rows_ready")
        s_fm = sem("feature_rows_ready")
        s_rope = sem("rotated_ready")
        s_rT = sem("rotated_transposed")
        s_qk = sem("qk_T_ready")
        s_ro = [sem(f"rotated_stored{i}") for i in range(3)]
        s_vo = sem("v_group_stored")
        s_gelu = sem("va_gelu_done")
        s_ln = sem("va_moments_ready")
        s_sc = sem("scores_ready")
        s_sb = sem("scores_masked")
        s_nm = sem("row_max_ready")
        s_ex = sem("prob_ready")
        s_pT = sem("prob_transposed")
        s_pTa = sem("prob_T_half0")
        s_pTb = sem("prob_T_half1")
        s_pv = sem("values_weighted")
        s_rec = sem("record_ready")
        s_recd = [sem(f"record_stored{i}") for i in range(4)]
        s_dve = sem("vector_chain")
        s_pool = sem("pool_chain")

        RING = [i for i, (c, t, _) in enumerate(STEPS)
                if CHUNKS[c][0] in "qk" or (CHUNKS[c][0] == "v" and t == NT)]
        RPOS = {s: n for n, s in enumerate(RING)}

        def stores(i):
            c, t, _ = STEPS[i]
            kind, g, _ = CHUNKS[c]
            if t == NT:
                return 1 if kind == "q" else 2
            return 1 if kind == "k" and keeps(g, t) else 0

        def ring_stored(n):
            return sum(stores(RING[m]) for m in range(n % 3, n + 1, 3))

        def v_stored(g):
            return sum(keeps(gg, t) for gg in range(g + 1) for t in range(NT))

        TRANSPOSED = [i for i in RING if STEPS[i][1] < NT and CHUNKS[STEPS[i][0]][0] in "qk"]
        TPOS = {s: n for n, s in enumerate(TRANSPOSED)}
        ROTATED = [i for i in RING if CHUNKS[STEPS[i][0]][0] in "qk"]
        ROTPOS = {s: n for n, s in enumerate(ROTATED)}
        EVICT_DVE = [i for i, s in enumerate(STEPS) if CHUNKS[s[0]][0] != "u"]
        DPOS = {s: n for n, s in enumerate(EVICT_DVE)}

        def wait_evicted(eng, i):
            if i in DPOS:
                eng.wait_ge(s_z, DPOS[i] + 1)
            else:
                eng.wait_ge(s_fm, i - len(EVICT_DVE) + 1)

        def with_prev(n):
            return sum(has_prev(*ATT[m]) for m in range(n))

        def rec_stored(n):
            return n // 4 + 1

        with nc.Block() as block:
            @block.sync
            def _(sp):
                def load_x(t):
                    if t >= 3:
                        sp.wait_ge(s_hT, t - 2)
                    sp.dma_start(xin[0:rows(t), t % 3, :], x_rows[t]).then_inc(s_x[t % 3], 16)

                def load_chunk(c):
                    kind, _, col = CHUNKS[c]
                    if c >= 2:
                        sp.wait_ge(s_wl, c - 1)
                    sp.dma_start(raw[:, c % 2], w_in_v[:, :, col:col + CW]).then_inc(s_w[c % 2], 16)
                    if kind != "u":
                        if c >= 2:
                            sp.wait_ge(s_z, DPOS[FIRST_STEP[c - 1] - 1] + 1)
                        sp.dma_start(brow[:, c % 2, :], a["b_in"][0, col:col + CW].partition_broadcast(P)) \
                          .then_inc(s_b[c % 2], 16)

                sp.dma_start(ident[:], a["c_ident"]).then_inc(s_const, 16)
                sp.dma_start(g1row[:], a["norm1_g"][0].partition_broadcast(P)).then_inc(s_const, 16)
                for t in range(3):
                    load_x(t)
                sp.dma_start(brows[:], a["b_in"][0].rearrange("(j p) -> j p", p=P)).then_inc(s_const, 16)
                sp.dma_start(raw[:, 0], w_in_v[:, :, CHUNKS[0][2]:CHUNKS[0][2] + CW]).then_inc(s_w[0], 16)
                sp.dma_start(raw[:, 1], w_in_v[:, :, CHUNKS[1][2]:CHUNKS[1][2] + CW]).then_inc(s_w[1], 16)
                for c in range(2):
                    sp.dma_start(brow[:, c], a["b_in"][0, CHUNKS[c][2]:CHUNKS[c][2] + CW].partition_broadcast(P)) \
                      .then_inc(s_b[c], 16)
                sp.dma_start(mask[:], a["c_mask"]).then_inc(s_mask, 16)
                sp.dma_start(mask2[:], a["c_mask2"]).then_inc(s_mask, 16)

                def store_rows(i):
                    c, t, _ = STEPS[i]
                    kind, g, _ = CHUNKS[c]
                    if kind in "qk":
                        if stores(i):
                            sp.wait_ge(s_rope, ROTPOS[i] + 1)
                    elif t == NT:
                        sp.wait_ge(s_z, DPOS[i] + 1)
                    if i in RPOS:
                        s = RPOS[i] % 3
                        which = "qkv".index(kind)
                        if t == NT:
                            sp.dma_start(new_d[3 * g + which], rot[0:NS, s, :]).then_inc(s_ro[s], 16)
                            if kind != "q":
                                sp.dma_start(kv_s[g][:, which - 1], rot[0:NS, s, :]).then_inc(s_ro[s], 16)
                        elif kind == "k" and keeps(g, t):
                            sp.dma_start(perm_rows(kv_p[g][:, 0], g, t, KEEP[g]), rot[:, s, :]) \
                              .then_inc(s_ro[s], 16)
                    elif kind == "v" and keeps(g, t):
                        sp.wait_ge(s_z, DPOS[i] + 1)
                        sp.dma_start(perm_rows(kv_p[g][:, 1], g, t, KEEP[g]), vg[:, t, :]).then_inc(s_vo, 16)

                def store_record(n):
                    g, j = ATT[n]
                    sp.wait_ge(s_rec, n + 1)
                    sp.dma_start(perm_rows(att_d[g, 0:SEQ], g, j), rec[:, n % 4, :]) \
                      .then_inc(s_recd[n % 4], 16)

                for i in range(NSTEP + 3):
                    if i + 3 < TILES:
                        load_x(i + 3)
                    c = STEPS[i][0] if i < NSTEP else None
                    if i < NSTEP and i == FIRST_STEP[c]:
                        if CHUNKS[c][0] == "q":
                            g = CHUNKS[c][1]
                            if g:
                                sp.wait_ge(s_rope, ROTPOS[FIRST_STEP[c - 2] - 1] + 1)
                            sp.dma_start(cs[:], a["c_rope"][g].rearrange("t p c -> p t c")).then_inc(s_cs, 16)
                        if 1 <= c and c + 1 < NC1:
                            load_chunk(c + 1)
                    if 2 <= i < NSTEP + 2:
                        store_rows(i - 2)
                    if i - 4 in AT_STEP:
                        store_record(AT_STEP[i - 4])
                for s in range(3):
                    sp.wait_ge(s_ro[s], 16 * ring_stored(max(n for n in range(len(RING)) if n % 3 == s)))
                for s in range(4):
                    sp.wait_ge(s_recd[s], 16 * rec_stored(max(n for n in range(len(ATT)) if n % 4 == s)))
                sp.wait_ge(s_vo, 16 * v_stored(NG - 1))

            @block.gpsimd
            def _(pool):
                link = chain_of(pool, s_pool)
                for i in ROTATED:
                    c, t, _ = STEPS[i]
                    g, r, n = CHUNKS[c][1], rows(STEPS[i][1]), ROTPOS[i]
                    slot = RPOS[i] % 3
                    pool.wait_ge(s_z, DPOS[i] + 1)
                    pool.wait_ge(s_cs, 16 * (g + 1))
                    z = zr[0:r, n % 2, :].rearrange("p (h e) -> p h e", h=H)
                    cosb = cs[0:r, t, 0:DH].unsqueeze(1).to_broadcast([r, H, DH])
                    sin_lo = cs[0:r, t, DH:DH + 32].unsqueeze(1).to_broadcast([r, H, 32])
                    sin_hi = cs[0:r, t, DH + 32:2 * DH].unsqueeze(1).to_broadcast([r, H, 32])
                    t0 = ropet[0:r, 0, :].rearrange("p (h e) -> p h e", h=H)
                    t1 = ropet[0:r, 1, :].rearrange("p (h e) -> p h e", h=H)
                    pool.tensor_tensor(t0, z, cosb, ALU.mult).then_inc(s_pool, 1)
                    pool.tensor_tensor(t1[:, :, 0:32], z[:, :, 32:DH], sin_lo, ALU.mult).then_inc(s_pool, 1)
                    pool.tensor_tensor(t1[:, :, 32:DH], z[:, :, 0:32], sin_hi, ALU.mult).then_inc(s_pool, 1)
                    pool.wait_ge(s_pool, 3 * (n + 1))
                    if RPOS[i] >= 3:
                        old = RING[RPOS[i] - 3]
                        if old in TPOS:
                            pool.wait_ge(s_rT, TPOS[old] + 1)
                        if ring_stored(RPOS[old]):
                            pool.wait_ge(s_ro[slot], 16 * ring_stored(RPOS[old]))
                    pool.tensor_tensor(rot[0:r, slot, :], ropet[0:r, 0, :], ropet[0:r, 1, :], ALU.add) \
                        .then_inc(s_rope, 1)
                    pool.wait_ge(s_rope, n + 1)

            @block.scalar
            def _(act):
                def h_hi(t):
                    r = rows(t)
                    act.wait_ge(s_hT, t + 1)
                    for half in range(2):
                        src = bank(3 + 2 * (t % 2) + half).rearrange("p (k q) -> p k q", k=4)[:, :, 0:r]
                        nc.scalar.copy(hh[:, 4 * half:4 * half + 4, t * P:t * P + r], src).then_inc(s_hh, 1)

                act.wait_ge(s_const, 16 * 3)
                act.wait_ge(s_eps, 2)
                act.wait_ge(s_bT, 1)
                nc.scalar.copy(bcol[:], bank(0)[:, 0:ZW // P]).then_inc(s_bcol, 1)
                def split_hi(c):
                    act.wait_ge(s_w[c % 2], 16 * (c // 2 + 1))
                    if c >= 2:
                        act.wait_ge(s_pj, FIRST_STEP[c - 1])
                    nc.scalar.activation(wh[:, c % 2].rearrange("p k n -> p (k n)"),
                                         raw[:, c % 2].rearrange("p k n -> p (k n)"),
                                         ACT.Copy).then_inc(s_wh, 1)

                def norm_root(t):
                    r = rows(t)
                    act.wait_ge(s_sq, 2 * t + 1)
                    nc.scalar.activation(ss[0:r, t:t + 1], ss[0:r, t:t + 1], ACT.Sqrt, scale=1.0 / D,
                                         bias=eps[0:r, :]).then_inc(s_sq, 1)

                norm_root(0)
                norm_root(1)
                h_hi(0)
                split_hi(0)
                h_hi(1)
                for i in range(NSTEP + 3):
                    if i + 2 < TILES:
                        norm_root(i + 2)
                        h_hi(i + 2)
                    if i < NSTEP and STEPS[i][0] + 1 < NC1 and i == FIRST_STEP[STEPS[i][0]] + 1:
                        split_hi(STEPS[i][0] + 1)
                    if i < NSTEP and CHUNKS[STEPS[i][0]][0] == "u":
                        c, n, j = STEPS[i]
                        f = 2 * CHUNKS[c][1] + n
                        act.wait_ge(s_pj, i + 1)
                        act.wait_ge(s_bcol, 1)
                        nc.scalar.activation(uT[:, f, j * TC:(j + 1) * TC], bank(i % 2)[:, 0:TC],
                                             ACT.Gelu_apprx_tanh,
                                             bias=bcol[:, COL_U // P + f:COL_U // P + f + 1]).then_inc(s_fm, 1)
                    if i >= 2 and i - 2 in TPOS:
                        n = TPOS[i - 2]
                        c, t, _ = STEPS[i - 2]
                        dst = qT if CHUNKS[c][0] == "q" else kT
                        act.wait_ge(s_rT, n + 1)
                        nc.scalar.copy(dst[:, :, t * P:(t + 1) * P],
                                       bank(2)[:, 0:2 * P].rearrange("p (a q) -> p a q", a=2)).then_inc(s_qk, 1)
                    if i >= 1 and i - 1 in AT_STEP:
                        b = AT_STEP[i - 1]
                        act.wait_ge(s_pT, b + 1)
                        nc.scalar.copy(probT[:, 0:H, :].rearrange("p a q -> p (a q)"), bank(5)).then_inc(s_pTa, 1)
                    if i in AT_STEP:
                        b = AT_STEP[i]
                        g, j = ATT[b]
                        k0 = 0 if has_prev(g, j) else P
                        act.wait_ge(s_nm, b + 1)
                        for h in range(H):
                            e = nc.scalar.activation(prob[:, h, k0:2 * P], prob[:, h, k0:2 * P], ACT.Exp,
                                                     bias=rec[:, b % 4, HW + h:HW + h + 1],
                                                     accum_out=rec[:, b % 4, HW + H + h:HW + H + h + 1])
                        e.then_inc(s_ex, 1)
                    if i >= 1 and i - 1 < NSTEP and CHUNKS[STEPS[i - 1][0]][0] == "va":
                        c, t, _ = STEPS[i - 1]
                        half = va[0:rows(t), t, CHUNKS[c][1] * CW:(CHUNKS[c][1] + 1) * CW]
                        act.wait_ge(s_z, DPOS[i - 1] + 1)
                        nc.scalar.activation(half, half, ACT.Gelu_apprx_tanh).then_inc(s_gelu, 1)

            @block.vector
            def _(dve):
                link = chain_of(dve, s_dve)
                nc.vector.memset(eps[:], EPS).then_inc(s_eps, 1)
                nc.vector.memset(logits[:, NT, :], 0.0).then_inc(s_eps, 1)
                dve.wait_ge(s_const, 16 * 3)

                def split_lo(c):
                    dve.wait_ge(s_wh, c + 1)
                    nc.vector.tensor_tensor(wl[:, c % 2].rearrange("p k n -> p (k n)"),
                                            raw[:, c % 2].rearrange("p k n -> p (k n)"),
                                            wh[:, c % 2].rearrange("p k n -> p (k n)").bitcast(F32),
                                            ALU.subtract).then_inc(s_wl, 1)

                def h_lo(t):
                    r = rows(t)
                    for half in range(2):
                        dve.wait_ge(s_hh, 2 * t + half + 1)
                        src = bank(3 + 2 * (t % 2) + half).rearrange("p (k q) -> p k q", k=4)[:, :, 0:r]
                        cols = slice(t * P, t * P + r)
                        ks = slice(4 * half, 4 * half + 4)
                        nc.vector.tensor_tensor(hl[:, ks, cols], src, hh[:, ks, cols].bitcast(F32),
                                                ALU.subtract).then_inc(s_hl, 1)

                def norm_rows(t):
                    r = rows(t)
                    xr = xin[0:r, t % 3, :]
                    dve.wait_ge(s_x[t % 3], 16 * (t // 3 + 1))
                    if t:
                        dve.wait_ge(s_sq, 2 * t)
                    nc.vector.tensor_tensor_reduce(junk[0:r, :], xr, xr, 1.0, 0.0, ALU.mult, ALU.add,
                                                   ss[0:r, t:t + 1]).then_inc(s_sq, 1)
                    dve.wait_ge(s_sq, 2 * (t + 1))
                    rs = rstd[0:r, t:t + 1]
                    link(nc.vector.reciprocal(rs, ss[0:r, t:t + 1]))
                    nc.vector.scalar_tensor_tensor(xr, xr, rs, g1row[0:r, :], ALU.mult, ALU.mult).then_inc(s_hn, 1)

                norm_rows(0)
                norm_rows(1)
                h_lo(0)
                split_lo(0)
                h_lo(1)
                for i in range(NSTEP + 3):
                    if i + 2 < TILES:
                        norm_rows(i + 2)
                    if i < NSTEP and STEPS[i][0] + 1 < NC1 and i == FIRST_STEP[STEPS[i][0]] + 1:
                        split_lo(STEPS[i][0] + 1)
                    if i in DPOS:
                        c, t, _ = STEPS[i]
                        kind, g, _ = CHUNKS[c]
                        r = rows(t)
                        dve.wait_ge(s_pj, i + 1)
                        dve.wait_ge(s_b[c % 2], 16 * (c // 2 + 1))
                        if kind in "qk":
                            if ROTPOS[i] >= 2:
                                dve.wait_ge(s_rope, ROTPOS[i] - 1)
                            dst = zr[0:r, ROTPOS[i] % 2, :]
                        elif kind == "va":
                            dst = va[0:r, t, g * CW:(g + 1) * CW]
                        elif t < NT:
                            if g and t == 0:
                                dve.wait_ge(s_vo, 16 * v_stored(g - 1))
                                dve.wait_ge(s_pv, NT * g)
                            dst = vg[:, t, :]
                        else:
                            old = RING[RPOS[i] - 3]
                            if old in TPOS:
                                dve.wait_ge(s_rT, TPOS[old] + 1)
                            if ring_stored(RPOS[old]):
                                dve.wait_ge(s_ro[RPOS[i] % 3], 16 * ring_stored(RPOS[old]))
                            dst = rot[0:r, RPOS[i] % 3, :]
                        nc.vector.tensor_tensor(dst, bank(i % 2)[0:r, 0:CW], brow[0:r, c % 2, :],
                                                ALU.add).then_inc(s_z, 1)
                    if i + 2 < TILES:
                        h_lo(i + 2)
                    if i >= 2 and i - 2 in AT_STEP:
                        b = AT_STEP[i - 2]
                        dve.wait_ge(s_pv, b + 1)
                        nc.vector.tensor_copy(rec[:, b % 4, 0:HW], bank(7)[:, 0:HW]).then_inc(s_rec, 1)
                    if i >= 1 and i - 1 in AT_STEP:
                        b = AT_STEP[i - 1]
                        if has_prev(*ATT[b]):
                            dve.wait_ge(s_pT, b + 1)
                            nc.vector.tensor_copy(probT[:, H:2 * H, :].rearrange("p a q -> p (a q)"),
                                                  bank(6)).then_inc(s_pTb, 1)
                    if i in AT_STEP:
                        b = AT_STEP[i]
                        g, j = ATT[b]
                        k0 = 0 if has_prev(g, j) else P
                        m = (mask2[:, :] if g == 2 else mask[:, k0:2 * P]).unsqueeze(1)
                        dve.wait_ge(s_sc, b + 1)
                        if b == 0:
                            dve.wait_ge(s_mask, 16 * 2)
                        if b:
                            dve.wait_ge(s_pT, b)
                        if b >= 4:
                            dve.wait_ge(s_recd[b % 4], 16 * rec_stored(b - 4))
                        for pair in range(2):
                            src = bank(3 + pair).rearrange("p (h k) -> p h k", h=2)[:, :, k0:2 * P]
                            nc.vector.scalar_tensor_tensor(
                                prob[:, pair:H:2, k0:2 * P], src, SCALE,
                                m.to_broadcast([P, 2, 2 * P - k0]), ALU.mult, ALU.add).then_inc(s_sb, 1)
                        dve.wait_ge(s_sb, 2 * b + 2)
                        nc.vector.tensor_reduce(rec[:, b % 4, HW:HW + H], prob[:, :, k0:2 * P], X, ALU.max,
                                                negate=True).then_inc(s_nm, 1)
                    if i >= 2 and i - 2 < NSTEP and CHUNKS[STEPS[i - 2][0]][:2] == ("va", 1):
                        t = STEPS[i - 2][1]
                        r = rows(t)
                        dve.wait_ge(s_gelu, TILES + t + 1)
                        v = va[0:r, t, :]
                        link(nc.vector.bn_stats(lnst[0:r, 0:6], v))
                        nc.vector.bn_aggr(mv[0:r, t, :], lnst[0:r, 0:6]).then_inc(s_ln, 1)
                        dve.wait_ge(s_ln, t + 1)

            @block.tensor
            def _(pe):
                pe.wait_ge(s_const, 16 * 3)
                nc.tensor.transpose(bank(0)[:, 0:ZW // P], brows[:], ident[0:ZW // P, 0:ZW // P]).then_inc(s_bT, 1)
                def norm_T(t):
                    r = rows(t)
                    pe.wait_ge(s_hn, t + 1)
                    if t >= 2:
                        pe.wait_ge(s_hl, 2 * (t - 1))
                    for k in range(KD):
                        dst = bank(3 + 2 * (t % 2) + k // 4)[:, (k % 4) * P:(k % 4) * P + r]
                        m = nc.tensor.transpose(dst, xin[0:r, t % 3, k * P:(k + 1) * P], ident[0:r, 0:r])
                    m.then_inc(s_hT, 1)

                norm_T(0)
                norm_T(1)

                def project(i):
                    c, t, j = STEPS[i]
                    kind, g, _ = CHUNKS[c]
                    if i < TILES:
                        pe.wait_ge(s_hl, 2 * (i + 1))
                    if i == 0:
                        pe.wait_ge(s_bcol, 1)
                    if i == FIRST_STEP[c]:
                        pe.wait_ge(s_wl, c + 1)
                    if i >= 2:
                        wait_evicted(pe, i - 2)
                    for k in range(KD):
                        H_, L_ = wh[:, c % 2, k], wl[:, c % 2, k]
                        if kind == "u":
                            dst = bank(i % 2)[:, 0:TC]
                            xs = (hh[:, k, j * TC:(j + 1) * TC], hl[:, k, j * TC:(j + 1) * TC])
                            H_, L_ = H_[:, t * P:(t + 1) * P], L_[:, t * P:(t + 1) * P]
                            trio = ((H_, xs[0]), (H_, xs[1]), (L_, xs[0]))
                        else:
                            dst = bank(i % 2)[0:rows(t), 0:CW]
                            order = g if kind in "qkv" else 0
                            xs = (perm_cols(hh[:, k, :], order, t), perm_cols(hl[:, k, :], order, t))
                            trio = ((xs[0], H_), (xs[0], L_), (xs[1], H_))
                        for n, (st, mv) in enumerate(trio):
                            m = nc.tensor.matmul(dst, st, mv, start=(k == 0 and n == 0),
                                                 stop=(k == KD - 1 and n == 2))
                    m.then_inc(s_pj, 1)

                for i in range(NSTEP + 3):
                    if i < NSTEP:
                        project(i)
                    if i + 2 < TILES:
                        norm_T(i + 2)
                    if i >= 2 and i - 2 in TPOS:
                        n = TPOS[i - 2]
                        pe.wait_ge(s_rope, ROTPOS[i - 2] + 1)
                        if n:
                            pe.wait_ge(s_qk, n)
                        for pair in range(2):
                            m = nc.tensor.transpose(bank(2)[:, pair * P:(pair + 1) * P],
                                                    rot[:, RPOS[i - 2] % 3, pair * P:(pair + 1) * P], ident[:])
                        m.then_inc(s_rT, 1)
                    if i >= 2 and i - 2 in AT_STEP:
                        b = AT_STEP[i - 2]
                        g, j = ATT[b]
                        pe.wait_ge(s_pTa, b + 1)
                        if has_prev(g, j):
                            pe.wait_ge(s_pTb, with_prev(b + 1))
                        if b:
                            pe.wait_ge(s_rec, b)
                        for h in range(H):
                            vcols = slice(h * DH, (h + 1) * DH)
                            m = nc.tensor.matmul(bank(7)[:, vcols], probT[:, h], vg[:, j, vcols],
                                                 start=True, stop=not has_prev(g, j))
                            if has_prev(g, j):
                                m = nc.tensor.matmul(bank(7)[:, vcols], probT[:, H + h], vg[:, j - 1, vcols],
                                                     start=False, stop=True)
                        m.then_inc(s_pv, 1)
                    if i >= 1 and i - 1 in AT_STEP:
                        b = AT_STEP[i - 1]
                        g, j = ATT[b]
                        pe.wait_ge(s_ex, b + 1)
                        if b:
                            pe.wait_ge(s_pTa, b)
                        if with_prev(b):
                            pe.wait_ge(s_pTb, with_prev(b))
                        for h in range(H):
                            m = nc.tensor.transpose(bank(5)[:, h * P:(h + 1) * P], prob[:, h, P:2 * P], ident[:])
                            if has_prev(g, j):
                                m = nc.tensor.transpose(bank(6)[:, h * P:(h + 1) * P], prob[:, h, 0:P], ident[:])
                        m.then_inc(s_pT, 1)
                    if i in AT_STEP:
                        b = AT_STEP[i]
                        g, j = ATT[b]
                        k0 = 0 if has_prev(g, j) else P
                        pe.wait_ge(s_qk, 2 * NT * (g + 1))
                        if b:
                            pe.wait_ge(s_sb, 2 * b)
                        for h in range(H):
                            hp = slice(DH * (h % 2), DH * (h % 2) + DH)
                            keys = kT[hp, h // 2, j * P - P + k0:(j + 1) * P]
                            m = nc.tensor.matmul(bank(3 + h % 2)[:, (h // 2) * 2 * P + k0:(h // 2 + 1) * 2 * P],
                                                 qT[hp, h // 2, j * P:(j + 1) * P], keys, start=True, stop=True)
                        m.then_inc(s_sc, 1)

        r2 = Region(r1b_at)
        sah = r2("s_a_T_hi", [P, 4, TOK], F32R)
        sal = r2("s_a_T_lo", [P, 4, TOK], F32R)
        r2b_at = r2.at
        wsT = r2("w_spatial_T", [P, 8, P])
        wsp = r2("w_spatial_rows", [P, 8, P])
        bsb = r2("b_spatial_rows", [P, 4, P])
        lng = r2("ln_gain_row", [P, AW])
        sar = r2("s_a_T", [P, AW])
        lnb = r2("ln_bias_row", [P, AW])
        causal = r2("causal_T", [P, P])
        w00 = r2("w_spatial_first", [NS, 8])
        b00 = r2("b_spatial_first", [NS, 8])

        s_mc = sem("mix_consts_in")
        s_dve2 = sem("vector_chain_mix")
        s_smix = sem("sample_mix_ready")
        s_wsT = sem("w_spatial_transposed")
        s_wsm = sem("w_spatial_masked")
        s_sd = sem("va_deviation_ready")
        s_ri = sem("va_scale_ready")
        s_nv = sem("va_scaled")
        s_vn = sem("va_normed")
        s_vno = sem("v_chunk_stored")
        s_mx = sem("mixed")
        s_sa = sem("s_a_ready")
        s_sah = sem("s_a_hi_ready")
        s_sal = sem("s_a_lo_ready")

        def split_hi_chunk(act, c):
            act.wait_ge(s_w[c % 2], 16 * (c // 2 + 1))
            nc.scalar.activation(wh[:, c % 2].rearrange("p k n -> p (k n)"),
                                 raw[:, c % 2].rearrange("p k n -> p (k n)"), ACT.Copy).then_inc(s_wh, 1)

        def split_lo_chunk(dve, c):
            dve.wait_ge(s_wh, c + 1)
            nc.vector.tensor_tensor(wl[:, c % 2].rearrange("p k n -> p (k n)"),
                                    raw[:, c % 2].rearrange("p k n -> p (k n)"),
                                    wh[:, c % 2].rearrange("p k n -> p (k n)").bitcast(F32),
                                    ALU.subtract).then_inc(s_wl, 1)

        with nc.Block() as block:
            @block.sync
            def _(sp):
                sp.dma_start(wsp[:], a["w_spatial"][0].rearrange("g t s -> t g s")).then_inc(s_mc, 16)
                sp.dma_start(causal[:], a["c_causal_T"]).then_inc(s_mc, 16)
                sp.dma_start(lng[:], a["a_ln_g"][0].partition_broadcast(P)).then_inc(s_mc, 16)
                sp.dma_start(lnb[:], a["a_ln_b"][0].partition_broadcast(P)).then_inc(s_mc, 16)
                bs = a["b_spatial"][0].rearrange("(m two) t -> two m t", two=2)
                for two in range(2):
                    sp.dma_start(bsb[64 * two:64 * two + 64], bs[two].partition_broadcast(64)).then_inc(s_mc, 16)
                with nc.allow_non_contiguous_dma(reason="eight single elements each"):
                    sp.dma_start(w00[:], a["w_spatial"][0, :, 0, 0:1].rearrange("g o -> o g")[0]
                                 .partition_broadcast(NS)).then_inc(s_mc, 16)
                    sp.dma_start(b00[:], a["b_spatial"][0, :, 0:1].rearrange("g o -> o g")[0]
                                 .partition_broadcast(NS)).then_inc(s_mc, 16)
                for c in range(NC1, NC1 + 2):
                    col = CHUNKS[c][2]
                    sp.dma_start(raw[:, c % 2], w_in_v[:, :, col:col + CW]).then_inc(s_w[c % 2], 16)
                sp.wait_ge(s_vn, TILES)
                sp.dma_start(v_chunk, va[0:NS, NT, :]).then_inc(s_vno, 16)
                sp.wait_ge(s_vno, 16)

            @block.gpsimd
            def _(pool):
                pool.wait_ge(s_mc, 16 * 8)
                for t in range(TILES):
                    r = rows(t)
                    pool.wait_ge(s_nv, t + 1)
                    pool.tensor_tensor(va[0:r, t, :], va[0:r, t, :], lng[0:r, :], ALU.mult).then_inc(s_pool, 1)
                    pool.wait_ge(s_pool, 3 * len(ROTATED) + t + 1)
                    pool.tensor_tensor(va[0:r, t, :], va[0:r, t, :], lnb[0:r, :], ALU.add).then_inc(s_vn, 1)

            @block.scalar
            def _(act):
                nc.scalar.activation(mv[:, 0:NT, 1], mv[:, 0:NT, 1], ACT.Sqrt, bias=eps[:]).then_inc(s_sd, 1)
                nc.scalar.activation(mv[0:NS, NT, 1:2], mv[0:NS, NT, 1:2], ACT.Sqrt,
                                     bias=eps[0:NS, :]).then_inc(s_sd, 1)
                for c in range(NC1, NC1 + 2):
                    split_hi_chunk(act, c)
                for t in range(TILES):
                    r = rows(t)
                    act.wait_ge(s_sa, t + 1)
                    nc.scalar.copy(sah[:, :, t * P:t * P + r],
                                   sar[:, 0:4 * r].rearrange("p (m q) -> p m q", m=4)).then_inc(s_sah, 1)

            @block.vector
            def _(dve):
                link = chain_of(dve, s_dve2)
                dve.wait_ge(s_sd, 2)
                nc.vector.reciprocal(mv[:, 0:NT, 1], mv[:, 0:NT, 1]).then_inc(s_ri, 1)
                nc.vector.reciprocal(mv[0:NS, NT, 1:2], mv[0:NS, NT, 1:2]).then_inc(s_ri, 1)
                dve.wait_ge(s_ri, 2)
                for t in range(TILES):
                    r = rows(t)
                    nc.vector.tensor_scalar(va[0:r, t, :], va[0:r, t, :], mv[0:r, t, 0:1], mv[0:r, t, 1:2],
                                            ALU.subtract, ALU.mult).then_inc(s_nv, 1)
                dve.wait_ge(s_mc, 16 * 8)
                for half in range(2):
                    dve.wait_ge(s_wsT, half + 1)
                    nc.vector.tensor_tensor(wsT[:, 4 * half:4 * half + 4, :],
                                            bank(6 + half).rearrange("p (g t) -> p g t", g=4),
                                            causal[:].unsqueeze(1).to_broadcast([P, 4, P]),
                                            ALU.mult).then_inc(s_wsm, 1)
                split_lo_chunk(dve, NC1)
                split_lo_chunk(dve, NC1 + 1)
                for t in range(TILES):
                    r = rows(t)
                    cols = slice(t * P, t * P + r)
                    sa4 = sar[:, 0:4 * r].rearrange("p (m q) -> p m q", m=4)
                    ps4 = bank(t % 2)[:, 0:4 * r].rearrange("p (m q) -> p m q", m=4)
                    if t == NT:
                        dve.wait_ge(s_vn, TILES)
                        dve.wait_ge(s_sal, NT)
                        v8 = sar[0:NS, :].rearrange("p (g c) -> p g c", g=8)
                        link(nc.vector.tensor_tensor(v8, va[0:NS, NT, :].rearrange("p (g c) -> p g c", g=8),
                                                     w00[:].unsqueeze(2).to_broadcast([NS, 8, 64]), ALU.mult))
                        nc.vector.tensor_tensor(v8, v8, b00[:].unsqueeze(2).to_broadcast([NS, 8, 64]),
                                                ALU.add).then_inc(s_smix, 1)
                        dve.wait_ge(s_mx, TILES)
                        nc.vector.tensor_tensor(sa4, ps4, uT[:, :, cols], ALU.mult).then_inc(s_sa, 1)
                    else:
                        dve.wait_ge(s_mx, t + 1)
                        if t:
                            dve.wait_ge(s_sal, t)
                        link(nc.vector.tensor_tensor(sa4, ps4, bsb[:], ALU.add))
                        nc.vector.tensor_tensor(sa4, sa4, uT[:, :, cols], ALU.mult).then_inc(s_sa, 1)
                    dve.wait_ge(s_sah, t + 1)
                    nc.vector.tensor_tensor(sal[:, :, cols], sa4, sah[:, :, cols].bitcast(F32),
                                            ALU.subtract).then_inc(s_sal, 1)

            @block.tensor
            def _(pe):
                pe.wait_ge(s_mc, 16 * 8)
                for g in range(8):
                    m = nc.tensor.transpose(bank(6 + g // 4)[:, (g % 4) * P:(g % 4 + 1) * P], wsp[:, g, :], ident[:])
                    if g % 4 == 3:
                        m.then_inc(s_wsT, 1)
                pe.wait_ge(s_wsm, 2)
                for t in range(NT):
                    pe.wait_ge(s_vn, t + 1)
                    if t >= 2:
                        pe.wait_ge(s_sa, t - 1)
                    for g in range(8):
                        dst = bank(t % 2)[64 * (g % 2):64 * (g % 2) + 64, (g // 2) * P:(g // 2 + 1) * P]
                        m = nc.tensor.matmul(dst, va[:, t, g * 64:(g + 1) * 64], wsT[:, g, :], start=True, stop=True)
                    m.then_inc(s_mx, 1)
                pe.wait_ge(s_smix, 1)
                for m4 in range(4):
                    m = nc.tensor.transpose(bank(NT % 2)[:, m4 * NS:(m4 + 1) * NS], sar[0:NS, m4 * P:(m4 + 1) * P],
                                            ident[0:NS, 0:NS])
                m.then_inc(s_mx, 1)

        NU = NCH - NC1
        GS = [(u, n, j) for u in range(NU) for n in range(2) for j in range(NTC)]
        EARLY = 2 * 2 * NTC
        s_gt = sem("gate_products")
        s_gl = sem("gate_logits_copied")
        s_glo = [sem(f"gate_logits_stored{i}") for i in range(2)]

        def gate_product(s, dst):
            u, n, j = GS[s]
            c, tok, col = NC1 + u, slice(j * TC, (j + 1) * TC), slice(n * P, (n + 1) * P)
            for k in range(KD):
                for i, (w_, x_) in enumerate(((wh, hh), (wh, hl), (wl, hh))):
                    m = nc.tensor.matmul(dst, w_[:, c % 2, k, col], x_[:, k, tok],
                                         start=(k == 0 and i == 0), stop=(k == KD - 1 and i == 2))
            m.then_inc(s_gt, 1)

        r3 = Region(r1_at, r1b_at)
        kc = r3("cached_kv", [P, NS, 2 * HW])
        qb = r3("sample_q_rows", [P, NS, HW])
        us = r3("sample_values", [H, NS, HW])
        r3b = Region(r2b_at)
        oh_ = r3b("o_T_hi", [P, 2, TOK], F32R)
        ol_ = r3b("o_T_lo", [P, 2, TOK], F32R)
        cmb_at = r3b.at
        cmb = r3b("records", [P, 2, NG, AR])
        ocm = r3b("combined_rows", [P, HW])
        wgt = r3b("chunk_weights", [P, 6, H])
        nrm = r3b("chunk_sums", [P, 6, H])
        mlo = r3b("least_minus_max", [P, H])
        den = r3b("denominator", [P, H])
        r3r = Region(raw_at, raw_at + 2 * KD * CW * 4)
        new = r3r("sample_new", [NS, 9, HW])
        ssc = r3r("sample_scores", [P, NS * H])
        spT = r3r("sample_prob_T", [P, NS * H])
        prs = r3r("sample_prob", [NS * H, P])
        sst = r3r("sample_row_stats", [NS * H, NG, 2])
        st6 = r3r("sample_stats6", [NS, 2, 6, H])
        glo = r3r("gate_logits_out", [P, 2, TC])

        s_kc = sem("cached_kv_in")
        s_qb = sem("sample_q_in")
        s_new = sem("sample_new_in")
        s_cd = sem("vector_chain_combine")
        s_ss = sem("sample_scores_ready")
        s_ssT = sem("sample_scores_transposed")
        s_snm = sem("sample_max_ready")
        s_sex = sem("sample_prob_ready")
        s_spT = sem("sample_prob_transposed")
        s_spc = sem("sample_prob_T_ready")
        s_spv = sem("sample_values_in_psum")
        s_us = sem("sample_values_ready")
        s_uso = sem("sample_records_stored")
        s_cm = [sem(f"records_in{i}") for i in range(2)]
        s_scu = sem("sample_records_in")
        s_cdf = sem("chunk_differences_ready")
        s_cw = sem("chunk_weights_ready")
        s_oc = sem("combined_ready")
        s_oT = sem("combined_transposed")
        s_oh = sem("o_T_hi_ready")
        s_ol = sem("o_T_lo_ready")

        with nc.Block() as block:
            @block.sync
            def _(sp):
                caches = [a[f"cache_kv_g{g}"][0].rearrange("b (s d) two h e -> s b d (two h e)", d=d)[:, :, 0, :]
                          for g, d in enumerate(DIL)]

                def load_group(g):
                    if g:
                        sp.wait_ge(s_spv, g)
                    sp.dma_start(kc[0:CACHED[g]], caches[g]).then_inc(s_kc, 16)
                    sp.dma_start(qb[:].rearrange("p b c -> p (b c)"),
                                 new_d[3 * g].rearrange("b c -> (b c)").partition_broadcast(P)).then_inc(s_qb, 16)

                def load_records(t):
                    if t >= 2:
                        sp.wait_ge(s_oc, t - 1)
                    sp.dma_start(cmb[:, t % 2], att_d[:, t * P:(t + 1) * P, :].rearrange("g t c -> t g c")) \
                        .then_inc(s_cm[t % 2], 16)

                load_group(0)
                sp.dma_start(new[:], new_d.rearrange("n b c -> b n c")).then_inc(s_new, 16)
                load_records(0)
                load_records(1)
                for g in range(NG):
                    if g + 1 < NG:
                        load_group(g + 1)
                    if g:
                        load_records(g + 1)
                    sp.wait_ge(s_us, g + 1)
                    for h in range(H):
                        sp.dma_start(att_d[g, SEQ:TOK, h * DH:(h + 1) * DH],
                                     us[h:h + 1, :, h * DH:(h + 1) * DH]).then_inc(s_uso, 16)
                    for n in range(2):
                        sp.dma_start(stat_d[g, n].rearrange("(r o) -> r o", o=1), sst[:, g, n:n + 1]) \
                            .then_inc(s_uso, 16)
                for t in range(NG + 1, NT):
                    load_records(t)
                sp.wait_ge(s_uso, 16 * 6 * NG)
                sp.wait_ge(s_oc, NT - 1)
                sp.dma_start(cmb[0:NS, 0, :, 0:HW], att_d[:, SEQ:TOK, 0:HW].rearrange("g b c -> b g c")) \
                    .then_inc(s_scu, 16)
                for n in range(2):
                    sp.dma_start(st6[:, n, 0:NG, :], stat_d[:, n].rearrange("g (b h) -> b g h", h=H)) \
                        .then_inc(s_scu, 16)

            @block.gpsimd
            def _(pool):
                for s in range(EARLY):
                    pool.wait_ge(s_gl, s + 1)
                    pool.dma_start(gl_d[s // NTC, :, s % NTC, :], glo[:, s % 2]).then_inc(s_glo[s % 2], 16)
                for i in range(2):
                    pool.wait_ge(s_glo[i], 16 * (EARLY // 2))

            @block.scalar
            def _(act):
                def group_exp(g):
                    nk = CACHED[g]
                    act.wait_ge(s_snm, g + 1)
                    nc.scalar.activation(prs[:, 0:nk], prs[:, 0:nk], ACT.Exp, bias=sst[:, g, 0:1],
                                         accum_out=sst[:, g, 1:2]).then_inc(s_sex, 1)
                    act.wait_ge(s_spv, g + 1)
                    if g:
                        act.wait_ge(s_uso, 16 * 6 * g)
                    for half in range(2):
                        u = nc.scalar.copy(us[:, 4 * half:4 * half + 4, :].rearrange("p b c -> p (b c)"),
                                           psum[0:H, 2 * half:2 * half + 2, :].rearrange("p b c -> p (b c)"))
                    u.then_inc(s_us, 1)

                def gate_logits(s):
                    act.wait_ge(s_gt, s + 1)
                    if s >= 2:
                        act.wait_ge(s_glo[s % 2], 16 * (s // 2))
                    nc.scalar.copy(glo[:, s % 2], bank(7)[:, 0:TC]).then_inc(s_gl, 1)

                for t in range(TILES + 1):
                    if t < NG:
                        gate_logits(2 * t)
                        gate_logits(2 * t + 1)
                        group_exp(t)
                    if t < TILES:
                        n = 6 if t == NT else NG
                        r = rows(t)
                        act.wait_ge(s_cdf, t + 1)
                        nc.scalar.activation(wgt[0:r, 0:n], nrm[0:r, 0:n], ACT.Exp).then_inc(s_cw, 1)
                    if t:
                        r = rows(t - 1)
                        cols = slice((t - 1) * P, (t - 1) * P + r)
                        act.wait_ge(s_oT, t)
                        nc.scalar.copy(oh_[:, :, cols], bank(6)[:, 0:2 * r].rearrange("p (a q) -> p a q", a=2)) \
                            .then_inc(s_oh, 1)
                    if NG <= t < TILES:
                        gate_logits(NG + t)

            @block.vector
            def _(dve):
                link = chain_of(dve, s_cd)

                def group_scores(g):
                    nk = CACHED[g]
                    dve.wait_ge(s_kc, 16 * (g + 1))
                    dve.wait_ge(s_qb, 16 * (g + 1))
                    if g:
                        dve.wait_ge(s_ssT, g)
                    link(nc.vector.tensor_tensor(kc[0:nk, :, 0:HW], kc[0:nk, :, 0:HW], qb[0:nk], ALU.mult))
                    nc.vector.tensor_reduce(ssc[0:nk, :],
                                            kc[0:nk, :, 0:HW].rearrange("p b (h e) -> p b h e", h=H),
                                            X, ALU.add).then_inc(s_ss, 1)

                def group_max(g):
                    nk = CACHED[g]
                    dve.wait_ge(s_ssT, g + 1)
                    if g:
                        dve.wait_ge(s_spT, g)
                    link(nc.vector.tensor_scalar(prs[:, 0:nk], bank(4)[0:NS * H, 0:nk], SCALE, None, ALU.mult))
                    nc.vector.tensor_reduce(sst[:, g, 0:1], prs[:, 0:nk], X, ALU.max, negate=True).then_inc(s_snm, 1)
                    dve.wait_ge(s_spT, g + 1)
                    if g:
                        dve.wait_ge(s_spv, g)
                    nc.vector.tensor_copy(spT[0:nk, :], bank(5)[0:nk, 0:NS * H]).then_inc(s_spc, 1)

                def combine(t):
                    r = rows(t)
                    if t < NT:
                        n = NG
                        dve.wait_ge(s_cm[t % 2], 16 * (t // 2 + 1))
                        rec_ = cmb[:, t % 2]
                        nm, ls = rec_[:, :, HW:HW + H], rec_[:, :, HW + H:AR]
                    else:
                        n = 6
                        dve.wait_ge(s_scu, 16 * 3)
                        dve.wait_ge(s_new, 16)
                        rec_ = cmb[0:NS, 0]
                        q3 = new[:].rearrange("p (g w) c -> p g w c", g=NG)
                        link(nc.vector.tensor_tensor(q3[:, :, 0, :], q3[:, :, 0, :], q3[:, :, 1, :], ALU.mult))
                        link(nc.vector.tensor_reduce(st6[:, 0, NG:6, :],
                                                     q3[:, :, 0, :].rearrange("p g (h e) -> p g h e", h=H),
                                                     X, ALU.add))
                        link(nc.vector.tensor_scalar(st6[:, 0, NG:6, :], st6[:, 0, NG:6, :], -SCALE, None,
                                                     ALU.mult))
                        link(nc.vector.memset(st6[:, 1, NG:6, :], 1.0))
                        nm, ls = st6[:, 0], st6[:, 1]
                    lo, w, dd = mlo[0:r, :], wgt[0:r, 0:n], den[0:r, :]
                    link(nc.vector.tensor_reduce(lo, nm.rearrange("p g h -> p h g"), X, ALU.min))
                    if t:
                        dve.wait_ge(s_cw, t)
                    nc.vector.tensor_tensor(nrm[0:r, 0:n], lo.unsqueeze(1).to_broadcast([r, n, H]), nm,
                                            ALU.subtract).then_inc(s_cdf, 1)
                    dve.wait_ge(s_cw, t + 1)
                    link(nc.vector.tensor_tensor(nrm[0:r, 0:n], w, ls, ALU.mult))
                    link(nc.vector.tensor_reduce(dd, nrm[0:r, 0:n].rearrange("p g h -> p h g"), X, ALU.add))
                    link(nc.vector.reciprocal(dd, dd))
                    link(nc.vector.tensor_tensor(w, w, dd.unsqueeze(1).to_broadcast([r, n, H]), ALU.mult))
                    u4 = rec_[:, :, 0:HW].rearrange("p g (h e) -> p g h e", h=H)
                    link(nc.vector.tensor_tensor(u4, u4, w[:, 0:NG].unsqueeze(3).to_broadcast([r, NG, H, DH]),
                                                 ALU.mult))
                    if t:
                        dve.wait_ge(s_oT, t)
                    red = nc.vector.tensor_reduce(ocm[0:r, :], rec_[:, :, 0:HW].rearrange("p g c -> p c g"),
                                                  X, ALU.add)
                    if t < NT:
                        red.then_inc(s_oc, 1)
                    else:
                        link(red)
                        vs = new[:].rearrange("p (g w) c -> p g w c", g=NG)
                        for g in range(NG):
                            v3 = vs[:, g, 2, :].rearrange("p (h e) -> p h e", h=H)
                            link(nc.vector.tensor_tensor(v3, v3, w[:, NG + g].unsqueeze(2)
                                                         .to_broadcast([NS, H, DH]), ALU.mult))
                            add = nc.vector.tensor_tensor(ocm[0:NS, :], ocm[0:NS, :], vs[:, g, 2, :], ALU.add)
                            if g < NG - 1:
                                link(add)
                        add.then_inc(s_oc, 1)

                for t in range(TILES + 1):
                    if t < NG:
                        group_scores(t)
                        group_max(t)
                    if t < TILES:
                        combine(t)
                    if t:
                        r = rows(t - 1)
                        cols = slice((t - 1) * P, (t - 1) * P + r)
                        dve.wait_ge(s_oh, t)
                        nc.vector.tensor_tensor(ol_[:, :, cols], bank(6)[:, 0:2 * r].rearrange("p (a q) -> p a q", a=2),
                                                oh_[:, :, cols].bitcast(F32), ALU.subtract).then_inc(s_ol, 1)

            @block.tensor
            def _(pe):
                def gates(s, steps):
                    for s in range(s, s + steps):
                        pe.wait_ge(s_wl, NC1 + GS[s][0] + 1)
                        if s:
                            pe.wait_ge(s_gl, s)
                        gate_product(s, bank(7)[:, 0:TC])

                for t in range(TILES):
                    if t < NG:
                        gates(2 * t, 2)
                        g, nk = t, CACHED[t]
                        pe.wait_ge(s_ss, g + 1)
                        if g:
                            pe.wait_ge(s_snm, g)
                        nc.tensor.transpose(bank(4)[0:NS * H, 0:nk], ssc[0:nk, :], ident[0:nk, 0:nk]).then_inc(s_ssT, 1)
                        pe.wait_ge(s_sex, g + 1)
                        if g:
                            pe.wait_ge(s_spc, g)
                        nc.tensor.transpose(bank(5)[0:nk, 0:NS * H], prs[:, 0:nk],
                                            ident[0:NS * H, 0:NS * H]).then_inc(s_spT, 1)
                        pe.wait_ge(s_spc, g + 1)
                        if g:
                            pe.wait_ge(s_us, g)
                        for b in range(NS):
                            m = nc.tensor.matmul(bank(b // 2)[0:H, (b % 2) * HW:(b % 2 + 1) * HW],
                                                 spT[0:nk, b * H:(b + 1) * H], kc[0:nk, b, HW:2 * HW],
                                                 start=True, stop=True)
                        m.then_inc(s_spv, 1)
                    else:
                        gates(NG + t, 1)
                    r = rows(t)
                    pe.wait_ge(s_oc, t + 1)
                    if t:
                        pe.wait_ge(s_ol, t)
                    for pair in range(2):
                        m = nc.tensor.transpose(bank(6)[:, pair * r:(pair + 1) * r], ocm[0:r, pair * P:(pair + 1) * P],
                                                ident[0:r, 0:r])
                    m.then_inc(s_oT, 1)

        r4 = Region(r1_at, r1b_at)
        abh = r4("proj_hi", [P, 2, 4, CW], F32R)
        abl = r4("proj_lo", [P, 2, 4, CW], F32R)
        abr = r4("proj_raw", [P, 4, CW])
        mrg = r4("merged_T", [P, 2, TOK])
        sig = r4("gate_sigmoid", [P, 2, TC])
        prd = r4("gated_product", [P, 2, TC])

        gl = Region(cmb_at)("gate_logits_in", [P, 2, NTC, TC])

        s_gli = [sem(f"gate_logits_in{n}") for n in range(2)]
        s_wo = [sem_b(f"w_o_chunk_in{i}") for i in range(2)]
        wo_v = a["w_o"][0].rearrange("(k p) n -> p k n", p=P)
        s_ab = sem("proj_in")
        s_abh = sem("proj_hi_ready")
        s_abl = sem("proj_lo_ready")
        s_pr = sem("proj_products")
        s_sg = sem("sigmoid_ready")
        s_gp = sem("gated_ready")
        s_mg = sem("merged_ready")
        s_mo = [sem(f"merged_stored{n}") for n in range(2)]

        def proj_k(u):
            return 4 if u % 2 == 0 else 2

        with nc.Block() as block:
            @block.sync
            def _(sp):
                def load_unit(u):
                    if u:
                        sp.wait_ge(s_abl, u)
                    cols = slice((u // 2) * CW, (u // 2 + 1) * CW)
                    w = wa_v if u % 2 == 0 else wb_v
                    sp.dma_start(abr[:, 0:proj_k(u)], w[:, :, cols]).then_inc(s_ab, 16)

                def store_merged(i, n):
                    sp.wait_ge(s_mg, (2 * i + n + 1) * NTC)
                    row = (2 * i + n) * P
                    sp.dma_start(mt_d[row:row + P, :], mrg[:, n, :]).then_inc(s_mo[n], 16)

                def load_logits(u, n):
                    if u:
                        sp.wait_ge(s_sg, NTC * (n + 1))
                    sp.dma_start(gl[:, n], gl_d[2 * u + n]).then_inc(s_gli[n], 16)

                load_unit(0)
                load_logits(0, 0)
                load_logits(0, 1)
                for u in range(NU):
                    if u + 1 < NU:
                        load_unit(u + 1)
                    if u + 2 < NU:
                        c = NC1 + u + 2
                        sp.wait_ge(s_wl, c - 1)
                        sp.dma_start(raw[:, c % 2], w_in_v[:, :, CHUNKS[c][2]:CHUNKS[c][2] + CW]) \
                            .then_inc(s_w[c % 2], 16)
                    if u == 0:
                        load_logits(1, 0)
                        load_logits(1, 1)
                    if u % 2 == 0 and u:
                        store_merged(u // 2 - 1, 0)
                        store_merged(u // 2 - 1, 1)
                for c in range(2):
                    sp.wait_ge(s_wl, NCH)
                    sp.dma_start(raw[:, c], wo_v[:, :, c * CW:(c + 1) * CW]).then_inc(s_wo[c], 16)
                store_merged(NU // 2 - 1, 0)
                store_merged(NU // 2 - 1, 1)
                for n in range(2):
                    sp.wait_ge(s_mo[n], 16 * (NU // 2))

            @block.scalar
            def _(act):
                def unit_hi(u):
                    act.wait_ge(s_ab, 16 * (u + 1))
                    if u >= 2:
                        act.wait_ge(s_pr, 6 * (u - 1))
                    nc.scalar.copy(abh[:, u % 2, 0:proj_k(u)], abr[:, 0:proj_k(u)]).then_inc(s_abh, 1)

                unit_hi(0)
                for s, (u, n, j) in enumerate(GS):
                    if n == 0 and j == 1:
                        if u + 1 < NU:
                            unit_hi(u + 1)
                            if u:
                                act.wait_ge(s_gt, 6 * u)
                                split_hi_chunk(act, NC1 + u + 1)
                    f = (2 * (u // 2) + n) + (COL_GA if u % 2 == 0 else COL_GB) // P
                    if s < EARLY:
                        act.wait_ge(s_gli[n], 16 * (u + 1))
                    else:
                        act.wait_ge(s_gt, s + 1)
                    if s >= 2:
                        act.wait_ge(s_gp, s - 1)
                    nc.scalar.activation(sig[:, s % 2], gl[:, n, j] if s < EARLY else bank(s % 2)[:, 0:TC], ACT.Sigmoid,
                                         bias=bcol[:, f:f + 1]).then_inc(s_sg, 1)

            @block.vector
            def _(dve):
                def unit_lo(u):
                    dve.wait_ge(s_abh, u + 1)
                    nc.vector.tensor_tensor(abl[:, u % 2, 0:proj_k(u)], abr[:, 0:proj_k(u)],
                                            abh[:, u % 2, 0:proj_k(u)].bitcast(F32), ALU.subtract).then_inc(s_abl, 1)

                unit_lo(0)
                nm = 0
                for s, (u, n, j) in enumerate(GS):
                    if n == 0 and j == 1:
                        if u + 1 < NU:
                            unit_lo(u + 1)
                            if u:
                                split_lo_chunk(dve, NC1 + u + 1)
                    dst = mrg[:, n, j * TC:(j + 1) * TC]
                    dve.wait_ge(s_sg, s + 1)
                    dve.wait_ge(s_pr, s + 1)
                    if u % 2 == 0:
                        if u:
                            dve.wait_ge(s_mo[n], 16 * (u // 2))
                        nc.vector.tensor_tensor(dst, bank(2 + s % 2)[:, 0:TC], sig[:, s % 2], ALU.mult) \
                            .then_inc(s_gp, 1)
                    else:
                        if nm >= 2:
                            dve.wait_ge(s_mg, nm - 1)
                        nc.vector.tensor_tensor(prd[:, nm % 2], bank(2 + s % 2)[:, 0:TC], sig[:, s % 2], ALU.mult) \
                            .then_inc(s_gp, 1)
                        dve.wait_ge(s_gp, s + 1)
                        nc.vector.tensor_tensor(dst, dst, prd[:, nm % 2], ALU.add).then_inc(s_mg, 1)
                        nm += 1

            @block.tensor
            def _(pe):
                for s, (u, n, j) in enumerate(GS):
                    tok, col = slice(j * TC, (j + 1) * TC), slice(n * P, (n + 1) * P)
                    if s >= EARLY:
                        pe.wait_ge(s_wl, NC1 + u + 1)
                        pe.wait_ge(s_sg, s - 1)
                        gate_product(s, bank(s % 2)[:, 0:TC])
                    pe.wait_ge(s_abl, u + 1)
                    if s >= 2:
                        pe.wait_ge(s_gp, s - 1)
                    xh, xl = (sah, sal) if u % 2 == 0 else (oh_, ol_)
                    for k in range(proj_k(u)):
                        for i, (w_, x_) in enumerate(((abh, xh), (abh, xl), (abl, xh))):
                            m = nc.tensor.matmul(bank(2 + s % 2)[:, 0:TC], w_[:, u % 2, k, col], x_[:, k, tok],
                                                 start=(k == 0 and i == 0), stop=(k == proj_k(u) - 1 and i == 2))
                    m.then_inc(s_pr, 1)

        nc.clear_and_free_semaphores(front)
        nc.all_engine_barrier()

        rw = Region(hh_at, raw_at)
        woh = rw("w_o_hi", [P, KD, D], F32R)
        wol = rw("w_o_lo", [P, KD, D], F32R)
        r5 = Region(r1_at)
        mtr = r5("merged_raw", [P, 2, KD, P])
        mth = r5("merged_hi", [P, 2, KD, P], F32R)
        mtl = r5("merged_lo", [P, 2, KD, P], F32R)
        xo = r5("x_rows", [P, 2, D])
        x2 = r5("x_mixed", [P, 2, D])
        h2 = r5("moe_rows", [P, 2, D])
        h2T = r5("moe_T", [P, 2, KD, P])
        jk5 = r5("square_junk2", [P, D])
        g2row = r5("norm2_row", [P, D])
        wr = r5("w_router", [P, KD, 36])
        brr = r5("b_router_row", [P, 36])

        UN = 6
        wraw = nc.alloc_sbuf_tensor_at("expert_raw", [P, UN, 2048], F32, offset=raw_at)
        assert r1_at == raw_at + UN * 2048 * 4
        rc_at = (top - 3072) // 64 * 64
        assert r5.at <= rc_at
        rc = Region(rc_at)
        cbef = rc("before", [P, P])
        cone = rc("ones", [P, P])
        ramp = rc("ramps", [P, 4 + NE + 2 * NBMAX + 1 + P])
        valid = rc("valid", [P, TILES])
        num = rc("assignment_numbers", [P, 2, 2 * TILES])

        s_fc = sem_b("routing_consts_in")
        s_ui = [sem_b(f"expert_half_in{u}") for u in range(UN)]
        SLOT = [2, 3, 4, 5, 0, 1]
        gate_v = a["w_gate"][0].rearrange("e (u k p) n -> e u p k n", u=2, p=P)
        up_v = a["w_up"][0].rearrange("e (u k p) n -> e u p k n", u=2, p=P)
        down_v = a["w_down"][0].rearrange("e (u k p) n -> e u p k n", u=2, p=P)

        def load_half(sp, u, e):
            src = (gate_v, up_v, down_v)[u // 2]
            sp.dma_start(wraw[:, SLOT[u]].rearrange("p (k n) -> p k n", k=(2 if u >= 4 else 4)),
                         src[bass.ds(e, 1), u % 2].rearrange("o p k n -> (o p) k n")).then_inc(s_ui[u], 16)

        s_rc = sem_b("router_consts_in")
        s_woh = sem_b("w_o_hi_ready")
        s_wol = sem_b("w_o_lo_ready")
        s_mi = [sem_b(f"merged_in{i}") for i in range(2)]
        s_xi = [sem_b(f"x_rows_in{i}") for i in range(2)]
        s_mth = sem_b("merged_hi_ready")
        s_mtl = sem_b("merged_lo_ready")
        s_wop = sem_b("w_o_products")
        s_x2 = sem_b("x_mixed_ready")
        s_x2o = [sem_b(f"x_mixed_stored{i}") for i in range(2)]
        s_sq5 = sem_b("squares2_summed")
        s_h2 = sem_b("moe_rows_ready")
        s_h2o = [sem_b(f"moe_rows_stored{i}") for i in range(2)]
        s_h2T = sem_b("moe_transposed")
        s_h2c = sem_b("moe_T_ready")
        s_rt = sem_b("router_products")
        s_lg = sem_b("logits_ready")
        s_c5 = sem_b("vector_chain_router")

        with nc.Block() as block:
            @block.sync
            def _(sp):
                def load_wo(c):
                    sp.wait_ge(s_wol, c - 1)
                    sp.dma_start(raw[:, c % 2], wo_v[:, :, c * CW:(c + 1) * CW]).then_inc(s_wo[c % 2], 16)

                def load_tile(t):
                    r = rows(t)
                    if t >= 2:
                        sp.wait_ge(s_mtl, t - 1)
                        sp.wait_ge(s_x2, 2 * (t - 1))
                    sp.dma_start(mtr[:, t % 2, :, 0:r],
                                 mt_d[:, t * P:t * P + r].rearrange("(k p) q -> p k q", p=P)).then_inc(s_mi[t % 2], 16)
                    sp.dma_start(xo[0:r, t % 2, :], x_rows[t]).then_inc(s_xi[t % 2], 16)

                load_tile(0)
                load_wo(2)
                load_wo(3)
                load_tile(1)
                sp.dma_start(g2row[:], a["norm2_g"][0].partition_broadcast(P)).then_inc(s_rc, 16)
                sp.dma_start(wr[:, :, 0:4], a["w_group_router"][0].rearrange("(k p) n -> p k n", p=P)).then_inc(s_rc, 16)
                sp.dma_start(wr[:, :, 4:36], a["w_expert_router"][0].rearrange("(k p) n -> p k n", p=P)) \
                    .then_inc(s_rc, 16)
                sp.dma_start(brr[:, 0:4], a["b_group_router"][0].partition_broadcast(P)).then_inc(s_rc, 16)
                sp.dma_start(brr[:, 4:36], a["b_expert_router"][0].partition_broadcast(P)).then_inc(s_rc, 16)
                sp.dma_start(cbef[:], a["c_before"]).then_inc(s_fc, 16)
                sp.dma_start(cone[:], a["c_ones"]).then_inc(s_fc, 16)
                sp.dma_start(ramp[:], a["c_ramp"].partition_broadcast(P)).then_inc(s_fc, 16)
                sp.dma_start(valid[:], a["c_valid"]).then_inc(s_fc, 16)
                sp.dma_start(num[:], a["c_number"].rearrange("p c k t -> p c (k t)")).then_inc(s_fc, 16)
                for t in range(TILES):
                    r = rows(t)
                    if t + 2 < TILES:
                        load_tile(t + 2)
                    if t < UN:
                        if t == 4:
                            sp.wait_ge(s_wol, 4)
                        load_half(sp, t, 0)
                    sp.wait_ge(s_x2, 2 * (t + 1))
                    sp.dma_start(x2_d[t * P:t * P + r], x2[0:r, t % 2, :]).then_inc(s_x2o[t % 2], 16)
                    sp.wait_ge(s_h2, t + 1)
                    sp.dma_start(h2_d[t * P:t * P + r], h2[0:r, t % 2, :]).then_inc(s_h2o[t % 2], 16)
                for i in range(2):
                    sp.wait_ge(s_x2o[i], 16 * len(range(i, TILES, 2)))
                    sp.wait_ge(s_h2o[i], 16 * len(range(i, TILES, 2)))

            @block.scalar
            def _(act):
                def tile_hi(t):
                    r = rows(t)
                    act.wait_ge(s_mi[t % 2], 16 * (t // 2 + 1))
                    if t >= 2:
                        act.wait_ge(s_wop, t - 1)
                    nc.scalar.copy(mth[:, t % 2, :, 0:r], mtr[:, t % 2, :, 0:r]).then_inc(s_mth, 1)

                def wo_hi(c):
                    act.wait_ge(s_wo[c % 2], 16 * (c // 2 + 1))
                    nc.scalar.copy(woh[:, :, c * CW:(c + 1) * CW], raw[:, c % 2]).then_inc(s_woh, 1)

                wo_hi(0)
                wo_hi(1)
                tile_hi(0)
                wo_hi(2)
                wo_hi(3)
                for t in range(TILES + 1):
                    if t + 1 < TILES:
                        tile_hi(t + 1)
                    if t < TILES:
                        r = rows(t)
                        act.wait_ge(s_sq5, 2 * t + 1)
                        nc.scalar.activation(ss[0:r, t:t + 1], ss[0:r, t:t + 1], ACT.Sqrt, scale=1.0 / D,
                                             bias=eps[0:r, :]).then_inc(s_sq5, 1)
                    if t:
                        r = rows(t - 1)
                        act.wait_ge(s_h2T, t)
                        if t >= 3:
                            act.wait_ge(s_rt, t - 2)
                        for half in range(2):
                            nc.scalar.copy(h2T[:, (t - 1) % 2, 4 * half:4 * half + 4, 0:r],
                                           bank(4 + half).rearrange("p (k q) -> p k q", k=4)[:, :, 0:r]) \
                                .then_inc(s_h2c, 1)

            @block.vector
            def _(dve):
                link = chain_of(dve, s_c5)

                def tile_lo(t):
                    r = rows(t)
                    dve.wait_ge(s_mth, t + 1)
                    nc.vector.tensor_tensor(mtl[:, t % 2, :, 0:r], mtr[:, t % 2, :, 0:r],
                                            mth[:, t % 2, :, 0:r].bitcast(F32), ALU.subtract).then_inc(s_mtl, 1)

                def wo_lo(c):
                    dve.wait_ge(s_woh, c + 1)
                    nc.vector.tensor_tensor(wol[:, :, c * CW:(c + 1) * CW], raw[:, c % 2],
                                            woh[:, :, c * CW:(c + 1) * CW].bitcast(F32),
                                            ALU.subtract).then_inc(s_wol, 1)

                wo_lo(0)
                wo_lo(1)
                tile_lo(0)
                wo_lo(2)
                wo_lo(3)
                for t in range(TILES + 2):
                    if t + 1 < TILES:
                        tile_lo(t + 1)
                    if t < TILES:
                        r = rows(t)
                        dve.wait_ge(s_wop, t + 1)
                        dve.wait_ge(s_xi[t % 2], 16 * (t // 2 + 1))
                        if t >= 2:
                            dve.wait_ge(s_x2o[t % 2], 16 * (t // 2))
                        for half in range(2):
                            cols = slice(512 * half, 512 * half + 512)
                            nc.vector.tensor_tensor(x2[0:r, t % 2, cols], bank(2 * (t % 2) + half)[0:r, :],
                                                    xo[0:r, t % 2, cols], ALU.add).then_inc(s_x2, 1)
                        dve.wait_ge(s_x2, 2 * (t + 1))
                        nc.vector.tensor_tensor_reduce(jk5[0:r, :], x2[0:r, t % 2, :], x2[0:r, t % 2, :], 1.0, 0.0,
                                                       ALU.mult, ALU.add, ss[0:r, t:t + 1]).then_inc(s_sq5, 1)
                        dve.wait_ge(s_sq5, 2 * t + 2)
                        link(nc.vector.reciprocal(rstd[0:r, t:t + 1], ss[0:r, t:t + 1]))
                        if t == 0:
                            dve.wait_ge(s_rc, 16 * 5)
                        if t >= 2:
                            dve.wait_ge(s_h2o[t % 2], 16 * (t // 2))
                            dve.wait_ge(s_h2T, t - 1)
                        nc.vector.scalar_tensor_tensor(h2[0:r, t % 2, :], x2[0:r, t % 2, :], rstd[0:r, t:t + 1],
                                                       g2row[0:r, :], ALU.mult, ALU.mult).then_inc(s_h2, 1)
                    if t >= 2:
                        r = rows(t - 2)
                        dve.wait_ge(s_rt, t - 1)
                        nc.vector.tensor_tensor(logits[0:r, t - 2, :], bank(6)[0:r, 0:36], brr[0:r, :],
                                                ALU.add).then_inc(s_lg, 1)

            @block.tensor
            def _(pe):
                def router(t):
                    r = rows(t)
                    pe.wait_ge(s_h2c, 2 * t + 2)
                    if t == 0:
                        pe.wait_ge(s_rc, 16 * 5)
                    if t:
                        pe.wait_ge(s_lg, t)
                    for k in range(KD):
                        m = nc.tensor.matmul(bank(6)[0:r, 0:36], h2T[:, t % 2, k, 0:r], wr[:, k, :],
                                             start=(k == 0), stop=(k == KD - 1))
                    m.then_inc(s_rt, 1)

                for t in range(TILES + 2):
                    if t < TILES:
                        r = rows(t)
                        pe.wait_ge(s_mtl, t + 1)
                        if t >= 2:
                            pe.wait_ge(s_x2, 2 * (t - 1))
                        for half in range(2):
                            cols = slice(512 * half, 512 * half + 512)
                            if t == 0:
                                pe.wait_ge(s_wol, 2 * half + 2)
                            for k in range(KD):
                                for i, (x_, w_) in enumerate(((mth, woh), (mth, wol), (mtl, woh))):
                                    m = nc.tensor.matmul(bank(2 * (t % 2) + half)[0:r, :], x_[:, t % 2, k, 0:r],
                                                         w_[:, k, cols], start=(k == 0 and i == 0),
                                                         stop=(k == KD - 1 and i == 2))
                        m.then_inc(s_wop, 1)
                    if t >= 2:
                        router(t - 2)
                    if 1 <= t <= TILES:
                        r = rows(t - 1)
                        pe.wait_ge(s_h2, t)
                        if t >= 2:
                            pe.wait_ge(s_h2c, 2 * (t - 1))
                        for k in range(KD):
                            m = nc.tensor.transpose(bank(4 + k // 4)[:, (k % 4) * P:(k % 4) * P + r],
                                                    h2[0:r, (t - 1) % 2, k * P:(k + 1) * P], ident[0:r, 0:r])
                        m.then_inc(s_h2T, 1)

        ra = Region(hh_at, raw_at)
        weh = ra("expert_hi", [P, UN, 2048], F32R)
        xTh = ra("block_T_hi", [P, KD, P], F32R)
        xTl = ra("block_T_lo", [P, KD, P], F32R)
        sil = ra("silu_gate", [P, DE])
        hid = ra("hidden", [P, DE])
        hTh = ra("hidden_T_hi", [P, 4, P], F32R)
        hTl = ra("hidden_T_lo", [P, 4, P], F32R)
        r7 = Region(r1_at, rc_at)
        wel = r7("expert_lo", [P, UN, 2048], F32R)
        r7_wel_end = r7.at
        xg = r7("block_rows", [P, D])
        yb = r7("block_out", [P, D])
        idx = r7("block_tokens", [P, 1], I32)
        odx = r7("block_out_rows", [P, 1], I32)
        tab = r7("slot_table", [P, 2 * NBMAX], I32)

        r6 = Region(r7.at, rc_at)
        gmx = r6("group_max", [P, TILES])
        ge = r6("group_exp", [P, TILES, 4])
        oh4 = r6("group_onehot", [P, TILES, 4])
        pg = r6("group_prob", [P, TILES])
        em = r6("expert_logits", [P, TILES, NE])
        tmp = r6("weighted_match", [P, TILES, NE])
        oh1 = r6("first_onehot", [P, TILES, NE])
        oh2 = r6("second_onehot", [P, TILES, NE])
        v12 = r6("top_values", [P, 2, TILES])
        wmx = r6("match_max", [P, TILES])
        msk = r6("chosen", [P, TILES, NE])
        pre = r6("earlier_in_tile", [P, TILES, NE])
        tbs = r6("earlier_tiles", [P, TILES + 1, NE])
        cmp9 = r6("block_compare", [P, NE, TILES])
        nb32 = r6("expert_blocks", [P, NE])
        scn = r6("scan", [P, 2, NE])
        slot = r6("slot", [P, TILES, NE])
        dsf = r6("dest_float", [P, 2, TILES])
        cmpb = r6("owner_compare", [1, NBMAX, NE])
        btf = r6("block_table_float", [1, 2, NBMAX])
        R4, R32, RB, R128 = 0, 4, 4 + NE, 4 + NE + NBMAX
        RP = R128 + NBMAX + 1
        NA = 2 * TILES
        r6w = Region(r1_at + 2 * 8192, r7_wel_end)
        ohp = r6w("place_onehot", [P, NA, P])
        reach = r6w("blocks_reached", [P, NA, NBMAX + 1])
        bval = r6w("block_numbers", [P, NA, 2 * NBMAX])
        ohb = r6("block_onehot", [P, NA, NBMAX])
        nbl = r6("block_number", [P, NA])

        s_c6 = sem_b("vector_chain_routing")
        s_ge = sem_b("group_diff_ready")
        s_gx = sem_b("group_exp_ready")
        s_vd = sem_b("value_diff_ready")
        s_vx = sem_b("value_exp_ready")
        s_mk = sem_b("chosen_ready")
        s_cn = sem_b("counts_ready")
        s_ow = sem_b("onehots_ready")
        s_tm = sem_b("slot_table_products")
        s_bt = sem_b("block_table_ready")

        s_uh = [sem_b(f"{n}_hi_ready") for n in ("gate", "up", "down")]
        s_ul = [sem_b(f"{n}_lo_ready") for n in ("gate", "up", "down")]
        s_um = [sem_b(f"{n}_multiplied") for n in ("gate", "up", "down")]
        s_tb = sem_b("slot_table_ready")
        s_ix = sem_b("block_tokens_copied")
        s_ox = sem_b("block_out_rows_copied")
        s_xg = sem_b("block_rows_in")
        s_xT = sem_b("block_transposed")
        s_xh = sem_b("block_T_hi_ready")
        s_xl = sem_b("block_T_lo_ready")
        s_si = sem_b("silu_ready")
        s_hd = sem_b("hidden_ready")
        s_hT7 = sem_b("hidden_transposed")
        s_th = sem_b("hidden_T_hi_ready")
        s_tl = sem_b("hidden_T_lo_ready")
        s_xz = sem_b("block_rows_cleared")
        s_y = sem_b("block_out_ready")
        s_yo = sem_b("block_out_stored")

        def expert_of(eng, b):
            if isinstance(b, int) and b == 0:
                return 0
            return eng.value_load(blk[0:1, 0, bass.ds(b, 1)], min_val=0, max_val=NE - 1)

        @contextmanager
        def if_fresh(eng, b):
            if isinstance(b, int) and b == 0:
                yield
            else:
                with eng.If(eng.value_load(blk[0:1, 1, bass.ds(b, 1)], min_val=0, max_val=1) > 0):
                    yield

        def over_blocks(eng, body):
            body(0)
            eng.wait_ge(s_bt, 1)
            n = eng.value_load(nblk[0:1, 0:1], min_val=NE, max_val=NBMAX)
            last2 = eng.value_load(nblk[0:1, 1:2], min_val=NE - 2, max_val=NBMAX - 2)
            body(1)
            with eng.Fori(2, NBMAX) as b:
                with eng.If(b < n):
                    body(b)
            return last2

        def later(b, d):
            return not isinstance(b, int) or b >= d

        with nc.Block() as block:
            @block.sync
            def _(sp):
                def load(e, halves):
                    for u in halves:
                        sp.wait_ge(s_ul[u // 2], 2 * e - 1 + u % 2)
                        load_half(sp, u, e)

                load(1, range(UN))
                load(2, range(4))
                with sp.Fori(3, NE) as e:
                    load(e, range(4))
                    load(e - 1, range(4, UN))
                load(NE - 1, range(4, UN))

            @block.gpsimd
            def _(pool):
                pool.memset(xg[:], 0.0).then_inc(s_xz, 1)
                pool.wait_ge(s_xz, 1)
                pool.wait_ge(s_tb, 1)
                count = pool.alloc_register("awaited_count")

                def gather(b):
                    if later(b, 1):
                        pool.wait_ge(s_xg, 16 * b)
                    nc.gpsimd.tensor_copy(idx[:], tab[:, bass.ds(b, 1)]).then_inc(s_ix, 1)
                    pool.reg_mov(count, b + 1)
                    pool.wait_ge(s_ix, 1)
                    pool.wait_ge(s_ix, count)
                    if later(b, 1):
                        pool.wait_ge(s_xT, b)
                    pool.indirect_dma_start(xg[:], None, h2_d[:, :],
                                            bass.IndirectOffsetOnAxis(ap=idx[:], axis=0),
                                            bounds_check=TOK - 1, oob_is_err=False).then_inc(s_xg, 16)

                def scatter(b):
                    if later(b, 1):
                        pool.wait_ge(s_yo, 16 * b)
                    nc.gpsimd.tensor_copy(odx[:], tab[:, bass.ds(b + NBMAX, 1)]).then_inc(s_ox, 1)
                    pool.reg_mov(count, b + 1)
                    pool.wait_ge(s_ox, 1)
                    pool.wait_ge(s_ox, count)
                    pool.reg_mov(count, 2 * b + 2)
                    pool.wait_ge(s_ox, 1)
                    pool.wait_ge(s_y, count)
                    pool.indirect_dma_start(ys_d[:, :], bass.IndirectOffsetOnAxis(ap=odx[:], axis=0),
                                            yb[:], None, bounds_check=2 * TOK - 1,
                                            oob_is_err=False).then_inc(s_yo, 16)

                def body(b):
                    gather(b)
                    if later(b, 2):
                        scatter(b - 2)
                last2 = over_blocks(pool, body)
                scatter(last2)
                scatter(last2 + 1)
                pool.wait_ge(s_yo, 16 * last2 + 32)

            @block.scalar
            def _(act):
                act.wait_ge(s_ge, 1)
                nc.scalar.activation(ge[:], ge[:], ACT.Exp).then_inc(s_gx, 1)
                act.wait_ge(s_vd, 1)
                nc.scalar.activation(v12[:, 1], v12[:, 1], ACT.Exp).then_inc(s_vx, 1)

                def split_hi(m, b):
                    with if_fresh(act, b):
                        e = expert_of(act, b)
                        for u in (2 * m, 2 * m + 1):
                            act.wait_ge(s_ui[u], 16 * e + 16)
                            if later(b, 1):
                                act.wait_ge(s_um[m], 2 * b - 1 + u % 2)
                            nc.scalar.copy(weh[:, u], wraw[:, SLOT[u]]).then_inc(s_uh[m], 1)

                for m in range(3):
                    split_hi(m, 0)

                def silu(b):
                    act.wait_ge(s_um[0], 2 * b + 2)
                    if later(b, 1):
                        act.wait_ge(s_hd, b)
                    nc.scalar.activation(sil[:], bank(0), ACT.Silu).then_inc(s_si, 1)

                def rows_hi(b):
                    act.wait_ge(s_xT, b + 1)
                    for half in range(2):
                        nc.scalar.copy(xTh[:, 4 * half:4 * half + 4].rearrange("p k q -> p (k q)"),
                                       bank(2 + half)).then_inc(s_xh, 1)

                def hidden_hi(b):
                    act.wait_ge(s_hT7, b + 1)
                    nc.scalar.copy(hTh[:].rearrange("p k q -> p (k q)"), bank(4)).then_inc(s_th, 1)

                def out_rows(b):
                    act.wait_ge(s_um[2], 2 * b + 2)
                    if later(b, 1):
                        act.wait_ge(s_yo, 16 * b)
                    for half in range(2):
                        nc.scalar.copy(yb[:, 512 * half:512 * half + 512], bank(5 + half)).then_inc(s_y, 1)

                def body(b):
                    if later(b, 1):
                        split_hi(0, b)
                        silu(b - 1)
                    rows_hi(b)
                    if later(b, 1):
                        split_hi(1, b)
                    if later(b, 2):
                        out_rows(b - 2)
                    if later(b, 1):
                        hidden_hi(b - 1)
                    if later(b, 2):
                        split_hi(2, b - 1)
                last2 = over_blocks(act, body)
                silu(last2 + 1)
                out_rows(last2)
                hidden_hi(last2 + 1)
                split_hi(2, last2 + 1)
                out_rows(last2 + 1)

            @block.vector
            def _(dve):
                link = chain_of(dve, s_c6)
                V = nc.vector
                dve.wait_ge(s_fc, 16 * 5)
                gl, el = logits[:, :, 0:4], logits[:, :, 4:36]
                B = [P, TILES, NE]

                def col(x, n=NE):
                    return x.unsqueeze(2).to_broadcast([P, TILES, n])

                def first_match(out_, val, mx, ramp0, n):
                    rp = ramp[:, ramp0:ramp0 + n].unsqueeze(1).to_broadcast([P, TILES, n])
                    w = tmp[:, :, 0:n]
                    link(V.tensor_tensor(w, val, col(mx, n), ALU.is_equal))
                    link(V.tensor_tensor(w, w, rp, ALU.mult))
                    link(V.tensor_reduce(wmx[:], w, X, ALU.max))
                    link(V.tensor_tensor(out_, w, col(wmx[:], n), ALU.is_equal))

                link(V.tensor_reduce(gmx[:], gl, X, ALU.max))
                V.tensor_tensor(ge[:], gl, col(gmx[:], 4), ALU.subtract).then_inc(s_ge, 1)
                first_match(oh4[:], gl, gmx[:], R4, 4)
                link(V.tensor_scalar(oh4[:], oh4[:], 1.0, -NEG, ALU.subtract, ALU.mult))
                link(V.tensor_tensor(em[:].rearrange("p t (g e) -> p t g e", g=4),
                                     el.rearrange("p t (g e) -> p t g e", g=4),
                                     oh4[:].unsqueeze(3).to_broadcast([P, TILES, 4, PER_GROUP]), ALU.add))
                link(V.tensor_reduce(v12[:, 0], em[:], X, ALU.max))
                first_match(oh1[:], em[:], v12[:, 0], R32, NE)
                link(V.scalar_tensor_tensor(em[:], oh1[:], NEG, em[:], ALU.mult, ALU.add))
                link(V.tensor_reduce(v12[:, 1], em[:], X, ALU.max))
                first_match(oh2[:], em[:], v12[:, 1], R32, NE)
                V.tensor_tensor(v12[:, 1], v12[:, 1], v12[:, 0], ALU.subtract).then_inc(s_vd, 1)
                link(V.tensor_tensor(msk[:], oh1[:], oh2[:], ALU.add))
                V.tensor_tensor(msk[:], msk[:], col(valid[:]), ALU.mult).then_inc(s_mk, 1)
                dve.wait_ge(s_gx, 1)
                link(V.tensor_reduce(pg[:], ge[:], X, ALU.add))
                link(V.reciprocal(pg[:], pg[:]))
                dve.wait_ge(s_vx, 1)
                link(V.tensor_scalar(wmx[:], v12[:, 1], 1.0, None, ALU.add))
                link(V.reciprocal(wmx[:], wmx[:]))
                link(V.tensor_tensor(gate2[:, :, 0], pg[:], wmx[:], ALU.mult))
                link(V.tensor_tensor(gate2[:, :, 1], gate2[:, :, 0], v12[:, 1], ALU.mult))
                dve.wait_ge(s_cn, 1)
                link(V.tensor_copy(pre[:].rearrange("p t e -> p (t e)"), bank(0)[:, 0:TILES * NE]))
                tot = bank(1)[:, 0:TILES * NE].rearrange("p (t e) -> p t e", t=TILES)
                link(V.memset(tbs[:, 0, :], 0.0))
                for t in range(TILES):
                    link(V.tensor_tensor(tbs[:, t + 1, :], tbs[:, t, :], tot[:, t, :], ALU.add))
                link(V.tensor_tensor(cmp9[:], tbs[:, TILES, :].unsqueeze(2).to_broadcast([P, NE, TILES]),
                                     ramp[:, R128:R128 + TILES].unsqueeze(1).to_broadcast([P, NE, TILES]), ALU.is_gt))
                link(V.tensor_reduce(nb32[:], cmp9[:], X, ALU.add))
                link(V.tensor_scalar(nb32[:], nb32[:], 1.0, None, ALU.max))
                link(V.tensor_copy(scn[:, 0], nb32[:]))
                cur, step = 0, 1
                while step < NE:
                    link(V.tensor_copy(scn[:, 1 - cur, 0:step], scn[:, cur, 0:step]))
                    link(V.tensor_tensor(scn[:, 1 - cur, step:NE], scn[:, cur, step:NE], scn[:, cur, 0:NE - step],
                                         ALU.add))
                    cur, step = 1 - cur, 2 * step
                ends = scn[:, cur, :]
                first = scn[:, 1 - cur, :]
                link(V.tensor_tensor(first, ends, nb32[:], ALU.subtract))
                link(V.tensor_scalar(first, first, float(BLK), None, ALU.mult))
                link(V.tensor_tensor(slot[:], pre[:], tbs[:, 0:TILES, :], ALU.add))
                link(V.tensor_tensor(slot[:], slot[:], first.unsqueeze(1).to_broadcast(B), ALU.add))
                for k, oh in enumerate((oh1, oh2)):
                    link(V.tensor_tensor(tmp[:], oh[:], slot[:], ALU.mult))
                    link(V.tensor_reduce(dsf[:, k], tmp[:], X, ALU.add))
                red_ = dsf[:].rearrange("p k t -> p (k t)")
                link(V.tensor_tensor(reach[:], red_.unsqueeze(2).to_broadcast([P, NA, NBMAX + 1]),
                                     ramp[:, R128:R128 + NBMAX + 1].unsqueeze(1).to_broadcast([P, NA, NBMAX + 1]),
                                     ALU.is_ge))
                link(V.tensor_reduce(nbl[:], reach[:], X, ALU.add))
                link(V.scalar_tensor_tensor(nbl[:], nbl[:], -float(BLK), red_, ALU.mult, ALU.add))
                link(V.tensor_tensor(ohp[:], nbl[:].unsqueeze(2).to_broadcast([P, NA, P]),
                                     ramp[:, RP:RP + P].unsqueeze(1).to_broadcast([P, NA, P]), ALU.is_equal))
                link(V.tensor_tensor(ohb[:], reach[:, :, 0:NBMAX], reach[:, :, 1:NBMAX + 1], ALU.subtract))
                for c in range(2):
                    V.tensor_tensor(bval[:, :, c * NBMAX:(c + 1) * NBMAX], ohb[:],
                                    num[:, c].unsqueeze(2).to_broadcast([P, NA, NBMAX]), ALU.mult).then_inc(s_ow, 1)

                def split_lo(m, b):
                    with if_fresh(dve, b):
                        e = expert_of(dve, b)
                        for u in (2 * m, 2 * m + 1):
                            dve.wait_ge(s_uh[m], 2 * e + 1 + u % 2)
                            nc.vector.tensor_tensor(wel[:, u], wraw[:, SLOT[u]], weh[:, u].bitcast(F32),
                                                    ALU.subtract).then_inc(s_ul[m], 1)

                def hidden(b):
                    dve.wait_ge(s_si, b + 1)
                    dve.wait_ge(s_um[1], 2 * b + 2)
                    if later(b, 1):
                        dve.wait_ge(s_hT7, b)
                    nc.vector.tensor_tensor(hid[:], bank(1), sil[:], ALU.mult).then_inc(s_hd, 1)

                def rows_lo(b):
                    for half in range(2):
                        dve.wait_ge(s_xh, 2 * b + half + 1)
                        nc.vector.tensor_tensor(
                            xTl[:, 4 * half:4 * half + 4].rearrange("p k q -> p (k q)"), bank(2 + half),
                            xTh[:, 4 * half:4 * half + 4].rearrange("p k q -> p (k q)").bitcast(F32),
                            ALU.subtract).then_inc(s_xl, 1)

                def hidden_lo(b):
                    dve.wait_ge(s_th, b + 1)
                    nc.vector.tensor_tensor(hTl[:].rearrange("p k q -> p (k q)"), bank(4),
                                            hTh[:].rearrange("p k q -> p (k q)").bitcast(F32),
                                            ALU.subtract).then_inc(s_tl, 1)

                def block_table():
                    link(V.tensor_tensor(cmpb[:], ramp[0:1, RB:RB + NBMAX].unsqueeze(2).to_broadcast([1, NBMAX, NE]),
                                         ends[0:1].unsqueeze(1).to_broadcast([1, NBMAX, NE]), ALU.is_ge))
                    owner, fresh = btf[:, 0, :], btf[:, 1, :]
                    link(V.tensor_reduce(owner, cmpb[:], X, ALU.add))
                    link(V.tensor_scalar(owner, owner, float(NE - 1), None, ALU.min))
                    link(V.memset(fresh[:, 0:1], 1.0))
                    link(V.tensor_tensor(fresh[:, 1:], owner[:, 1:], owner[:, 0:NBMAX - 1], ALU.not_equal))
                    link(V.tensor_copy(nblk[:, 0:1], ends[0:1, NE - 1:NE]))
                    link(V.tensor_scalar(nblk[:, 1:2], ends[0:1, NE - 1:NE], -2.0, None, ALU.add))
                    V.tensor_copy(blk[:], btf[:]).then_inc(s_bt, 1)

                split_lo(0, 0)
                dve.wait_ge(s_tm, 1)
                V.tensor_scalar(tab[:], bank(4)[:, 0:2 * NBMAX], float(NONE), None, ALU.add).then_inc(s_tb, 1)
                split_lo(1, 0)

                def body(b):
                    if later(b, 1):
                        split_lo(0, b)
                        hidden(b - 1)
                    rows_lo(b)
                    if not later(b, 1):
                        split_lo(2, b)
                        block_table()
                    if later(b, 1):
                        split_lo(1, b)
                        hidden_lo(b - 1)
                    if later(b, 2):
                        split_lo(2, b - 1)
                last2 = over_blocks(dve, body)
                hidden(last2 + 1)
                hidden_lo(last2 + 1)
                split_lo(2, last2 + 1)

            @block.tensor
            def _(pe):
                pe.wait_ge(s_mk, 1)
                pe.wait_ge(s_fc, 16 * 5)
                mv_ = msk[:].rearrange("p t e -> p (t e)")
                nc.tensor.matmul(bank(0)[:, 0:TILES * NE], cbef[:], mv_, start=True, stop=True)
                nc.tensor.matmul(bank(1)[:, 0:TILES * NE], cone[:], mv_, start=True, stop=True).then_inc(s_cn, 1)
                pe.wait_ge(s_ow, 2)
                for j in range(NA):
                    m = nc.tensor.matmul(bank(4)[:, 0:2 * NBMAX], ohp[:, j, :], bval[:, j, :],
                                         start=(j == 0), stop=(j == NA - 1))
                m.then_inc(s_tm, 1)

                def rows_T(b):
                    pe.wait_ge(s_xg, 16 * b + 16)
                    if later(b, 1):
                        pe.wait_ge(s_xl, 2 * b)
                    for k in range(KD):
                        m = nc.tensor.transpose(bank(2 + k // 4)[:, (k % 4) * P:(k % 4 + 1) * P],
                                                xg[:, k * P:(k + 1) * P], ident[:])
                    m.then_inc(s_xT, 1)

                def gate_up(m_, b):
                    e = expert_of(pe, b)
                    if later(b, 1):
                        pe.wait_ge((s_si, s_hd)[m_], b)
                    for u in range(2):
                        pe.wait_ge(s_ul[m_], 2 * e + 1 + u)
                        if m_ == 0:
                            pe.wait_ge(s_xl, 2 * b + 1 + u)
                        for k in range(4):
                            cols = slice(512 * k, 512 * k + 512)
                            h_, l_ = weh[:, 2 * m_ + u, cols], wel[:, 2 * m_ + u, cols]
                            xh, xl = xTh[:, 4 * u + k], xTl[:, 4 * u + k]
                            for i, (x_, w_) in enumerate(((xh, h_), (xh, l_), (xl, h_))):
                                m = nc.tensor.matmul(bank(m_), x_, w_, start=(u == 0 and k == 0 and i == 0),
                                                     stop=(u == 1 and k == 3 and i == 2))
                        m.then_inc(s_um[m_], 1)

                def hidden_T(b):
                    pe.wait_ge(s_hd, b + 1)
                    if later(b, 1):
                        pe.wait_ge(s_tl, b)
                    for k in range(4):
                        m = nc.tensor.transpose(bank(4)[:, k * P:(k + 1) * P], hid[:, k * P:(k + 1) * P], ident[:])
                    m.then_inc(s_hT7, 1)

                def down(b):
                    e = expert_of(pe, b)
                    pe.wait_ge(s_tl, b + 1)
                    if later(b, 1):
                        pe.wait_ge(s_y, 2 * b)
                    for u in range(2):
                        pe.wait_ge(s_ul[2], 2 * e + 1 + u)
                        for k in range(2):
                            for half in range(2):
                                cols = slice(1024 * k + 512 * half, 1024 * k + 512 * half + 512)
                                h_, l_ = weh[:, 4 + u, cols], wel[:, 4 + u, cols]
                                xh, xl = hTh[:, 2 * u + k], hTl[:, 2 * u + k]
                                for i, (x_, w_) in enumerate(((xh, h_), (xh, l_), (xl, h_))):
                                    m = nc.tensor.matmul(bank(5 + half), x_, w_,
                                                         start=(u == 0 and k == 0 and i == 0),
                                                         stop=(u == 1 and k == 1 and i == 2))
                        m.then_inc(s_um[2], 1)

                def body(b):
                    rows_T(b)
                    if later(b, 2):
                        down(b - 2)
                    if later(b, 1):
                        hidden_T(b - 1)
                    gate_up(0, b)
                    gate_up(1, b)
                last2 = over_blocks(pe, body)
                down(last2)
                hidden_T(last2 + 1)
                down(last2 + 1)

        r8 = Region(hh_at)
        y1 = r8("first_rows", [P, 3, D])
        y2 = r8("second_rows", [P, 3, D])
        xf = r8("x_rows_final", [P, 3, D])
        yo = r8("y_out", [P, 2, D])
        jk8 = r8("square_junk3", [P, D])
        gfr = r8("final_norm_row", [P, D])

        s_gf = sem_b("final_gain_in")
        s_y1 = [sem_b(f"first_rows_in{i}") for i in range(3)]
        s_y2 = [sem_b(f"second_rows_in{i}") for i in range(3)]
        s_xf = [sem_b(f"x_final_in{i}") for i in range(3)]
        s_f1 = sem_b("first_added")
        s_f2 = sem_b("second_added")
        s_ms8 = sem_b("squares3_summed")
        s_sq8 = sem_b("root3_ready")
        s_r8 = sem_b("scale3_ready")
        s_fo = sem_b("y_ready")
        s_out = [sem_b(f"y_stored{i}") for i in range(2)]
        y_rows = [out[0][0, t * P:(t + 1) * P] for t in range(NT)] + [out[1].rearrange("b s d -> (b s) d")]

        with nc.Block() as block:
            @block.sync
            def _(sp):
                sp.dma_start(gfr[:], a["final_norm_g"].partition_broadcast(P)).then_inc(s_gf, 16)

                def load_rows(t):
                    r = rows(t)
                    if t >= 3:
                        sp.wait_ge(s_fo, t - 2)
                    sp.dma_start(xf[0:r, t % 3, :], x2_d[t * P:t * P + r]).then_inc(s_xf[t % 3], 16)
                    sp.dma_start(y1[0:r, t % 3, :], ys_d[t * P:t * P + r]).then_inc(s_y1[t % 3], 16)
                    sp.dma_start(y2[0:r, t % 3, :], ys_d[TOK + t * P:TOK + t * P + r]).then_inc(s_y2[t % 3], 16)

                for t in range(3):
                    load_rows(t)
                for t in range(TILES):
                    r = rows(t)
                    sp.wait_ge(s_fo, t + 1)
                    sp.dma_start(y_rows[t], yo[0:r, t % 2, :]).then_inc(s_out[t % 2], 16)
                    if t + 3 < TILES:
                        load_rows(t + 3)
                for i in range(2):
                    sp.wait_ge(s_out[i], 16 * len(range(i, TILES, 2)))

            @block.scalar
            def _(act):
                for t in range(TILES):
                    r = rows(t)
                    act.wait_ge(s_ms8, t + 1)
                    nc.scalar.activation(ss[0:r, t:t + 1], ss[0:r, t:t + 1], ACT.Sqrt, scale=1.0 / D,
                                         bias=eps[0:r, :]).then_inc(s_sq8, 1)

            @block.vector
            def _(dve):
                dve.wait_ge(s_gf, 16)
                for t in range(TILES + 1):
                    if t < TILES:
                        r = rows(t)
                        for s_in in (s_y1, s_y2, s_xf):
                            dve.wait_ge(s_in[t % 3], 16 * (t // 3 + 1))
                        nc.vector.scalar_tensor_tensor(y1[0:r, t % 3, :], y1[0:r, t % 3, :], gate2[0:r, t, 0:1],
                                                       xf[0:r, t % 3, :], ALU.mult, ALU.add).then_inc(s_f1, 1)
                        dve.wait_ge(s_f1, t + 1)
                        nc.vector.scalar_tensor_tensor(y1[0:r, t % 3, :], y2[0:r, t % 3, :], gate2[0:r, t, 1:2],
                                                       y1[0:r, t % 3, :], ALU.mult, ALU.add).then_inc(s_f2, 1)
                        dve.wait_ge(s_f2, t + 1)
                        if t:
                            dve.wait_ge(s_ms8, t)
                        nc.vector.tensor_tensor_reduce(jk8[0:r, :], y1[0:r, t % 3, :], y1[0:r, t % 3, :], 1.0, 0.0,
                                                       ALU.mult, ALU.add, ss[0:r, t:t + 1]).then_inc(s_ms8, 1)
                    if t:
                        r = rows(t - 1)
                        p = (t - 1) % 2
                        dve.wait_ge(s_sq8, t)
                        nc.vector.reciprocal(rstd[0:r, t - 1:t], ss[0:r, t - 1:t]).then_inc(s_r8, 1)
                        dve.wait_ge(s_r8, t)
                        if t >= 3:
                            dve.wait_ge(s_out[p], 16 * ((t - 1) // 2))
                        nc.vector.scalar_tensor_tensor(yo[0:r, p, :], y1[0:r, (t - 1) % 3, :], rstd[0:r, t - 1:t],
                                                       gfr[0:r, :], ALU.mult, ALU.mult).then_inc(s_fo, 1)


_INS = ["x_prompt", "x_sample", "cache_kv_g0", "cache_kv_g1", "cache_kv_g2", "norm1_g", "w_in", "b_in",
        "a_ln_g", "a_ln_b", "w_spatial", "b_spatial", "w_a_proj", "w_b_proj", "w_o", "norm2_g",
        "w_group_router", "b_group_router", "w_expert_router", "b_expert_router", "w_gate", "w_up",
        "w_down", "final_norm_g"]
_OUTS = [(1, SEQ, D), (NS, 1, D)] + [(1, 1, KEEP[g], 2, H, DH) for g in range(NG)] + \
        [(1, NS, 1, 2, H, DH)] * NG + [(1, NS, 1, AW)]


def _constants():
    f = np.float32
    c = {"c_ident": np.eye(P, dtype=f)}
    q, k = np.arange(P)[:, None], np.arange(P)[None, :]
    band = np.concatenate([k >= q, k <= q], axis=1)
    c["c_mask"] = np.where(band, f(0), f(NEG)).astype(f)
    c["c_mask2"] = np.where(((q - k) % 2 == 0) & (k <= q), f(0), f(NEG)).astype(f)
    inv = (f(1.0) / (f(10000.0) ** (np.arange(DH // 2, dtype=f) * f(2.0 / DH)))).astype(f)
    table = np.zeros((NG, TILES, P, 2 * DH), f)
    tokens = np.arange(SEQ)
    for g, d in enumerate((1, 4, NT)):
        order = tokens.reshape(SEQ // d, d).T.reshape(-1)
        pos = np.concatenate([order, np.full(P, PAST)]).astype(f)
        ang = (pos[:, None] * inv[None]).astype(f).astype(np.float64)
        cos, sin = np.cos(ang).astype(f), np.sin(ang).astype(f)
        table[g] = np.concatenate([cos, cos, -sin, sin], axis=1).reshape(TILES, P, 2 * DH)
    c["c_rope"] = table
    c["c_before"] = (q < k).astype(f)
    c["c_ones"] = np.ones((P, P), f)
    c["c_causal_T"] = (q <= k).astype(f)
    c["c_ramp"] = np.concatenate([NEG_GROUPS - np.arange(NEG_GROUPS), NE - np.arange(NE),
                                  np.arange(NBMAX), BLK * np.arange(NBMAX + 1), np.arange(P) - P]).astype(f)
    token = np.arange(TILES)[None] * P + np.arange(P)[:, None]
    c["c_valid"] = (token < TOK).astype(f)
    number = np.stack([np.stack([token, token], 1), np.stack([token, token + TOK], 1)], 1) - NONE
    c["c_number"] = (number * (token < TOK)[:, None, None]).astype(f)
    return c


def kernel(**inputs):
    import concourse.bacc as _bacc
    from concourse.bass_utils import run_bass_kernel_spmd as _run

    nc = _bacc.Bacc("TRN2", target_bir_lowering=False, num_devices=1)
    arrays, a = {}, {}
    for name, v in [(n, np.ascontiguousarray(inputs[n])) for n in _INS] + list(_constants().items()):
        arrays[f"in_{name}_dram"] = v
        a[name] = nc.dram_tensor(f"in_{name}_dram", v.shape, mybir.dt.from_np(v.dtype), kind="ExternalInput").ap()
    outs = [nc.dram_tensor(f"out_{i}_dram", shape, F32, kind="ExternalOutput").ap()
            for i, shape in enumerate(_OUTS)]
    build(nc, a, outs)
    r = _run(nc, [arrays], core_ids=[0])
    return tuple(r.results[0][f"out_{i}_dram"] for i in range(len(_OUTS)))
```
